# Optimizing a Trainium2 kernel written in Bass

```python
import numpy as np
import jax, jax.numpy as jnp
from jax import lax

D_MODEL = 1024
BATCH = 1
SEQ = 256
DEPTH = 2

D_MIX = D_MODEL
N_MIXERS = 4
GROUP_W = D_MIX // N_MIXERS

MLA_HEADS = 4
MLA_V = GROUP_W // MLA_HEADS
MLA_NOPE = MLA_V
MLA_ROPE = MLA_NOPE // 2
MLA_Q_RANK = D_MODEL // 4
MLA_KV_RANK = D_MODEL // 8
ROPE_THETA = 10000.0
MAX_START = 4096

CONV_CH = GROUP_W
CONV_K = 3

GMLP_GROUPS = 4
GMLP_CHUNK = 128

NSA_HEADS = 4
NSA_DH = GROUP_W // NSA_HEADS
CMP_LEN = 32
CMP_STRIDE = 16
CMP_HIDDEN = 4 * NSA_DH
SEL_LEN = 64
N_SELECT = 16
WINDOW = 512
Q_BLOCK = 128
FORCE_SCORE = 1e4

D_FF = 7 * D_MODEL // 2
N_EXPERTS = 8
TOP_K = 2

EPS = 1e-6
NEG = -1e30

IN_SIZES = (MLA_Q_RANK, MLA_KV_RANK, MLA_ROPE,
            CONV_CH, CONV_CH, CONV_CH,
            GROUP_W, GROUP_W,
            NSA_HEADS * NSA_DH,
            NSA_DH, NSA_DH, NSA_DH, NSA_DH, NSA_DH, NSA_DH,
            NSA_HEADS * 3)
D_IN = sum(IN_SIZES)

kernel_name = 'hybrid_mla_conv_gmlp_nsa_moe'

def rms_norm(x, g):
    xf = x.astype(jnp.float32)
    y = xf * lax.rsqrt(jnp.mean(xf * xf, axis=-1, keepdims=True) + EPS)
    return (y * g.astype(jnp.float32)).astype(x.dtype)

def layer_norm(x, g):
    xf = x.astype(jnp.float32)
    mu = jnp.mean(xf, axis=-1, keepdims=True)
    var = jnp.mean(jnp.square(xf - mu), axis=-1, keepdims=True)
    return ((xf - mu) * lax.rsqrt(var + EPS) * g.astype(jnp.float32)).astype(x.dtype)

def masked_softmax(s, mask):
    return jax.nn.softmax(jnp.where(mask, s.astype(jnp.float32), NEG), axis=-1)

def rope(x, positions):
    half = x.shape[-1] // 2
    inv = ROPE_THETA ** (-jnp.arange(half, dtype=jnp.float32) / half)
    ang = positions.astype(jnp.float32)[..., None] * inv
    cos = jnp.cos(ang)[:, :, None, :]
    sin = jnp.sin(ang)[:, :, None, :]
    xf = x.astype(jnp.float32)
    x1, x2 = xf[..., :half], xf[..., half:]
    return jnp.concatenate([x1 * cos - x2 * sin, x1 * sin + x2 * cos], axis=-1).astype(x.dtype)

def causal_attention_blocked(q, k, v, scale):
    B, S, H, dk = q.shape
    nq = S // Q_BLOCK
    qb = q.reshape(B, nq, Q_BLOCK, H, dk).transpose(1, 0, 2, 3, 4)
    k_idx = jnp.arange(S)

    def block(args):
        qi, i = args
        s = jnp.einsum('bqhd,bkhd->bhqk', qi, k).astype(jnp.float32) * scale
        q_idx = i * Q_BLOCK + jnp.arange(Q_BLOCK)
        p = masked_softmax(s, k_idx[None, :] <= q_idx[:, None])
        return jnp.einsum('bhqk,bkhd->bqhd', p.astype(v.dtype), v)

    out = lax.map(block, (qb, jnp.arange(nq)))
    return out.transpose(1, 0, 2, 3, 4).reshape(B, S, H, v.shape[-1])

def mla_mixer(cq, ckv, kr, positions, q_norm, w_uq, kv_norm, w_ukv):
    B, S, _ = cq.shape
    q = (rms_norm(cq, q_norm) @ w_uq).reshape(B, S, MLA_HEADS, MLA_NOPE + MLA_ROPE)
    q = jnp.concatenate([q[..., :MLA_NOPE], rope(q[..., MLA_NOPE:], positions)], axis=-1)
    kv = (rms_norm(ckv, kv_norm) @ w_ukv).reshape(B, S, MLA_HEADS, MLA_NOPE + MLA_V)
    k_rope = jnp.broadcast_to(rope(kr[:, :, None, :], positions), (B, S, MLA_HEADS, MLA_ROPE))
    k = jnp.concatenate([kv[..., :MLA_NOPE], k_rope], axis=-1)
    v = kv[..., MLA_NOPE:]
    o = causal_attention_blocked(q, k, v, (MLA_NOPE + MLA_ROPE) ** -0.5)
    return o.reshape(B, S, MLA_HEADS * MLA_V)

def short_conv_mixer(b_gate, c_gate, h, conv_w):
    u = c_gate * h
    y = lax.conv_general_dilated(u, conv_w[:, None, :].astype(u.dtype), window_strides=(1,),
                                 padding=[(CONV_K - 1, 0)],
                                 dimension_numbers=('NWC', 'WIO', 'NWC'),
                                 feature_group_count=u.shape[-1])
    return b_gate * y

def gmlp_mixer(u, v, ln_g, w_s, b_s):
    B, S, W = u.shape
    u = jax.nn.gelu(u)
    v = layer_norm(jax.nn.gelu(v), ln_g)
    n = S // GMLP_CHUNK
    dg = W // GMLP_GROUPS
    vc = v.reshape(B, n, GMLP_CHUNK, GMLP_GROUPS, dg)
    causal = jnp.tril(jnp.ones((GMLP_CHUNK, GMLP_CHUNK), dtype=bool))
    ws = jnp.where(causal[None], w_s, 0)
    sv = jnp.einsum('gij,bnjgd->bnigd', ws, vc) + b_s.T[None, None, :, :, None]
    return u * sv.reshape(B, S, W)

def compress_blocks(z, pe, w1, w2):
    B, S, d = z.shape
    r = CMP_LEN // CMP_STRIDE
    n = S // CMP_STRIDE
    ch = z.reshape(B, n, CMP_STRIDE, d)
    blocks = jnp.concatenate([ch[:, j:n - r + 1 + j] for j in range(r)], axis=2)
    nc = blocks.shape[1]
    blocks = (blocks + pe).reshape(B, nc, CMP_LEN * d)
    return jax.nn.gelu(blocks @ w1) @ w2

def cmp_to_sel_matrix(S):
    nc = S // CMP_STRIDE - CMP_LEN // CMP_STRIDE + 1
    ns = S // SEL_LEN
    cs = np.arange(nc)[:, None] * CMP_STRIDE
    ss = np.arange(ns)[None, :] * SEL_LEN
    ov = np.clip(np.minimum(cs + CMP_LEN, ss + SEL_LEN) - np.maximum(cs, ss), 0, None)
    return jnp.asarray(ov.astype(np.float32) / np.float32(CMP_LEN))

def nsa_mixer(q, kc_raw, vc_raw, ks, vs, kw, vw, g_logits,
              pe_k, w1_k, w2_k, pe_v, w1_v, w2_v):
    B, S, _ = q.shape
    H, dh = NSA_HEADS, NSA_DH
    scale = dh ** -0.5
    q = q.reshape(B, S, H, dh)
    t_idx = jnp.arange(S)
    nq = S // Q_BLOCK

    kc = compress_blocks(kc_raw, pe_k, w1_k, w2_k)
    vc = compress_blocks(vc_raw, pe_v, w1_v, w2_v)
    nc = kc.shape[1]
    blk_end = jnp.arange(nc) * CMP_STRIDE + CMP_LEN - 1
    cmask = blk_end[None, :] <= t_idx[:, None]
    s_c = jnp.einsum('bshd,bcd->bshc', q, kc).astype(jnp.float32) * scale
    p_c = masked_softmax(s_c, cmask[None, :, None, :]) * jnp.any(cmask, axis=-1)[None, :, None, None]
    o_cmp = jnp.einsum('bshc,bcd->bshd', p_c.astype(vc.dtype), vc)

    ns = S // SEL_LEN
    p_sel = jnp.einsum('bshc,cn->bsn', p_c, cmp_to_sel_matrix(S))
    blk = jnp.arange(ns)[None, :]
    cur = (t_idx // SEL_LEN)[:, None]
    valid = blk <= cur
    forced = (blk == 0) | (blk == cur) | (blk == cur - 1)
    p_sel = jnp.where(forced[None], FORCE_SCORE, jnp.where(valid[None], p_sel, -1.0))
    n_sel = min(N_SELECT, ns)
    _, sel_idx = lax.top_k(p_sel, n_sel)

    ks_blk = ks.reshape(B, ns, SEL_LEN, dh)
    vs_blk = vs.reshape(B, ns, SEL_LEN, dh)
    qb = q.reshape(B, nq, Q_BLOCK, H, dh).transpose(1, 0, 2, 3, 4)
    ib = sel_idx.reshape(B, nq, Q_BLOCK, n_sel).transpose(1, 0, 2, 3)
    b_ar = jnp.arange(B)[:, None, None]

    def sel_block(args):
        qi, idx, i = args
        kg = ks_blk[b_ar, idx]
        vg = vs_blk[b_ar, idx]
        key_pos = idx[..., None] * SEL_LEN + jnp.arange(SEL_LEN)
        q_pos = i * Q_BLOCK + jnp.arange(Q_BLOCK)
        mask = (key_pos <= q_pos[None, :, None, None]).reshape(B, Q_BLOCK, 1, n_sel * SEL_LEN)
        s = jnp.einsum('bqhd,bqnld->bqhnl', qi, kg).astype(jnp.float32) * scale
        p = masked_softmax(s.reshape(B, Q_BLOCK, H, n_sel * SEL_LEN), mask)
        p = p.reshape(B, Q_BLOCK, H, n_sel, SEL_LEN)
        return jnp.einsum('bqhnl,bqnld->bqhd', p.astype(vg.dtype), vg)

    o_sel = lax.map(sel_block, (qb, ib, jnp.arange(nq)))
    o_sel = o_sel.transpose(1, 0, 2, 3, 4).reshape(B, S, H, dh)

    n_band = WINDOW // Q_BLOCK + 1

    def band(z):
        zc = z.reshape(B, nq, Q_BLOCK, dh)
        zp = jnp.pad(zc, ((0, 0), (n_band - 1, 0), (0, 0), (0, 0)))
        return jnp.concatenate([zp[:, j:j + nq] for j in range(n_band)], axis=2)

    kb, vb = band(kw), band(vw)
    qc = q.reshape(B, nq, Q_BLOCK, H, dh)
    q_pos = jnp.arange(nq)[:, None] * Q_BLOCK + jnp.arange(Q_BLOCK)
    k_pos = (jnp.arange(nq)[:, None] - (n_band - 1)) * Q_BLOCK + jnp.arange(n_band * Q_BLOCK)
    diff = q_pos[:, :, None] - k_pos[:, None, :]
    wmask = (diff >= 0) & (diff < WINDOW) & (k_pos[:, None, :] >= 0)
    s_w = jnp.einsum('bnqhd,bnkd->bnhqk', qc, kb).astype(jnp.float32) * scale
    p_w = masked_softmax(s_w, wmask[None, :, None])
    o_win = jnp.einsum('bnhqk,bnkd->bnqhd', p_w.astype(vb.dtype), vb).reshape(B, S, H, dh)

    g = jax.nn.sigmoid(g_logits.astype(jnp.float32)).reshape(B, S, H, 3).astype(q.dtype)
    o = g[..., 0:1] * o_cmp + g[..., 1:2] * o_sel + g[..., 2:3] * o_win
    return o.reshape(B, S, H * dh)

def swiglu(x, wg, wu, wd):
    return (jax.nn.silu(x @ wg) * (x @ wu)) @ wd

def moe_ffn(x, w_router, wg, wu, wd):
    B, S, D = x.shape
    xt = x.reshape(B * S, D)
    logits = (xt @ w_router).astype(jnp.float32)
    top_v, top_i = lax.top_k(logits, TOP_K)
    w = jax.nn.softmax(top_v, axis=-1)
    gates = jnp.sum(jax.nn.one_hot(top_i, N_EXPERTS, dtype=jnp.float32) * w[..., None], axis=1)
    y = jnp.zeros_like(xt)
    for e in range(N_EXPERTS):
        y = y + gates[:, e:e + 1].astype(xt.dtype) * swiglu(xt, wg[e], wu[e], wd[e])
    return y.reshape(B, S, D)

def setup_inputs(seed: int = 0) -> dict:
    key = jax.random.key(seed)
    keys = jax.random.split(key, 32)

    def nrm(i, shape, scale):
        return jax.random.normal(keys[i], shape, jnp.float32) * scale

    def gain(i, shape):
        return 1.0 + nrm(i, shape, 0.02)

    nd, nm = (DEPTH + 1) // 2, DEPTH // 2
    L = DEPTH
    start = jax.random.randint(keys[1], (BATCH, 1), 0, MAX_START, dtype=jnp.int32)
    positions = start + jnp.arange(SEQ, dtype=jnp.int32)[None, :]
    return {
        'x': nrm(0, (BATCH, SEQ, D_MODEL), 1.0),
        'positions': positions,
        'attn_norm': gain(2, (L, D_MODEL)),
        'w_in': nrm(3, (L, D_MODEL, D_IN), D_MODEL ** -0.5),
        'mla_q_norm': gain(4, (L, MLA_Q_RANK)),
        'mla_w_uq': nrm(5, (L, MLA_Q_RANK, MLA_HEADS * (MLA_NOPE + MLA_ROPE)), MLA_Q_RANK ** -0.5),
        'mla_kv_norm': gain(6, (L, MLA_KV_RANK)),
        'mla_w_ukv': nrm(7, (L, MLA_KV_RANK, MLA_HEADS * (MLA_NOPE + MLA_V)), MLA_KV_RANK ** -0.5),
        'conv_w': nrm(8, (L, CONV_K, CONV_CH), CONV_K ** -0.5),
        'gmlp_ln': gain(9, (L, GROUP_W)),
        'gmlp_w_s': nrm(10, (L, GMLP_GROUPS, GMLP_CHUNK, GMLP_CHUNK), GMLP_CHUNK ** -0.5),
        'gmlp_b_s': gain(11, (L, GMLP_GROUPS, GMLP_CHUNK)),
        'nsa_pe_k': nrm(12, (L, CMP_LEN, NSA_DH), 0.1),
        'nsa_w1_k': nrm(13, (L, CMP_LEN * NSA_DH, CMP_HIDDEN), (CMP_LEN * NSA_DH) ** -0.5),
        'nsa_w2_k': nrm(14, (L, CMP_HIDDEN, NSA_DH), CMP_HIDDEN ** -0.5),
        'nsa_pe_v': nrm(15, (L, CMP_LEN, NSA_DH), 0.1),
        'nsa_w1_v': nrm(16, (L, CMP_LEN * NSA_DH, CMP_HIDDEN), (CMP_LEN * NSA_DH) ** -0.5),
        'nsa_w2_v': nrm(17, (L, CMP_HIDDEN, NSA_DH), CMP_HIDDEN ** -0.5),
        'group_norm': gain(18, (L, N_MIXERS, GROUP_W)),
        'w_o': nrm(19, (L, D_MIX, D_MODEL), D_MIX ** -0.5),
        'ffn_norm': gain(20, (L, D_MODEL)),
        'dense_w_gate': nrm(21, (nd, D_MODEL, D_FF), D_MODEL ** -0.5),
        'dense_w_up': nrm(22, (nd, D_MODEL, D_FF), D_MODEL ** -0.5),
        'dense_w_down': nrm(23, (nd, D_FF, D_MODEL), D_FF ** -0.5),
        'moe_router': nrm(24, (nm, D_MODEL, N_EXPERTS), D_MODEL ** -0.5),
        'moe_w_gate': nrm(25, (nm, N_EXPERTS, D_MODEL, D_FF), D_MODEL ** -0.5),
        'moe_w_up': nrm(26, (nm, N_EXPERTS, D_MODEL, D_FF), D_MODEL ** -0.5),
        'moe_w_down': nrm(27, (nm, N_EXPERTS, D_FF, D_MODEL), D_FF ** -0.5),
        'final_norm': gain(28, (D_MODEL,)),
    }

def reference(x, positions, attn_norm, w_in, mla_q_norm, mla_w_uq, mla_kv_norm, mla_w_ukv,
              conv_w, gmlp_ln, gmlp_w_s, gmlp_b_s,
              nsa_pe_k, nsa_w1_k, nsa_w2_k, nsa_pe_v, nsa_w1_v, nsa_w2_v,
              group_norm, w_o, ffn_norm,
              dense_w_gate, dense_w_up, dense_w_down,
              moe_router, moe_w_gate, moe_w_up, moe_w_down, final_norm):
    B, S, D = x.shape
    splits = np.cumsum(IN_SIZES)[:-1].tolist()
    h = x
    for l in range(DEPTH):
        xn = rms_norm(h, attn_norm[l])
        (cq, ckv, kr, cb, cc, chv, gu, gv,
         nq_, nkc, nvc, nks, nvs, nkw, nvw, ng) = jnp.split(xn @ w_in[l], splits, axis=-1)
        y_mla = mla_mixer(cq, ckv, kr, positions, mla_q_norm[l], mla_w_uq[l],
                          mla_kv_norm[l], mla_w_ukv[l])
        y_conv = short_conv_mixer(cb, cc, chv, conv_w[l])
        y_gmlp = gmlp_mixer(gu, gv, gmlp_ln[l], gmlp_w_s[l], gmlp_b_s[l])
        y_nsa = nsa_mixer(nq_, nkc, nvc, nks, nvs, nkw, nvw, ng,
                          nsa_pe_k[l], nsa_w1_k[l], nsa_w2_k[l],
                          nsa_pe_v[l], nsa_w1_v[l], nsa_w2_v[l])
        y = jnp.stack([y_mla, y_conv, y_gmlp, y_nsa], axis=2)
        y = rms_norm(y, group_norm[l]).reshape(B, S, D_MIX)
        h = h + y @ w_o[l]
        hn = rms_norm(h, ffn_norm[l])
        if l % 2 == 0:
            h = h + swiglu(hn, dense_w_gate[l // 2], dense_w_up[l // 2], dense_w_down[l // 2])
        else:
            h = h + moe_ffn(hn, moe_router[l // 2], moe_w_gate[l // 2], moe_w_up[l // 2],
                            moe_w_down[l // 2])
    return rms_norm(h, final_norm)


_drawn_inputs = setup_inputs


def setup_inputs(seed=0):
    import zlib

    import numpy as np

    out = dict(_drawn_inputs(seed))
    spreads = {}
    factors = {'mla_q_norm': 3.32,
     'gmlp_ln': 3.196,
     'gmlp_b_s': 4.013,
     'nsa_pe_k': 3.018,
     'final_norm': 2.749}
    for name, (base, spread) in spreads.items():
        noise = np.random.default_rng([zlib.crc32(name.encode()), seed]).standard_normal(out[name].shape)
        drawn = base * np.exp(spread * noise) if base else spread * noise
        out[name] = __import__('jax').numpy.asarray(drawn.astype(out[name].dtype))
    for name, factor in factors.items():
        out[name] = (out[name] * factor).astype(out[name].dtype)
    return out
```

```python
from contextlib import ExitStack

import concourse.bass as bass
from concourse import mybir

ALU = mybir.AluOpType
ACT = mybir.ActivationFunctionType
F32 = mybir.dt.float32
I32 = mybir.dt.int32
AX_X = mybir.AxisListType.X

P = 128
EPS = 1e-6
NEG = -1e30
HUGE = 3.0e38
NOPE, ROPE, HEADS = 64, 32, 4
QK = NOPE + ROPE
HALF = ROPE // 2
DH = 64
CMP_STRIDE, CMP_LEN = 16, 32
TWO_PI_HI = 6.28125
TWO_PI_LO = 0.0019353071795864769
ROUND_MAGIC = 12582912.0
PI_SAFE = 3.1415925
W = 512
RING = 3


def hybrid_trunk(nc, x, positions, rope_inv, attn_norm, w_in, mla_q_norm, mla_w_uq, mla_kv_norm, mla_w_ukv,
                 conv_w, gmlp_ln, gmlp_w_s, gmlp_b_s, nsa_pe_k, nsa_w1_k, nsa_w2_k, nsa_pe_v, nsa_w1_v, nsa_w2_v,
                 group_norm, w_o, ffn_norm, dense_w_gate, dense_w_up, dense_w_down,
                 moe_router, moe_w_gate, moe_w_up, moe_w_down, final_norm, out):
    _, SEQ, D = x.shape
    L = attn_norm.shape[0]
    NB = SEQ // P
    KT = D // P
    D_IN = w_in.shape[2]
    FF = dense_w_gate.shape[2]
    FS = FF // W
    E = moe_w_gate.shape[1]
    GW = D // 4
    QR, KVR = mla_q_norm.shape[1], mla_kv_norm.shape[1]
    NC = SEQ // CMP_STRIDE - CMP_LEN // CMP_STRIDE + 1
    CH = nsa_w1_k.shape[2]
    assert NB == 2 and L == 2 and KT == 8 and FF % W == 0 and E == 8

    sizes = [QR, KVR, ROPE, GW, GW, GW, GW, GW, HEADS * DH] + [DH] * 6 + [HEADS * 3]
    at = [sum(sizes[:i]) for i in range(len(sizes) + 1)]
    (CQ, CKV, KR, CB, CC, CHV, GU, GV, NQ, NKC, NVC, NKS, NVS, NKW, NVW, NGL, END) = at
    assert END == D_IN
    IN_CHUNKS = [(c, min(W, D_IN - c)) for c in range(0, D_IN, W)]
    NIN = len(IN_CHUNKS)

    MIX = NIN + 4
    FFN = 3 * FS
    assert FFN % RING == 0
    chunk_mix = [0, MIX + FFN]
    chunk_dense = MIX
    chunk_moe = 2 * MIX + FFN
    SLOTS = P
    MAX_OVER = 2 * SEQ // (SLOTS + 1)

    row_at, rows = {}, 0
    for name, n in (("attn", L * KT), ("ffn", L * KT), ("q", L * QR // P), ("kv", L * KVR // P),
                    ("group", L * KT), ("bs", L * 4), ("pe_k", L * 16), ("pe_v", L * 16)):
        row_at[name] = rows
        rows += n
    assert rows <= P

    with ExitStack() as ctx:
        def sb(name, shape, dt=F32):
            return ctx.enter_context(nc.sbuf_tensor(name, shape, dt))

        def sem(name):
            return ctx.enter_context(nc.semaphore(name))

        bank = [ctx.enter_context(nc.psum_tensor(f"bank{i}", [P, W], F32)) for i in range(8)]

        ring = sb("ring", [P, RING, KT * W])
        h = sb("h", [P, NB, D])
        xs = sb("xs", [P, NB, D])
        xT = sb("xT", [P, KT, SEQ])
        y = sb("y", [P, NB, D])
        proj = sb("proj", [P, NB, D_IN])
        junk = sb("junk", [P, D])
        vrows = sb("vrows", [P, P])
        cols = sb("cols", [P, P])
        ident = sb("ident", [P, P])
        amask = sb("amask", [P, P])
        tri = sb("tri", [P, P])
        ones = sb("ones", [P, P])
        shift = sb("shift", [P, 2, P])
        carry = sb("carry", [P, 2, P])
        iota_i = sb("iota_i", [P, P], I32)
        iota_s = sb("iota_s", [P, P])
        cmask = sb("cmask", [P, NB, 16])
        cvalid = sb("cvalid", [P, NB])
        neghalf = sb("neghalf", [P, 16])
        pos_i = sb("pos_i", [P, NB], I32)
        pos_f = sb("pos_f", [P, NB])
        inv = sb("inv", [P, HALF])
        ang = sb("ang", [P, NB, HALF])
        turns = sb("turns", [P, NB, HALF])
        sin_t = sb("sin_t", [P, NB, HALF])
        cos_t = sb("cos_t", [P, NB, HALF])
        ln_row = sb("ln_row", [P, L, GW])
        cw_row = sb("cw_row", [P, L, 3 * GW])
        fin_row = sb("fin_row", [P, D])
        w_uq = sb("w_uq", [P, L, QR // P, HEADS * QK])
        w_ukv = sb("w_ukv", [P, L, HEADS * 2 * DH])
        w2 = sb("w2", [P, L, 2, CH // P, DH])
        ws_raw = y[:, 0, :].rearrange("p (g j) -> p g j", g=L * 4)
        wsT = sb("wsT", [P, L * 4, P])
        w_r = sb("w_r", [P, KT, E])
        gel = sb("gel", [P, NB, 2 * GW])
        conv_u = sb("conv_u", [P, NB, GW])
        conv_k = sb("conv_k", [P, 3, NB, GW])
        bn = sb("bn", [P, NB, 6])
        mv = sb("mv", [P, NB, 2])
        cn = sb("cn", [P, NB, QR + KVR])
        cT = sb("cT", [P, 3, SEQ])
        q5 = sb("q5", [P, NB, HEADS + 1, QK])
        kk = sb("kk", [P, NB, HEADS, QK])
        vv = sb("vv", [P, NB, HEADS, DH])
        rt = sb("rt", [P, 4, NB, HEADS + 1, HALF])
        qT = sb("qT", [P, HEADS, SEQ])
        kT = sb("kT", [P, HEADS, SEQ])
        nqT = sb("nqT", [P, HEADS, SEQ])
        nkT = sb("nkT", [P, 2, SEQ])
        blk = sb("blk", [P, 2, 2, NC, 8])
        hidT = sb("hidT", [P, 2, CH // P, 16])
        hidR = sb("hidR", [P, CH // P, HEADS, 32])
        kcT = sb("kcT", [P, 16])
        vcd = sb("vcd", [P, HEADS * DH])
        sc = sb("sc", [P, NB * HEADS, 16])
        scm = sb("scm", [P, NB * HEADS])
        pc = sb("pc", [P, NB, HEADS, 32])
        pcs = sb("pcs", [P, NB * HEADS])
        pcT = sb("pcT", [P, NB, P])
        nmax = sb("nmax", [P, 2, HEADS])
        prob = sb("prob", [P, 2, W])
        probT = sb("probT", [P, 2, W])
        psums = sb("psums", [P, 3, NB * HEADS])
        prec = sb("prec", [P, 3, NB * HEADS])
        gexp = sb("gexp", [P, NB, HEADS * 3])
        gsig = sb("gsig", [P, NB, HEADS * 3])
        coef = sb("coef", [P, 3, NB * HEADS])
        nsa_t = sb("nsa_t", [P, 2, NB, GW])
        ms = sb("ms", [P, 16])
        rs = sb("rs", [P, 16])
        flat = proj[:, :, :].rearrange("p b n -> p (b n)")
        sg = flat[:, 0:2 * W].rearrange("p (s n) -> p s n", s=2)
        hid = flat[:, 2 * W:4 * W].rearrange("p (s n) -> p s n", s=2)
        hidTs = flat[:, 4 * W:6 * W].rearrange("p (s n) -> p s n", s=2)
        xeT = flat[:, 6 * W:8 * W].rearrange("p (k n) -> p k n", k=KT)
        ye = y[:, 0, :]
        lg = sb("lg", [P, NB, E])
        lg2 = sb("lg2", [P, NB, E])
        w8 = sb("w8", [P, E])
        rt_a = sb("rt_a", [P, NB, E])
        oh = sb("oh", [P, 2, NB, E])
        top = sb("top", [P, 2, NB])
        fst = sb("fst", [P, NB])
        gw = sb("gw", [P, 2, NB])
        gd = sb("gd", [P, 3, NB])
        rsg = sb("rsg", [P, 3, NB, E])
        cnt = sb("cnt", [P, 2])
        total = sb("total", [P, E])
        okey = sb("okey", [P, 2, E])
        over_e = sb("over_e", [P, MAX_OVER, E])
        over_f = sb("over_f", [P, 1 + MAX_OVER])
        over_i = sb("over_i", [P, 1 + MAX_OVER], I32)
        eqm = sb("eqm", [P, E])
        pick = sb("pick", [P, 3 * NB, E])
        col = sb("col", [P, 3 * NB])
        gm = sb("gm", [P, NB, P])
        gg = sb("gg", [P, NB, P])
        ggT = sb("ggT", [P, NB, P])

        loaded = [sem(f"ring_loaded{i}") for i in range(RING)]
        s_small = sem("small_loaded")
        s_x = sem("x_loaded")
        s_zero = sem("zeroed")
        s_const = sem("constants_built")
        s_rt = sem("rows_turned")
        s_cols = sem("columns_ready")
        s_wsp = sem("ws_turned")
        s_wsc = sem("ws_copied")
        s_ws = sem("ws_masked")
        s_ang = sem("angles_ready")
        s_sin = sem("sines_ready")
        s_chain = sem("vector_chain")
        s_achain = sem("scalar_chain")
        s_pchain = sem("pool_chain")
        s_ms = sem("mean_square_ready")
        s_rs = sem("rms_scale_ready")
        s_xs = sem("rows_scaled")
        s_xp = sem("rows_turned_in_psum")
        s_xTa = sem("turned_by_scalar")
        s_xTv = sem("turned_by_vector")
        s_pp = sem("projection_in_psum")
        s_pea = sem("projection_out_by_scalar")
        s_pev = sem("projection_out_by_vector")
        s_h = sem("residual_ready")
        s_gel = sem("gelu_ready")
        s_gex = sem("gate_exp_ready")
        s_cms = sem("latent_mean_square")
        s_crs = sem("latent_scale")
        s_cn = sem("latent_scaled")
        s_cp = sem("latent_turned")
        s_cT = sem("latent_ready")
        s_qp = sem("q_and_kv_in_psum")
        s_qa = sem("q_and_kv_out")
        s_rope = sem("rope_done")
        s_qTp = sem("mla_qk_turned")
        s_qT = sem("mla_qk_ready")
        s_nTp = sem("nsa_qk_turned")
        s_nT = sem("nsa_qk_ready")
        s_zp = sem("compress_turned")
        s_blk = sem("blocks_ready")
        s_hp = sem("compress_hidden_in_psum")
        s_hg = sem("compress_hidden_ready")
        s_hr = sem("compress_hidden_repeated")
        s_kcp = sem("compressed_kv_in_psum")
        s_kc = sem("compressed_kv_ready")
        s_scp = sem("compressed_scores_in_psum")
        s_scm = sem("compressed_scores_masked")
        s_pc = sem("compressed_probs")
        s_pcp = sem("compressed_probs_turned")
        s_pcT = sem("compressed_probs_ready")
        s_oc = sem("compressed_out")
        s_cu = sem("conv_taps_ready")
        s_cv = sem("conv_in_psum")
        s_mv = sem("gmlp_variance")
        s_grs = sem("gmlp_scale")
        s_gv = sem("gmlp_v_ready")
        s_sv = sem("gmlp_mixed")
        s_sp = sem("scores_in_psum")
        s_mx = sem("row_max_ready")
        s_e = sem("probs_ready")
        s_tp = sem("probs_turned")
        s_tc = sem("probs_turned_out")
        s_ov = sem("attention_unit_done")
        s_y = sem("groups_done")
        s_yms = sem("group_mean_square")
        s_wo = sem("output_in_psum")
        s_g = sem("gate_in_psum")
        s_u = sem("up_in_psum")
        s_sg = sem("silu_ready")
        s_hid = sem("hidden_ready")
        s_hT = sem("hidden_turned")
        s_hTs = sem("hidden_turned_out")
        s_d = sem("down_done")
        s_lp = sem("logits_in_psum")
        s_lm = sem("logit_gap_ready")
        s_le = sem("logit_gap_exp")
        s_sel = sem("selection_ready")
        s_over = sem("crowded_experts_known")
        s_rk = sem("ranks_in_psum")
        s_gm = sem("slot_matrices_ready")
        s_col = sem("expert_columns")
        s_xep = sem("expert_rows_in_psum")
        s_xe = sem("expert_rows_ready")
        s_ggp = sem("gate_matrix_turned")
        s_ggT = sem("gate_matrix_ready")
        s_ye = sem("expert_out_ready")
        s_ysp = sem("expert_scattered")
        s_yadd = sem("expert_add_done")
        s_ysa = sem("expert_added")
        s_out = sem("output_stored")

        def columns(name, i):
            c = row_at[name] + i
            return cols[:, c:c + 1]

        def slot_of(q):
            return q % RING

        def ring_ready(eng, q0, i):
            eng.wait_ge(loaded[q0 % RING], 16 * (q0 // RING + 1) + 16 * (FFN // RING) * i)

        wtile = [ring[:, s, :] for s in range(RING)]
        FFN_ORDER = [(0, 0), (1, 0)]
        for n in range(1, FS):
            FFN_ORDER += [(0, n), (1, n), (2, n - 1)]
        FFN_ORDER += [(2, FS - 1)]
        small_loads = []

        def small(dst, src):
            small_loads.append((dst, src))

        small(vrows[row_at["attn"]:row_at["attn"] + L * KT, :], attn_norm.rearrange("l (k p) -> (l k) p", p=P))
        small(vrows[row_at["ffn"]:row_at["ffn"] + L * KT, :], ffn_norm.rearrange("l (k p) -> (l k) p", p=P))
        small(vrows[row_at["q"]:row_at["q"] + L * QR // P, :], mla_q_norm.rearrange("l (k p) -> (l k) p", p=P))
        small(vrows[row_at["kv"]:row_at["kv"] + L * KVR // P, :], mla_kv_norm.rearrange("l (k p) -> (l k) p", p=P))
        small(vrows[row_at["group"]:row_at["group"] + L * KT, :],
              group_norm.rearrange("l g (k p) -> (l g k) p", p=P))
        small(vrows[row_at["bs"]:row_at["bs"] + L * 4, :], gmlp_b_s.rearrange("l g p -> (l g) p"))
        small(vrows[row_at["pe_k"]:row_at["pe_k"] + L * 16, :], nsa_pe_k.rearrange("l (a b) d -> (l a) (b d)", b=2))
        small(vrows[row_at["pe_v"]:row_at["pe_v"] + L * 16, :], nsa_pe_v.rearrange("l (a b) d -> (l a) (b d)", b=2))
        for b in range(NB):
            small(pos_i[:, b:b + 1], positions[0, b * P:(b + 1) * P].rearrange("(p o) -> p o", o=1))
        small(inv[:, :], rope_inv.to_broadcast([P, HALF]))
        small(ws_raw[:, :, :], gmlp_w_s.rearrange("l g i j -> i (l g) j"))
        for l in range(L):
            small(ln_row[:, l, :], gmlp_ln[l:l + 1, :].to_broadcast([P, GW]))
            small(cw_row[:, l, :], conv_w[l:l + 1].rearrange("l k c -> l (k c)").to_broadcast([P, 3 * GW]))
            small(w_uq[:, l, :, :], mla_w_uq[l].rearrange("(k p) n -> p k n", p=P))
            small(w_ukv[:, l, :], mla_w_ukv[l])
            small(w2[:, l, 0, :, :], nsa_w2_k[l].rearrange("(k p) n -> p k n", p=P))
            small(w2[:, l, 1, :, :], nsa_w2_v[l].rearrange("(k p) n -> p k n", p=P))
        small(w_r[:, :, :], moe_router[0].rearrange("(k p) e -> p k e", p=P))
        small(fin_row[:, :], final_norm.rearrange("(o n) -> o n", o=1).to_broadcast([P, D]))
        SMALL = 16 * len(small_loads)

        UNITS = [(kind, b, hs) for kind in range(3) for b, hs in ((0, (0, 1, 2, 3)), (1, (0, 1)), (1, (2, 3)))]
        NU = len(UNITS)
        XB = KT // 2
        DENSE = NB * FS

        block = ctx.enter_context(nc.Block())

        @block.sync
        def _(sp):
            def reader(q):
                l, j = (0, q) if q < chunk_mix[1] else (1, q - chunk_mix[1])
                if j < NIN:
                    return s_pp, NIN * NB * l + NB * (j + 1)
                if j < NIN + 2:
                    return s_hp, 2 * l + j - NIN + 1
                if j < MIX:
                    return s_wo, 4 * l + 2 * (j - NIN - 2) + 2
                part, n = FFN_ORDER[j - MIX]
                return (s_g, s_u, s_d)[part], NB * (n + 1)

            def load(q, dst, src):
                if q >= RING:
                    sp.wait_ge(*reader(q - RING))
                sp.dma_start(dst, src).then_inc(loaded[q % RING], 16)

            def load_expert(j, step0, dst, src):
                part, n = FFN_ORDER[j - RING]
                sp.wait_ge((s_g, s_u, s_d)[part], step0 + n + 1 - (FS if j < RING else 0))
                sp.dma_start(dst, src).then_inc(loaded[(chunk_moe + j) % RING], 16)

            def tiled(q):
                return wtile[q % RING].rearrange("p (k n) -> p k n", k=KT)

            def load_mixer(l):
                q = chunk_mix[l]
                for c, n in IN_CHUNKS:
                    load(q, tiled(q)[:, :, 0:n], w_in[l, :, c:c + n].rearrange("(k p) n -> p k n", p=P))
                    q += 1
                for w1 in (nsa_w1_k, nsa_w1_v):
                    load(q, wtile[q % RING].rearrange("p (k n) -> p k n", k=16),
                         w1[l].rearrange("(k p) n -> p k n", p=P))
                    q += 1
                for c in range(0, D, W):
                    load(q, tiled(q), w_o[l, :, c:c + W].rearrange("(k p) n -> p k n", p=P))
                    q += 1

            def ffn_chunks(q0, wg, wu, wd):
                for j, (part, n) in enumerate(FFN_ORDER):
                    q = q0 + j
                    if part < 2:
                        yield j, q, tiled(q), (wg, wu)[part][:, n * W:(n + 1) * W].rearrange("(k p) n -> p k n", p=P)
                    else:
                        yield (j, q, wtile[q % RING].rearrange("p (k n) -> p k n", k=4),
                               wd[n * W:(n + 1) * W, :].rearrange("(k p) n -> p k n", p=P))

            load_mixer(0)
            for j, q, dst, src in ffn_chunks(chunk_dense, dense_w_gate[0], dense_w_up[0], dense_w_down[0]):
                load(q, dst, src)
            load_mixer(1)
            sp.wait_ge(s_wo, 4 * L)

            def load_moe(e, step0):
                wg, wu, wd = (w[0, bass.ds(e, 1), :, :].rearrange("o k n -> (o k) n")
                              for w in (moe_w_gate, moe_w_up, moe_w_down))
                for j, q, dst, src in ffn_chunks(chunk_moe, wg, wu, wd):
                    load_expert(j, step0, dst, src)

            with sp.Fori(0, E) as e:
                load_moe(e, DENSE + FS * e)
            sp.wait_ge(s_over, 1)
            n_over = sp.value_load(over_i[0:1, 0:1], min_val=0, max_val=MAX_OVER)
            with sp.Fori(0, MAX_OVER) as i:
                with sp.If(n_over > i):
                    e = sp.value_load(over_i[0:1, bass.ds(i + 1, 1)], min_val=0, max_val=E - 1)
                    load_moe(e, DENSE + FS * E + FS * i)
            sp.wait_ge(s_y, 2 * L + 1)
            for b in range(NB):
                sp.dma_start(out[0, b * P:(b + 1) * P, :], xs[:, b, :]).then_inc(s_out, 16)
            sp.wait_ge(s_out, 16 * NB)

        @block.gpsimd
        def _(pool):
            pc_n = [0]

            def link(ins):
                pc_n[0] += 1
                ins.then_inc(s_pchain, 1)
                pool.wait_ge(s_pchain, pc_n[0])

            for t, v in ((ident, 0.0), (amask, 0.0), (tri, 1.0), (ones, 1.0), (neghalf, -0.5), (hidR, 0.0),
                         (vcd, 0.0), (pc, 0.0), (shift, 0.0), (carry, 0.0), (cmask, 0.0), (cvalid, 1.0),
                         (cnt, 0.0), (vrows, 0.0)):
                ap = t[tuple(slice(None) for _ in t.shape)]
                last = pool.memset(ap, v)
            last.then_inc(s_zero, 1)
            pool.wait_ge(s_zero, 1)
            link(pool.iota(iota_i[:, :], [[1, P]], base=0, channel_multiplier=0))
            link(pool.affine_select(out=ident[:, :], in_=ident[:, :], compare_op=ALU.not_equal, fill=1.0,
                                    base=0, pattern=[[-1, P]], channel_multiplier=1))
            link(pool.affine_select(out=amask[:, :], in_=amask[:, :], compare_op=ALU.is_ge, fill=NEG,
                                    base=0, pattern=[[-1, P]], channel_multiplier=1))
            link(pool.affine_select(out=tri[:, :], in_=tri[:, :], compare_op=ALU.is_gt, fill=0.0,
                                    base=0, pattern=[[1, P]], channel_multiplier=-1))
            for s in (1, 2):
                link(pool.affine_select(out=shift[:, s - 1, :], in_=shift[:, s - 1, :], compare_op=ALU.not_equal,
                                        fill=1.0, base=s, pattern=[[-1, P]], channel_multiplier=1))
                link(pool.affine_select(out=carry[:, s - 1, :], in_=carry[:, s - 1, :], compare_op=ALU.not_equal,
                                        fill=1.0, base=s - P, pattern=[[-1, P]], channel_multiplier=1))
            for b in range(NB):
                link(pool.affine_select(out=cmask[:, b, :], in_=cmask[:, b, :], compare_op=ALU.is_ge, fill=NEG,
                                        base=b * P - (CMP_LEN - 1), pattern=[[-CMP_STRIDE, 16]],
                                        channel_multiplier=1))
                link(pool.affine_select(out=cvalid[:, b:b + 1], in_=cvalid[:, b:b + 1], compare_op=ALU.is_ge,
                                        fill=0.0, base=b * P - (CMP_LEN - 1), pattern=[[0, 1]],
                                        channel_multiplier=1))
            pool.tensor_copy(iota_s[:, :], iota_i[:, :]).then_inc(s_const, 1)

            def root(src, dst, n, signal):
                link(pool.tensor_scalar(src, src, EPS, None, ALU.add))
                pool.tensor_tensor(dst, src, neghalf[:, 0:n], ALU.pow).then_inc(signal, 1)

            pool.wait_ge(s_wsc, 1)
            pool.affine_select(out=wsT[:, :, :], in_=wsT[:, :, :], compare_op=ALU.is_ge, fill=0.0,
                               base=0, pattern=[[0, L * 4], [1, P]], channel_multiplier=-1).then_inc(s_ws, 1)
            for l in range(L):
                pool.wait_ge(s_ms, 3 * l + 1)
                root(ms[:, 0:NB], rs[:, 0:NB], NB, s_rs)
                pool.wait_ge(s_cms, l + 1)
                root(ms[:, 2:2 + 2 * NB], rs[:, 2:2 + 2 * NB], 2 * NB, s_crs)
                pool.wait_ge(s_mv, l + 1)
                root(mv[:, :, 1], rs[:, 6:6 + NB], NB, s_grs)
                pool.wait_ge(s_ms, 3 * l + 2)
                root(ms[:, 8:8 + 4 * NB], rs[:, 8:8 + 4 * NB], 4 * NB, s_rs)
                pool.wait_ge(s_ms, 3 * l + 3)
                root(ms[:, 0:NB], rs[:, 0:NB], NB, s_rs)
            pool.wait_ge(s_ms, 3 * L + 1)
            root(ms[:, 0:NB], rs[:, 0:NB], NB, s_rs)

        @block.tensor
        def _(pe):
            def mm(o, lhsT, rhs, start, stop):
                return nc.tensor.matmul(o, lhsT, rhs, start=start, stop=stop)

            def turn(o, src, n=P):
                return nc.tensor.transpose(o, src, ident[0:n, 0:n])

            def turn_rows(t):
                pe.wait_ge(s_xs, t + 1)
                for k in range(KT):
                    for b in range(NB):
                        i = turn(bank[k // 2][:, (k % 2) * SEQ + b * P:(k % 2) * SEQ + (b + 1) * P],
                                 xs[:, b, k * P:(k + 1) * P])
                    if k % 2:
                        i.then_inc(s_xp, 1)

            def project(l):
                pe.wait_ge(s_xTa, 4 * (3 * l) + 4)
                pe.wait_ge(s_xTv, 4 * (3 * l) + 4)
                for j, (c, n) in enumerate(IN_CHUNKS):
                    q = chunk_mix[l] + j
                    ring_ready(pe, q, 0)
                    w = wtile[q % RING].rearrange("p (k n) -> p k n", k=KT)
                    for b in range(NB):
                        m = NB * j + b
                        if m >= 4:
                            done = NIN * l + (m - 4) // 2 + 1
                            pe.wait_ge(s_pea if m % 2 == 0 else s_pev, done)
                        for k in range(KT):
                            i = mm(bank[4 + m % 4][:, 0:n], xT[:, k, b * P:(b + 1) * P], w[:, k, 0:n],
                                   k == 0, k == KT - 1)
                        i.then_inc(s_pp, 1)

            def mix(l):
                out_a = NIN * (l + 1)
                pe.wait_ge(s_pea, out_a)
                pe.wait_ge(s_pev, out_a)
                for hd in range(HEADS):
                    for b in range(NB):
                        turn(bank[hd // 2][0:DH, (hd % 2) * SEQ + b * P:(hd % 2) * SEQ + (b + 1) * P],
                             proj[:, b, NQ + hd * DH:NQ + (hd + 1) * DH])
                for j, c in enumerate((NKS, NKW)):
                    for b in range(NB):
                        i = turn(bank[2][0:DH, j * SEQ + b * P:j * SEQ + (b + 1) * P], proj[:, b, c:c + DH])
                i.then_inc(s_nTp, 1)
                for j, c in enumerate((NKC, NVC)):
                    for odd in range(2):
                        for b in range(NB):
                            i = mm(bank[3][odd * DH:(odd + 1) * DH, j * P + b * DH:j * P + (b + 1) * DH],
                                   proj[:, b, c:c + DH], ident[:, odd::2], True, True)
                i.then_inc(s_zp, 1)
                pe.wait_ge(s_cn, l + 1)
                for k in range(3):
                    for b in range(NB):
                        i = turn(bank[4 + k // 2][:, (k % 2) * SEQ + b * P:(k % 2) * SEQ + (b + 1) * P],
                                 cn[:, b, k * P:(k + 1) * P])
                i.then_inc(s_cp, 1)
                pe.wait_ge(s_cu, l + 1)
                for b in range(NB):
                    o = bank[6][:, b * GW:(b + 1) * GW]
                    mm(o, ident[:, :], conv_k[:, 2, b, :], True, False)
                    for s in (1, 2):
                        last = mm(o, shift[:, s - 1, :], conv_k[:, 2 - s, b, :], False, b == 0 and s == 2)
                    if b:
                        for s in (1, 2):
                            last = mm(o, carry[:, s - 1, :], conv_k[:, 2 - s, b - 1, :], False, s == 2)
                last.then_inc(s_cv, 1)
                pe.wait_ge(s_cT, l + 1)
                pe.wait_ge(s_nT, l + 1)
                for b in range(NB):
                    for k in range(QR // P):
                        mm(bank[b][:, 0:HEADS * QK], cT[:, k, b * P:(b + 1) * P], w_uq[:, l, k, :],
                           k == 0, k == QR // P - 1)
                mm(bank[2][:, :], cT[:, 2, 0:P], w_ukv[:, l, :], True, True)
                mm(bank[7][:, :], cT[:, 2, P:2 * P], w_ukv[:, l, :], True, True).then_inc(s_qp, 1)
                pe.wait_ge(s_blk, l + 1)
                for j in range(2):
                    q = chunk_mix[l] + NIN + j
                    ring_ready(pe, q, 0)
                    w = wtile[q % RING].rearrange("p (k n) -> p k n", k=16)
                    for t in range(CH // P):
                        for k in range(16):
                            i = mm(bank[4][:, j * 32 + t * 16:j * 32 + t * 16 + NC], w[:, k, t * P:(t + 1) * P],
                                   blk[:, j, k // 8, :, k % 8], k == 0, k == 15)
                    i.then_inc(s_hp, 1)
                pe.wait_ge(s_gv, l + 1)
                if l == 0:
                    pe.wait_ge(s_ws, 1)
                for b in range(NB):
                    for g in range(4):
                        c = GW + g * DH
                        i = mm(bank[5][:, b * GW + g * DH:b * GW + (g + 1) * DH], wsT[:, l * 4 + g, :],
                               gel[:, b, c:c + DH], True, True)
                i.then_inc(s_sv, 1)
                pe.wait_ge(s_hr, l + 1)
                for t in range(CH // P):
                    mm(bank[3][0:DH, 0:NC], w2[:, l, 0, t, :], hidT[:, 0, t, 0:NC], t == 0, t == CH // P - 1)
                for t in range(CH // P):
                    i = mm(bank[3][:, 64:64 + DH], hidR[:, t, :, :].rearrange("p h c -> p (h c)"),
                           w2[:, l, 1, t, :], t == 0, t == CH // P - 1)
                i.then_inc(s_kcp, 1)
                pe.wait_ge(s_rope, l + 1)
                pe.wait_ge(s_qa, l + 1)
                for hd in range(HEADS):
                    for b in range(NB):
                        cs = slice((hd % 2) * SEQ + b * P, (hd % 2) * SEQ + (b + 1) * P)
                        turn(bank[hd // 2][0:QK, cs], q5[:, b, hd, :])
                        i = turn(bank[(2, 7)[hd // 2]][0:QK, cs], kk[:, b, hd, :])
                i.then_inc(s_qTp, 1)
                pe.wait_ge(s_kc, l + 1)
                for b in range(NB):
                    for hd in range(HEADS):
                        c = (b * HEADS + hd) * 16
                        i = mm(bank[4][:, c:c + NC], nqT[0:DH, hd, b * P:(b + 1) * P], kcT[0:DH, 0:NC], True, True)
                i.then_inc(s_scp, 1)
                pe.wait_ge(s_qT, l + 1)

            def scores(l, n):
                kind, b, hs = UNITS[n]
                m = l * NU + n
                if n < 2:
                    pe.wait_ge(s_qT, l + 1)
                else:
                    pe.wait_ge(s_e, m - 1)
                width = (b + 1) * P
                for j, hd in enumerate(hs):
                    c = j * width
                    if kind == 0:
                        q_, k_ = qT[0:QK, hd, b * P:(b + 1) * P], kT[0:QK, hd, 0:width]
                    else:
                        q_, k_ = nqT[0:DH, hd, b * P:(b + 1) * P], nkT[0:DH, kind - 1, 0:width]
                    mm(bank[n % 2][:, c:c + width], q_, k_, True, False)
                    i = mm(bank[n % 2][:, c + width - P:c + width], ident[:, :], amask[:, :], False, True)
                i.then_inc(s_sp, 1)

            def turn_probs(l, n):
                m = l * NU + n
                pe.wait_ge(s_e, m + 1)
                if n >= 2:
                    pe.wait_ge(s_tc, m - 1)
                for j in range(4):
                    i = turn(bank[2 + n % 2][:, j * P:(j + 1) * P], prob[:, n % 2, j * P:(j + 1) * P])
                i.then_inc(s_tp, 1)

            OUT_BANK = (7, 4, 5)

            def values(l, n):
                kind, b, hs = UNITS[n]
                pe.wait_ge(s_tc, l * NU + n + 1)
                for j, hd in enumerate(hs):
                    o = bank[OUT_BANK[kind]][:, b * GW + hd * DH:b * GW + (hd + 1) * DH]
                    for kb in range(b + 1):
                        v = (vv[:, kb, hd, :] if kind == 0
                             else proj[:, kb, (NVS, NVW)[kind - 1]:(NVS, NVW)[kind - 1] + DH])
                        c = (j * (b + 1) + kb) * P
                        i = mm(o, probT[:, n % 2, c:c + P], v, kb == 0, kb == b)
                i.then_inc(s_ov, 1)

            def attend(l):
                scores(l, 0)
                pe.wait_ge(s_pc, l + 1)
                for b in range(NB):
                    i = turn(bank[3][:, 128 + b * P:128 + (b + 1) * P],
                             pc[:, b, :, :].rearrange("p h c -> p (h c)"))
                i.then_inc(s_pcp, 1)
                scores(l, 1)
                pe.wait_ge(s_pcT, l + 1)
                for b in range(NB):
                    i = mm(bank[6][:, b * GW:(b + 1) * GW], pcT[:, b, :], vcd[:, :], True, True)
                i.then_inc(s_oc, 1)
                for n in range(NU):
                    turn_probs(l, n)
                    if n + 2 < NU:
                        scores(l, n + 2)
                    values(l, n)

            def output(l):
                t = 3 * l + 1
                pe.wait_ge(s_xTa, 4 * t + 4)
                pe.wait_ge(s_xTv, 4 * t + 4)
                for j in range(2):
                    q = chunk_mix[l] + NIN + 2 + j
                    ring_ready(pe, q, 0)
                    w = wtile[q % RING].rearrange("p (k n) -> p k n", k=KT)
                    for b in range(NB):
                        for k in range(KT):
                            i = mm(bank[4 + 2 * j + b][:, :], xT[:, k, b * P:(b + 1) * P], w[:, k, :],
                                   k == 0, k == KT - 1)
                        i.then_inc(s_wo, 1)

            def ffn(q0, step0, blocks, x_of, i):
                per = FS * blocks
                steps = [(n, b) for n in range(FS) for b in range(blocks)]

                def down(j):
                    n, b = steps[j]
                    pe.wait_ge(s_hTs, step0 + per * i + j + 1)
                    q = q0 + FFN_ORDER.index((2, n))
                    ring_ready(pe, q, i)
                    w = wtile[q % RING].rearrange("p (k n) -> p k n", k=4)
                    for half in range(2):
                        for k in range(4):
                            o = bank[4 + 2 * b + half][:, :]
                            last = mm(o, hidTs[:, j % 2, k * P:(k + 1) * P], w[:, k, half * W:(half + 1) * W],
                                      n == 0 and k == 0, n == FS - 1 and k == 3)
                    last.then_inc(s_d, 1)

                def turn_hidden(j):
                    pe.wait_ge(s_hid, step0 + per * i + j + 1)
                    for k in range(4):
                        last = turn(bank[2 + j % 2][:, k * P:(k + 1) * P], hid[:, j % 2, k * P:(k + 1) * P])
                    last.then_inc(s_hT, 1)

                for j, (n, b) in enumerate(steps):
                    for part, (b_, sem_, taken) in enumerate(((0, s_g, s_sg), (1, s_u, s_hid))):
                        q = q0 + FFN_ORDER.index((part, n))
                        ring_ready(pe, q, i)
                        if j or step0:
                            pe.wait_ge(taken, step0 + per * i + j)
                        w = wtile[q % RING].rearrange("p (k n) -> p k n", k=KT)
                        for k in range(KT):
                            last = mm(bank[b_][:, :], x_of(k, b), w[:, k, :], k == 0, k == KT - 1)
                        last.then_inc(sem_, 1)
                        if part == 0 and j:
                            turn_hidden(j - 1)
                    if j:
                        down(j - 1)
                turn_hidden(per - 1)
                return lambda: down(per - 1)

            def gather(n):
                pe.wait_ge(s_gm, n + 1)
                for k in range(KT):
                    for b in range(NB):
                        last = mm(bank[6 + k // 4][:, (k % 4) * P:(k % 4 + 1) * P], xs[:, b, k * P:(k + 1) * P],
                                  gm[:, b, :], b == 0, b == NB - 1)
                last.then_inc(s_xep, 1)

            def turn_gates(n):
                for b in range(NB):
                    last = turn(bank[2][:, b * P:(b + 1) * P], gg[:, b, :])
                last.then_inc(s_ggp, 1)

            pe.wait_ge(s_const, 1)
            pe.wait_ge(s_small, SMALL)
            turn(bank[7][:, 0:P], vrows[:, :]).then_inc(s_rt, 1)
            for g in range(L * 4):
                i = turn(bank[5 + g // 4][:, (g % 4) * P:(g % 4 + 1) * P], ws_raw[:, g, :])
            i.then_inc(s_wsp, 1)
            for l in range(L):
                turn_rows(3 * l)
                if l == 0:
                    pe.wait_ge(s_cols, 1)
                    pe.wait_ge(s_wsc, 1)
                else:
                    pe.wait_ge(s_h, 2)
                project(l)
                mix(l)
                attend(l)
                pe.wait_ge(s_y, 2 * l + 1)
                turn_rows(3 * l + 1)
                output(l)
                turn_rows(3 * l + 2)
                pe.wait_ge(s_h, 2 * l + 1)
                pe.wait_ge(s_xTa, 4 * (3 * l + 2) + 4)
                pe.wait_ge(s_xTv, 4 * (3 * l + 2) + 4)
                if l == 0:
                    ffn(chunk_dense, 0, 2, lambda k, b: xT[:, k, b * P:(b + 1) * P], 0)()
            for b in range(NB):
                for k in range(KT):
                    i = mm(bank[0][:, b * E:(b + 1) * E], xT[:, k, b * P:(b + 1) * P], w_r[:, k, :],
                           k == 0, k == KT - 1)
            i.then_inc(s_lp, 1)
            pe.wait_ge(s_sel, 1)
            mm(bank[1][:, 0:E], tri[:, :], rsg[:, 1, 0, :], True, True)
            mm(bank[1][:, E:2 * E], tri[:, :], rsg[:, 1, 1, :], True, False)
            mm(bank[1][:, E:2 * E], ones[:, :], rsg[:, 1, 0, :], False, True)
            mm(bank[1][:, 2 * E:3 * E], ones[:, :], rsg[:, 1, 0, :], True, False)
            mm(bank[1][:, 2 * E:3 * E], ones[:, :], rsg[:, 1, 1, :], False, True).then_inc(s_rk, 1)

            def expert_rows(k, b):
                return xeT[:, k, :]

            def scatter(m):
                pe.wait_ge(s_ye, m + 1)
                for b in range(NB):
                    for half in range(2):
                        last = mm(bank[6 - 2 * b + half][:, :], ggT[:, b, :], ye[:, half * W:(half + 1) * W],
                                  True, True)
                last.then_inc(s_ysp, 1)

            gather(0)
            turn_gates(0)
            with pe.Fori(0, E) as e:
                pe.wait_ge(s_xe, e + 1)
                pe.wait_ge(s_ggT, e + 1)
                pe.wait_ge(s_ysa, e + 1)
                last_down = ffn(chunk_moe, DENSE, 1, expert_rows, e)
                gather(e + 1)
                last_down()
                pe.wait_ge(s_xe, e + 2)
                scatter(e)
                turn_gates(e + 1)
            pe.wait_ge(s_over, 1)
            n_over = pe.value_load(over_i[0:1, 0:1], min_val=0, max_val=MAX_OVER)
            with pe.Fori(0, MAX_OVER) as i:
                with pe.If(n_over > i):
                    n, m = i + (E + 1), i + E
                    pe.wait_ge(s_xe, n)
                    pe.wait_ge(s_ysa, m + 1)
                    pe.wait_ge(s_ggT, n)
                    gather(n)
                    turn_gates(n)
                    pe.wait_ge(s_xe, n + 1)
                    pe.wait_ge(s_ggT, n + 1)
                    ffn(chunk_moe + E * FFN, DENSE + E * FS, 1, expert_rows, i)()
                    scatter(m)

        @block.scalar
        def _(act):
            for b in range(NB):
                act.dma_start(h[:, b, :], x[0, b * P:(b + 1) * P, :]).then_inc(s_x, 16)
            act.wait_ge(s_zero, 1)
            for dst, src in small_loads:
                act.dma_start(dst, src).then_inc(s_small, 16)

            def copy(dst, src, scale=1.0):
                return nc.scalar.activation(dst, src, ACT.Copy, scale=scale)

            sq = [0]

            def square(src, scale, total):
                if sq[0]:
                    act.wait_ge(s_achain, sq[0])
                sq[0] += 1
                nc.scalar.activation(junk[:, 0:src.shape[-1]], src, ACT.Square, scale=scale,
                                     accum_out=total).then_inc(s_achain, 1)

            def squares_done(signal):
                act.wait_ge(s_achain, sq[0])
                act.sem_inc(signal, 1)

            def mean_squares(src, first):
                for b in range(NB):
                    square(src[:, b, :], D ** -0.5, ms[:, first + b:first + b + 1])
                squares_done(s_ms)

            def turned(t, name, first):
                for k in (0, 1, 4, 5):
                    act.wait_ge(s_xp, XB * t + k // 2 + 1)
                    copy(xT[:, k, :], bank[k // 2][:, (k % 2) * SEQ:(k % 2 + 1) * SEQ],
                         columns(name, first + k)).then_inc(s_xTa, 1)

            act.wait_ge(s_x, 16 * NB)
            mean_squares(h, 0)
            act.wait_ge(s_rt, 1)
            copy(cols[:, :], bank[7][:, 0:P]).then_inc(s_cols, 1)
            act.wait_ge(s_cols, 1)
            act.wait_ge(s_wsp, 1)
            copy(wsT[:, 0:4, :].rearrange("p g j -> p (g j)"), bank[5][:, :])
            copy(wsT[:, 4:8, :].rearrange("p g j -> p (g j)"), bank[6][:, :]).then_inc(s_wsc, 1)
            act.wait_ge(s_ang, 1)
            nc.scalar.activation(sin_t[:, :, :], turns[:, :, :], ACT.Sin)
            nc.scalar.activation(cos_t[:, :, :], ang[:, :, :], ACT.Sin).then_inc(s_sin, 1)

            for l in range(L):
                if l:
                    act.wait_ge(s_h, 2)
                    mean_squares(h, 0)
                turned(3 * l, "attn", KT * l)
                for j, (c, n) in enumerate(IN_CHUNKS):
                    act.wait_ge(s_pp, NIN * NB * l + NB * j + 1)
                    copy(proj[:, 0, c:c + n], bank[4 + (NB * j) % 4][:, 0:n]).then_inc(s_pea, 1)
                act.wait_ge(s_pea, NIN * (l + 1))
                act.wait_ge(s_pev, NIN * (l + 1))
                for b in range(NB):
                    square(proj[:, b, CQ:CQ + QR], QR ** -0.5, ms[:, 2 + b:3 + b])
                    square(proj[:, b, CKV:CKV + KVR], KVR ** -0.5, ms[:, 4 + b:5 + b])
                squares_done(s_cms)
                nc.scalar.activation(gel[:, :, :], proj[:, :, GU:GU + 2 * GW], ACT.Gelu_apprx_tanh).then_inc(s_gel, 1)
                act.wait_ge(s_nTp, l + 1)
                for j in range(2):
                    copy(nqT[0:DH, 2 * j:2 * j + 2, :].rearrange("p h t -> p (h t)"), bank[j][0:DH, :], DH ** -0.5)
                copy(nkT[0:DH, :, :].rearrange("p h t -> p (h t)"), bank[2][0:DH, :]).then_inc(s_nT, 1)
                act.wait_ge(s_cp, l + 1)
                for k in range(2):
                    copy(cT[:, k, :], bank[4][:, k * SEQ:(k + 1) * SEQ], columns("q", 2 * l + k))
                copy(cT[:, 2, :], bank[5][:, 0:SEQ], columns("kv", l)).then_inc(s_cT, 1)
                act.wait_ge(s_qp, l + 1)
                for b in range(NB):
                    copy(q5[:, b, 0:HEADS, :], bank[b][:, 0:HEADS * QK].rearrange("p (h d) -> p h d", h=HEADS))
                    kv = bank[(2, 7)[b]][:, :].rearrange("p (h d) -> p h d", h=HEADS)
                    copy(kk[:, b, :, 0:NOPE], kv[:, :, 0:NOPE])
                    copy(vv[:, b, :, :], kv[:, :, NOPE:])
                    i = copy(q5[:, b, HEADS, NOPE:QK], proj[:, b, KR:KR + ROPE])
                i.then_inc(s_qa, 1)
                act.wait_ge(s_hp, 2 * l + 2)
                nc.scalar.activation(hidT[:, :, :, 0:NC], bank[4][:, 0:64].rearrange(
                    "p (j t c) -> p j t c", j=2, t=2)[:, :, :, 0:NC], ACT.Gelu_apprx_tanh).then_inc(s_hg, 1)
                nc.scalar.activation(gexp[:, :, :], proj[:, :, NGL:END], ACT.Exp, scale=-1.0).then_inc(s_gex, 1)
                act.wait_ge(s_qTp, l + 1)
                for j in range(2):
                    copy(qT[0:QK, 2 * j:2 * j + 2, :].rearrange("p h t -> p (h t)"), bank[j][0:QK, :], QK ** -0.5)
                    i = copy(kT[0:QK, 2 * j:2 * j + 2, :].rearrange("p h t -> p (h t)"), bank[(2, 7)[j]][0:QK, :])
                i.then_inc(s_qT, 1)
                act.wait_ge(s_scm, l + 1)
                nc.scalar.activation(pc[:, :, :, 0:NC].rearrange("p b h c -> p (b h) c"), sc[:, :, 0:NC],
                                     ACT.Exp).then_inc(s_pc, 1)

                def turned_probs(n):
                    m = l * NU + n
                    act.wait_ge(s_tp, m + 1)
                    if n >= 2:
                        act.wait_ge(s_ov, m - 1)
                    copy(probT[:, n % 2, :], bank[2 + n % 2][:, :]).then_inc(s_tc, 1)

                for n, (kind, b, hs) in enumerate(UNITS):
                    m = l * NU + n
                    width = (b + 1) * P
                    act.wait_ge(s_mx, m + 1)
                    if n >= 2:
                        act.wait_ge(s_tp, m - 1)
                    for j, hd in enumerate(hs):
                        i = nc.scalar.activation(
                            prob[:, n % 2, j * width:(j + 1) * width], bank[n % 2][:, j * width:(j + 1) * width],
                            ACT.Exp, bias=nmax[:, n % 2, j:j + 1],
                            accum_out=psums[:, kind, b * HEADS + hd:b * HEADS + hd + 1])
                    i.then_inc(s_e, 1)
                    if n >= 1:
                        turned_probs(n - 1)
                turned_probs(NU - 1)
                act.wait_ge(s_y, 2 * l + 1)
                for b in range(NB):
                    for g in range(4):
                        square(y[:, b, g * GW:(g + 1) * GW], GW ** -0.5, ms[:, 8 + 4 * b + g:9 + 4 * b + g])
                squares_done(s_ms)
                turned(3 * l + 1, "group", KT * l)
                act.wait_ge(s_h, 2 * l + 1)
                mean_squares(h, 0)
                turned(3 * l + 2, "ffn", KT * l)
                if l == 0:
                    def ffn(step0, per, i):
                        for j in range(per):
                            act.wait_ge(s_g, step0 + per * i + j + 1)
                            need = max(j - 1, 0)
                            if need or step0:
                                act.wait_ge(s_hid, step0 + per * i + need)
                            nc.scalar.activation(sg[:, j % 2, :], bank[0][:, :], ACT.Silu).then_inc(s_sg, 1)
                            if j:
                                hidden_out(step0, per, i, j - 1)
                        hidden_out(step0, per, i, per - 1)

                    def hidden_out(step0, per, i, j):
                        act.wait_ge(s_hT, step0 + per * i + j + 1)
                        need = max(j - 1, 0)
                        if need or step0:
                            act.wait_ge(s_d, step0 + per * i + need)
                        copy(hidTs[:, j % 2, :], bank[2 + j % 2][:, :]).then_inc(s_hTs, 1)

                    ffn(0, NB * FS, 0)
            act.wait_ge(s_lm, 1)
            nc.scalar.activation(gd[:, 1, :], gd[:, 0, :], ACT.Exp).then_inc(s_le, 1)

            def rows_out(n):
                act.wait_ge(s_xep, n + 1)
                for k in range(KT):
                    i = copy(xeT[:, k, :], bank[6 + k // 4][:, (k % 4) * P:(k % 4 + 1) * P],
                             columns("ffn", KT * (L - 1) + k))
                i.then_inc(s_xe, 1)

            def gates_out(n):
                act.wait_ge(s_ggp, n + 1)
                copy(ggT[:, :, :].rearrange("p b t -> p (b t)"), bank[2][:, 0:NB * P]).then_inc(s_ggT, 1)

            rows_out(0)
            gates_out(0)
            with act.Fori(0, E) as e:
                ffn(DENSE, FS, e)
                rows_out(e + 1)
                gates_out(e + 1)
            act.wait_ge(s_over, 1)
            n_over = act.value_load(over_i[0:1, 0:1], min_val=0, max_val=MAX_OVER)
            with act.Fori(0, MAX_OVER) as i:
                with act.If(n_over > i):
                    rows_out(i + (E + 1))
                    gates_out(i + (E + 1))
                    ffn(DENSE + E * FS, FS, i)
            act.wait_ge(s_h, 2 * L)
            mean_squares(h, 0)

        @block.vector
        def _(dve):
            ch = [0]

            def link(ins):
                ch[0] += 1
                ins.then_inc(s_chain, 1)
                dve.wait_ge(s_chain, ch[0])

            def tt(o, a, b, op):
                return nc.vector.tensor_tensor(o, a, b, op)

            def ts(o, a, s1, s2, op0, op1=None):
                if op1 is None:
                    return nc.vector.tensor_scalar(o, a, s1, None, op0)
                return nc.vector.tensor_scalar(o, a, s1, s2, op0, op1)

            dve.wait_ge(s_const, 1)
            dve.wait_ge(s_small, SMALL)
            link(nc.vector.tensor_copy(pos_f[:, :], pos_i[:, :]))
            for b in range(NB):
                link(ts(ang[:, b, :], inv[:, :], pos_f[:, b:b + 1], None, ALU.mult))
            link(ts(turns[:, :, :], ang[:, :, :], 0.15915494309189535, ROUND_MAGIC, ALU.mult, ALU.add))
            link(ts(turns[:, :, :], turns[:, :, :], -ROUND_MAGIC, None, ALU.add))
            for part in (TWO_PI_HI, TWO_PI_LO):
                link(ts(sin_t[:, :, :], turns[:, :, :], part, None, ALU.mult))
                link(tt(ang[:, :, :], ang[:, :, :], sin_t[:, :, :], ALU.subtract))
            link(ts(turns[:, :, :], ang[:, :, :], PI_SAFE, -PI_SAFE, ALU.min, ALU.max))
            link(ts(ang[:, :, :], ang[:, :, :], 1.5707963267948966, None, ALU.add))
            link(ts(cos_t[:, :, :], ang[:, :, :], PI_SAFE, -6.283185307179586, ALU.is_gt, ALU.mult))
            link(tt(ang[:, :, :], ang[:, :, :], cos_t[:, :, :], ALU.add))
            ts(ang[:, :, :], ang[:, :, :], PI_SAFE, -PI_SAFE, ALU.min, ALU.max).then_inc(s_ang, 1)
            link(ts(w8[:, :], iota_s[:, 0:E], -1.0, float(E), ALU.mult, ALU.add))

            def scale_rows(src, t):
                dve.wait_ge(s_rs, t + 1)
                if t:
                    dve.wait_ge(s_xp, XB * t)
                for b in range(NB):
                    i = ts(xs[:, b, :], src[:, b, :], rs[:, b:b + 1], None, ALU.mult)
                i.then_inc(s_xs, 1)

            def turned(t, name, first):
                if t == 0:
                    dve.wait_ge(s_cols, 1)
                for k in (2, 3, 6, 7):
                    dve.wait_ge(s_xp, XB * t + k // 2 + 1)
                    ts(xT[:, k, :], bank[k // 2][:, (k % 2) * SEQ:(k % 2 + 1) * SEQ], columns(name, first + k), None,
                       ALU.mult).then_inc(s_xTv, 1)

            for l in range(L):
                scale_rows(h, 3 * l)
                turned(3 * l, "attn", KT * l)
                for j, (c, n) in enumerate(IN_CHUNKS):
                    dve.wait_ge(s_pp, NIN * NB * l + NB * j + 2)
                    nc.vector.tensor_copy(proj[:, 1, c:c + n], bank[4 + (NB * j + 1) % 4][:, 0:n]).then_inc(s_pev, 1)
                dve.wait_ge(s_pea, NIN * (l + 1))
                dve.wait_ge(s_pev, NIN * (l + 1))
                link(tt(conv_u[:, :, :], proj[:, :, CC:CC + GW], proj[:, :, CHV:CHV + GW], ALU.mult))
                for k in range(3):
                    w = cw_row[:, l:l + 1, k * GW:(k + 1) * GW].to_broadcast([P, NB, GW])
                    i = tt(conv_k[:, k, :, :], conv_u[:, :, :], w, ALU.mult)
                i.then_inc(s_cu, 1)
                dve.wait_ge(s_crs, l + 1)
                for b in range(NB):
                    ts(cn[:, b, 0:QR], proj[:, b, CQ:CQ + QR], rs[:, 2 + b:3 + b], None, ALU.mult)
                    i = ts(cn[:, b, QR:], proj[:, b, CKV:CKV + KVR], rs[:, 4 + b:5 + b], None, ALU.mult)
                i.then_inc(s_cn, 1)
                dve.wait_ge(s_zp, l + 1)
                for j, name in enumerate(("pe_k", "pe_v")):
                    z = bank[3][:, j * P:(j + 1) * P].rearrange("p (c r) -> p c r", r=8)
                    for a in range(2):
                        c = row_at[name] + 16 * l + 8 * a
                        pe_ = cols[:, None, c:c + 8].to_broadcast([P, NC, 8])
                        i = tt(blk[:, j, a, :, :], z[:, a:a + NC, :], pe_, ALU.add)
                i.then_inc(s_blk, 1)
                dve.wait_ge(s_gel, l + 1)
                for b in range(NB):
                    link(nc.vector.bn_stats(bn[:, b, :], gel[:, b, GW:]))
                    i = nc.vector.bn_aggr(mv[:, b, :], bn[:, b, :])
                i.then_inc(s_mv, 1)
                dve.wait_ge(s_grs, l + 1)
                for b in range(NB):
                    link(ts(gel[:, b, GW:], gel[:, b, GW:], mv[:, b, 0:1], rs[:, 6 + b:7 + b],
                            ALU.subtract, ALU.mult))
                tt(gel[:, :, GW:], gel[:, :, GW:], ln_row[:, l:l + 1, :].to_broadcast([P, NB, GW]),
                   ALU.mult).then_inc(s_gv, 1)
                dve.wait_ge(s_cv, l + 1)
                link(tt(y[:, :, GW:2 * GW], bank[6][:, :].rearrange("p (b n) -> p b n", b=NB),
                        proj[:, :, CB:CB + GW], ALU.mult))
                dve.wait_ge(s_qa, l + 1)
                if l == 0:
                    dve.wait_ge(s_sin, 1)
                x1, x2 = q5[:, :, :, NOPE:NOPE + HALF], q5[:, :, :, NOPE + HALF:]
                five = [P, NB, HEADS + 1, HALF]
                cos_b = cos_t[:, :, None, :].to_broadcast(five)
                sin_b = sin_t[:, :, None, :].to_broadcast(five)
                tt(rt[:, 0], x1, cos_b, ALU.mult)
                tt(rt[:, 1], x2, sin_b, ALU.mult)
                tt(rt[:, 2], x1, sin_b, ALU.mult)
                link(tt(rt[:, 3], x2, cos_b, ALU.mult))
                tt(x1, rt[:, 0], rt[:, 1], ALU.subtract)
                link(tt(x2, rt[:, 2], rt[:, 3], ALU.add))
                for b in range(NB):
                    i = nc.vector.tensor_copy(kk[:, b, :, NOPE:],
                                              q5[:, b, HEADS:HEADS + 1, NOPE:].to_broadcast([P, HEADS, ROPE]))
                i.then_inc(s_rope, 1)
                dve.wait_ge(s_hg, l + 1)
                for t in range(CH // P):
                    i = nc.vector.tensor_copy(hidR[:, t, :, 0:NC],
                                              hidT[:, 1, t:t + 1, 0:NC].to_broadcast([P, HEADS, NC]))
                i.then_inc(s_hr, 1)
                dve.wait_ge(s_sv, l + 1)
                for g in range(4):
                    link(nc.vector.scalar_tensor_tensor(
                        out=y[:, :, 2 * GW + g * DH:2 * GW + (g + 1) * DH],
                        in0=bank[5][:, :].rearrange("p (b n) -> p b n", b=NB)[:, :, g * DH:(g + 1) * DH],
                        scalar=columns("bs", 4 * l + g), in1=gel[:, :, g * DH:(g + 1) * DH],
                        op0=ALU.add, op1=ALU.mult))
                dve.wait_ge(s_kcp, l + 1)
                nc.vector.tensor_copy(kcT[0:DH, 0:NC], bank[3][0:DH, 0:NC])
                for hd in range(HEADS):
                    i = nc.vector.tensor_copy(vcd[32 * hd:32 * hd + 32, hd * DH:(hd + 1) * DH],
                                              bank[3][32 * hd:32 * hd + 32, 64:64 + DH])
                i.then_inc(s_kc, 1)
                dve.wait_ge(s_gex, l + 1)
                link(ts(gexp[:, :, :], gexp[:, :, :], 1.0, None, ALU.add))
                link(nc.vector.reciprocal(gsig[:, :, :], gexp[:, :, :]))
                dve.wait_ge(s_scp, l + 1)
                for b in range(NB):
                    link(tt(sc[:, b * HEADS:(b + 1) * HEADS, :][:, :, 0:NC],
                            bank[4][:, b * 64:(b + 1) * 64].rearrange("p (h c) -> p h c", c=16)[:, :, 0:NC],
                            cmask[:, b:b + 1, 0:NC].to_broadcast([P, HEADS, NC]), ALU.add))
                link(nc.vector.tensor_reduce(scm[:, :], sc[:, :, 0:NC], AX_X, ALU.max))
                tt(sc[:, :, 0:NC], sc[:, :, 0:NC], scm[:, :, None].to_broadcast([P, NB * HEADS, NC]),
                   ALU.subtract).then_inc(s_scm, 1)

                def row_max(n):
                    kind, b, hs = UNITS[n]
                    m = l * NU + n
                    dve.wait_ge(s_sp, m + 1)
                    if n >= 2:
                        dve.wait_ge(s_e, m - 1)
                    nc.vector.tensor_reduce(
                        nmax[:, n % 2, 0:len(hs)],
                        bank[n % 2][:, :].rearrange("p (h k) -> p h k", h=len(hs)), AX_X, ALU.max,
                        negate=True).then_inc(s_mx, 1)

                row_max(0)
                dve.wait_ge(s_pc, l + 1)
                link(nc.vector.tensor_reduce(pcs[:, :], pc[:, :, :, 0:NC].rearrange("p b h c -> p (b h) c"),
                                             AX_X, ALU.add))
                dve.wait_ge(s_pcp, l + 1)
                nc.vector.tensor_copy(pcT[:, :, :].rearrange("p b t -> p (b t)"),
                                      bank[3][:, 128:128 + NB * P]).then_inc(s_pcT, 1)
                row_max(1)
                link(nc.vector.reciprocal(pcs[:, :], pcs[:, :]))
                link(tt(pcs[:, :].rearrange("p (b h) -> p b h", b=NB), pcs[:, :].rearrange("p (b h) -> p b h", b=NB),
                        cvalid[:, :, None].to_broadcast([P, NB, HEADS]), ALU.mult))
                for n in range(2, NU):
                    row_max(n)
                dve.wait_ge(s_ov, l * NU + NU)
                link(nc.vector.reciprocal(prec[:, :, :], psums[:, :, :]))
                full = [P, NB * HEADS, DH]

                def spread(ap):
                    return ap[:, :, None].to_broadcast(full)

                def heads(ap):
                    return ap.rearrange("p (h d) -> p h d", d=DH)

                for b in range(NB):
                    link(tt(y[:, b, 0:GW].rearrange("p (h d) -> p h d", d=DH),
                            heads(bank[7][:, :])[:, b * HEADS:(b + 1) * HEADS, :],
                            prec[:, 0, b * HEADS:(b + 1) * HEADS, None].to_broadcast([P, HEADS, DH]), ALU.mult))
                gate3 = gsig[:, :, :].rearrange("p b (h k) -> p (b h) k", k=3)
                tt(coef[:, 0, :], pcs[:, :], gate3[:, :, 0], ALU.mult)
                tt(coef[:, 1, :], prec[:, 1, :], gate3[:, :, 1], ALU.mult)
                link(tt(coef[:, 2, :], prec[:, 2, :], gate3[:, :, 2], ALU.mult))
                dve.wait_ge(s_oc, l + 1)
                t0 = nsa_t[:, 0].rearrange("p b (h d) -> p (b h) d", d=DH)
                t1 = nsa_t[:, 1].rearrange("p b (h d) -> p (b h) d", d=DH)
                tt(t0, heads(bank[6][:, :]), spread(coef[:, 0, :]), ALU.mult)
                link(tt(t1, heads(bank[4][:, :]), spread(coef[:, 1, :]), ALU.mult))
                link(tt(t0, t0, t1, ALU.add))
                link(tt(t1, heads(bank[5][:, :]), spread(coef[:, 2, :]), ALU.mult))
                tt(y[:, :, 3 * GW:], nsa_t[:, 0], nsa_t[:, 1], ALU.add).then_inc(s_y, 1)
                dve.wait_ge(s_y, 2 * l + 1)
                dve.wait_ge(s_rs, 3 * l + 2)
                dve.wait_ge(s_xp, XB * (3 * l + 1))
                for b in range(NB):
                    for g in range(4):
                        i = ts(xs[:, b, g * GW:(g + 1) * GW], y[:, b, g * GW:(g + 1) * GW],
                               rs[:, 8 + 4 * b + g:9 + 4 * b + g], None, ALU.mult)
                i.then_inc(s_xs, 1)
                turned(3 * l + 1, "group", KT * l)
                for j in range(2):
                    dve.wait_ge(s_wo, 4 * l + 2 * (j + 1))
                    for b in range(NB):
                        i = tt(h[:, b, j * W:(j + 1) * W], h[:, b, j * W:(j + 1) * W], bank[4 + 2 * j + b][:, :],
                               ALU.add)
                i.then_inc(s_h, 1)
                dve.wait_ge(s_h, 2 * l + 1)
                scale_rows(h, 3 * l + 2)
                turned(3 * l + 2, "ffn", KT * l)
                dve.sem_inc(s_y, 1)
                if l == 0:
                    def products(step0, per, i):
                        for j in range(per):
                            dve.wait_ge(s_sg, step0 + per * i + j + 1)
                            dve.wait_ge(s_u, step0 + per * i + j + 1)
                            need = max(j - 1, 0)
                            if need or step0:
                                dve.wait_ge(s_hT, step0 + per * i + need)
                            tt(hid[:, j % 2, :], bank[1][:, :], sg[:, j % 2, :], ALU.mult).then_inc(s_hid, 1)

                    products(0, NB * FS, 0)
                    dve.wait_ge(s_d, DENSE)
                    for b in range(NB):
                        for half in range(2):
                            i = tt(h[:, b, half * W:(half + 1) * W], h[:, b, half * W:(half + 1) * W],
                                   bank[4 + 2 * b + half][:, :], ALU.add)
                    i.then_inc(s_h, 1)
                    dve.wait_ge(s_h, 2)

            dve.wait_ge(s_lp, 1)
            wide = [P, NB, E]
            link(nc.vector.tensor_copy(lg[:, :, :].rearrange("p b e -> p (b e)"), bank[0][:, 0:NB * E]))
            for k in range(2):
                src = lg if k == 0 else lg2
                link(nc.vector.tensor_reduce(top[:, k, :], src[:, :, :], AX_X, ALU.max))
                link(tt(rt_a[:, :, :], src[:, :, :], top[:, k, :, None].to_broadcast(wide), ALU.is_equal))
                link(tt(rt_a[:, :, :], rt_a[:, :, :], w8[:, None, :].to_broadcast(wide), ALU.mult))
                link(nc.vector.tensor_reduce(fst[:, :], rt_a[:, :, :], AX_X, ALU.max))
                link(tt(oh[:, k], rt_a[:, :, :], fst[:, :, None].to_broadcast(wide), ALU.is_equal))
                if k == 0:
                    link(ts(lg2[:, :, :], oh[:, 0], -HUGE, None, ALU.mult))
                    link(tt(lg2[:, :, :], lg2[:, :, :], lg[:, :, :], ALU.add))
            tt(gd[:, 0, :], top[:, 1, :], top[:, 0, :], ALU.subtract).then_inc(s_lm, 1)
            tt(rsg[:, 1], oh[:, 0], oh[:, 1], ALU.add).then_inc(s_sel, 1)
            dve.wait_ge(s_le, 1)
            link(ts(gd[:, 2, :], gd[:, 1, :], 1.0, None, ALU.add))
            link(nc.vector.reciprocal(gw[:, 0, :], gd[:, 2, :]))
            link(tt(gw[:, 1, :], gd[:, 1, :], gw[:, 0, :], ALU.mult))
            for k in range(2):
                link(tt(oh[:, k], oh[:, k], gw[:, k, :, None].to_broadcast(wide), ALU.mult))
            link(tt(rsg[:, 2], oh[:, 0], oh[:, 1], ALU.add))
            dve.wait_ge(s_rk, 1)
            nc.vector.tensor_copy(total[:, :], bank[1][:, NB * E:(NB + 1) * E])
            link(nc.vector.tensor_copy(rsg[:, 0].rearrange("p b e -> p (b e)"), bank[1][:, 0:NB * E]))

            def slots(n, key):
                ts(eqm[:, :], key, cnt[:, 0:1], None, ALU.is_equal).then_inc(s_col, 1)
                dve.wait_ge(s_col, COLS * n + 1)
                tt(pick[:, :, :], rsg[:, :, :, :].rearrange("p k b e -> p (k b) e"),
                   eqm[:, None, :].to_broadcast([P, 3 * NB, E]), ALU.mult).then_inc(s_col, 1)
                ts(cnt[:, 0:1], cnt[:, 0:1], 1.0, None, ALU.add).then_inc(s_col, 1)
                dve.wait_ge(s_col, COLS * n + 3)
                nc.vector.tensor_reduce(col[:, :], pick[:, :, :], AX_X, ALU.add).then_inc(s_col, 1)
                dve.wait_ge(s_col, COLS * n + 4)
                for b in range(NB):
                    ts(gm[:, b, :], iota_s[:, :], col[:, b:b + 1], col[:, NB + b:NB + b + 1],
                       ALU.is_equal, ALU.mult)
                    i = ts(gg[:, b, :], iota_s[:, :], col[:, b:b + 1], col[:, 2 * NB + b:2 * NB + b + 1],
                           ALU.is_equal, ALU.mult)
                i.then_inc(s_gm, 1)

            COLS = 4

            def expert_out(m):
                dve.wait_ge(s_d, (m + 1) * FS + DENSE)
                nc.vector.tensor_copy(ye[:, 0:W], bank[4][:, :])
                nc.vector.tensor_copy(ye[:, W:], bank[5][:, :]).then_inc(s_ye, 1)
                dve.wait_ge(s_ysp, m + 1)
                for b in range(NB):
                    for half in range(2):
                        i = tt(h[:, b, half * W:(half + 1) * W], h[:, b, half * W:(half + 1) * W],
                               bank[6 - 2 * b + half][:, :], ALU.add)
                i.then_inc(s_yadd, 1)
                dve.wait_ge(s_yadd, m + 1)
                dve.sem_inc(s_ysa, 1)

            experts = iota_s[:, 0:E]
            dve.sem_inc(s_ysa, 1)
            slots(0, experts)
            link(ts(okey[:, 0, :], total[:, :], float(SLOTS), None, ALU.is_gt))
            link(nc.vector.tensor_tensor_scan(okey[:, 1, :], ones[:, 0:E], okey[:, 0, :], 0.0,
                                              ALU.mult, ALU.add))
            link(nc.vector.tensor_reduce(over_f[:, 0:1], okey[:, 1, :], AX_X, ALU.max))
            link(tt(okey[:, 0, :], okey[:, 0, :], okey[:, 1, :], ALU.mult))
            link(tt(over_e[:, :, :], okey[:, 0:1, :].to_broadcast([P, MAX_OVER, E]),
                    iota_s[:, 1:MAX_OVER + 1, None].to_broadcast([P, MAX_OVER, E]), ALU.is_equal))
            link(tt(over_e[:, :, :], over_e[:, :, :], iota_s[:, None, 0:E].to_broadcast([P, MAX_OVER, E]), ALU.mult))
            link(nc.vector.tensor_reduce(over_f[:, 1:], over_e[:, :, :], AX_X, ALU.add))
            nc.vector.tensor_copy(over_i[:, :], over_f[:, :]).then_inc(s_over, 1)
            with dve.Fori(0, E) as e:
                dve.wait_ge(s_xep, e + 1)
                dve.wait_ge(s_ggp, e + 1)
                slots(e + 1, experts)
                products(DENSE, FS, e)
                expert_out(e)
            dve.wait_ge(s_col, COLS * (E + 1))
            link(ts(rsg[:, 0], rsg[:, 0], -float(SLOTS), None, ALU.add))
            link(nc.vector.memset(cnt[:, :], 1.0))
            dve.wait_ge(s_over, 1)
            n_over = dve.value_load(over_i[0:1, 0:1], min_val=0, max_val=MAX_OVER)
            with dve.Fori(0, MAX_OVER) as i:
                with dve.If(n_over > i):
                    n = i + (E + 1)
                    dve.wait_ge(s_xep, n)
                    dve.wait_ge(s_ggp, n)
                    slots(n, okey[:, 0, :])
                    products(DENSE + E * FS, FS, i)
                    expert_out(i + E)
            dve.sem_inc(s_h, 1)
            dve.wait_ge(s_rs, 3 * L + 1)
            for b in range(NB):
                link(ts(xs[:, b, :], h[:, b, :], rs[:, b:b + 1], None, ALU.mult))
                i = tt(xs[:, b, :], xs[:, b, :], fin_row[:, :], ALU.mult)
            i.then_inc(s_y, 1)


_INS = ['x', 'positions', 'rope_inv', 'attn_norm', 'w_in', 'mla_q_norm', 'mla_w_uq', 'mla_kv_norm', 'mla_w_ukv',
        'conv_w', 'gmlp_ln', 'gmlp_w_s', 'gmlp_b_s', 'nsa_pe_k', 'nsa_w1_k', 'nsa_w2_k', 'nsa_pe_v', 'nsa_w1_v',
        'nsa_w2_v', 'group_norm', 'w_o', 'ffn_norm', 'dense_w_gate', 'dense_w_up', 'dense_w_down',
        'moe_router', 'moe_w_gate', 'moe_w_up', 'moe_w_down', 'final_norm']


def kernel(**inputs):
    import numpy as _np
    import concourse.bacc as _bacc
    from concourse import mybir as _mybir
    from concourse.bass_utils import run_bass_kernel_spmd as _run

    rope_inv = (_np.float32(10000.0) ** (-_np.arange(HALF, dtype=_np.float32) / _np.float32(HALF))).reshape(1, HALF)
    nc = _bacc.Bacc("TRN2", target_bir_lowering=False, num_devices=1)
    arrays, args = {}, []
    for name in _INS:
        a = _np.ascontiguousarray(rope_inv if name == 'rope_inv' else inputs[name])
        arrays[f"in_{name}_dram"] = a
        args.append(nc.dram_tensor(f"in_{name}_dram", a.shape, _mybir.dt.from_np(a.dtype), kind="ExternalInput").ap())
    shape = tuple(inputs['x'].shape)
    args.append(nc.dram_tensor("out_0_dram", shape, F32, kind="ExternalOutput").ap())
    hybrid_trunk(nc, *args)
    r = _run(nc, [arrays], core_ids=[0])
    return r.results[0]["out_0_dram"]
```

```python
from contextlib import ExitStack

import concourse.bass as bass
from concourse import mybir

ALU = mybir.AluOpType
ACT = mybir.ActivationFunctionType
F32 = mybir.dt.float32
F32R = mybir.dt.float32r
I32 = mybir.dt.int32
AX_X = mybir.AxisListType.X

P = 128
EPS = 1e-6
NEG = -1e30
HUGE = 3.0e38
NOPE, ROPE, HEADS = 64, 32, 4
QK = NOPE + ROPE
HALF = ROPE // 2
DH = 64
CMP_STRIDE, CMP_LEN = 16, 32
TWO_PI_HI = 6.28125
TWO_PI_LO = 0.0019353071795864769
ROUND_MAGIC = 12582912.0
PI_SAFE = 3.1415925
W = 512
RING = 3
PARTS = 3


def hybrid_trunk(nc, x, positions, rope_inv, attn_norm, w_in, mla_q_norm, mla_w_uq, mla_kv_norm, mla_w_ukv,
                 conv_w, gmlp_ln, gmlp_w_s, gmlp_b_s, nsa_pe_k, nsa_w1_k, nsa_w2_k, nsa_pe_v, nsa_w1_v, nsa_w2_v,
                 group_norm, w_o, ffn_norm, dense_w_gate, dense_w_up, dense_w_down,
                 moe_router, moe_w_gate, moe_w_up, moe_w_down, final_norm, out):
    _, SEQ, D = x.shape
    L = attn_norm.shape[0]
    NB = SEQ // P
    KT = D // P
    D_IN = w_in.shape[2]
    FF = dense_w_gate.shape[2]
    FS = FF // W
    E = moe_w_gate.shape[1]
    GW = D // 4
    QR, KVR = mla_q_norm.shape[1], mla_kv_norm.shape[1]
    NC = SEQ // CMP_STRIDE - CMP_LEN // CMP_STRIDE + 1
    CH = nsa_w1_k.shape[2]
    assert NB == 2 and L == 2 and KT == 8 and FF % W == 0 and E == 8

    sizes = [QR, KVR, ROPE, GW, GW, GW, GW, GW, HEADS * DH] + [DH] * 6 + [HEADS * 3]
    at = [sum(sizes[:i]) for i in range(len(sizes) + 1)]
    (CQ, CKV, KR, CB, CC, CHV, GU, GV, NQ, NKC, NVC, NKS, NVS, NKW, NVW, NGL, END) = at
    assert END == D_IN
    IN_CHUNKS = [(c, min(W, D_IN - c)) for c in range(0, D_IN, W)]
    NIN = len(IN_CHUNKS)

    MIX = NIN + 4
    assert MIX % RING == 0
    ORDER = [(0, 0, 0), (0, 0, 1), (1, 0, 0), (1, 0, 1)]
    for n in range(1, FS):
        ORDER += [(0, n, 0), (0, n, 1), (1, n, 0), (1, n, 1), (2, n - 1, 0), (2, n - 1, 1)]
    ORDER += [(2, FS - 1, 0), (2, FS - 1, 1)]
    PIECES = len(ORDER)
    AT = {piece: j for j, piece in enumerate(ORDER)}
    assert PIECES % (2 * RING) == 0 and PIECES % PARTS == 0
    chunk_mix = [0, MIX]
    SLOTS = P
    MAX_OVER = 2 * SEQ // (SLOTS + 1)

    row_at, rows = {}, 0
    for name, n in (("attn", L * KT), ("ffn", L * KT), ("q", L * QR // P), ("kv", L * KVR // P),
                    ("group", L * KT), ("bs", L * 4), ("pe_k", L * 16), ("pe_v", L * 16)):
        row_at[name] = rows
        rows += n
    assert rows <= P

    with ExitStack() as ctx:
        def sb(name, shape, dt=F32):
            return ctx.enter_context(nc.sbuf_tensor(name, shape, dt))

        def sem(name):
            return ctx.enter_context(nc.semaphore(name))

        bank = [ctx.enter_context(nc.psum_tensor(f"bank{i}", [P, W], F32)) for i in range(8)]

        ring = sb("ring", [P, RING, KT * W])
        h = sb("h", [P, NB, D])
        xs = sb("xs", [P, NB, D])
        xT = sb("xT", [P, KT, SEQ])
        y = sb("y", [P, NB, D])
        vrows = sb("vrows", [P, P])
        cols = sb("cols", [P, P])
        ident = sb("ident", [P, P])
        amask = sb("amask", [P, P])
        tri = sb("tri", [P, P])
        ones = sb("ones", [P, P])
        shift = sb("shift", [P, 2, P])
        carry = sb("carry", [P, 2, P])
        iota_i = sb("iota_i", [P, P], I32)
        iota_s = sb("iota_s", [P, P])
        cmask = sb("cmask", [P, NB, 16])
        cvalid = sb("cvalid", [P, NB])
        neghalf = sb("neghalf", [P, 16])
        pos_i = sb("pos_i", [P, NB], I32)
        pos_f = sb("pos_f", [P, NB])
        inv = sb("inv", [P, HALF])
        ang = sb("ang", [P, NB, HALF])
        turns = sb("turns", [P, NB, HALF])
        sin_t = sb("sin_t", [P, NB, HALF])
        cos_t = sb("cos_t", [P, NB, HALF])
        ln_row = sb("ln_row", [P, L, GW])
        cw_row = sb("cw_row", [P, L, 3 * GW])
        fin_row = sb("fin_row", [P, D])
        w_uq = sb("w_uq", [P, L, QR // P, HEADS * QK])
        w_ukv = sb("w_ukv", [P, L, HEADS * 2 * DH])
        w2 = sb("w2", [P, L, 2, CH // P, DH])
        ws_raw = y[:, 0, :].rearrange("p (g j) -> p g j", g=L * 4)
        wsT = sb("wsT", [P, L * 4, P])
        w_r = sb("w_r", [P, KT, E])
        bn = sb("bn", [P, NB, 6])
        mv = sb("mv", [P, NB, 2])
        hidT = sb("hidT", [P, CH // P, 16])
        hidR = sb("hidR", [P, CH // P, HEADS, 32])
        kcT = sb("kcT", [P, 16])
        vcd = sb("vcd", [P, HEADS * DH])
        sc = sb("sc", [P, NB * HEADS, 16])
        scm = sb("scm", [P, NB * HEADS])
        pc = sb("pc", [P, NB, HEADS, 32])
        pcs = sb("pcs", [P, NB * HEADS])
        nmax = sb("nmax", [P, 2, HEADS])
        psums = sb("psums", [P, 3, NB * HEADS])
        prec = sb("prec", [P, 3, NB * HEADS])
        gexp = sb("gexp", [P, NB, HEADS * 3])
        gsig = sb("gsig", [P, NB, HEADS * 3])
        coef = sb("coef", [P, 3, NB * HEADS])
        ms = sb("ms", [P, 16])
        rs = sb("rs", [P, 16])
        lg = sb("lg", [P, NB, E])
        lg2 = sb("lg2", [P, NB, E])
        w8 = sb("w8", [P, E])
        rt_a = sb("rt_a", [P, NB, E])
        oh = sb("oh", [P, 2, NB, E])
        top = sb("top", [P, 2, NB])
        fst = sb("fst", [P, NB])
        gw = sb("gw", [P, 2, NB])
        gd = sb("gd", [P, 3, NB])
        rsg = sb("rsg", [P, 3, NB, E])
        cnt = sb("cnt", [P, 2])
        total = sb("total", [P, E])
        okey = sb("okey", [P, 2, E])
        over_e = sb("over_e", [P, MAX_OVER, E])
        over_f = sb("over_f", [P, 1 + MAX_OVER])
        over_i = sb("over_i", [P, 1 + MAX_OVER], I32)
        eqm = sb("eqm", [P, E])
        pick = sb("pick", [P, 3 * NB, E])
        col = sb("col", [P, 3 * NB])
        gm = sb("gm", [P, NB, P])
        gg = sb("gg", [P, NB, P])
        ggT = sb("ggT", [P, NB, P])

        temporary = ExitStack()

        def tsb(name, shape):
            return temporary.enter_context(nc.sbuf_tensor(name, shape, F32))

        proj = tsb("proj", [P, NB, D_IN])
        junk = tsb("junk", [P, D])
        gel = tsb("gel", [P, NB, 2 * GW])
        conv_u = tsb("conv_u", [P, NB, GW])
        conv_k = tsb("conv_k", [P, 3, NB, GW])
        cn = tsb("cn", [P, NB, QR + KVR])
        cT = tsb("cT", [P, 3, SEQ])
        q5 = tsb("q5", [P, NB, HEADS + 1, QK])
        kk = tsb("kk", [P, NB, HEADS, QK])
        vv = tsb("vv", [P, NB, HEADS, DH])
        rt = tsb("rt", [P, 4, NB, HEADS + 1, HALF])
        qT = tsb("qT", [P, HEADS, SEQ])
        kT = tsb("kT", [P, HEADS, SEQ])
        nqT = tsb("nqT", [P, HEADS, SEQ])
        nkT = tsb("nkT", [P, 2, SEQ])
        blk = tsb("blk", [P, 2, 2, NC, 8])
        pcT = tsb("pcT", [P, NB, P])
        prob = tsb("prob", [P, 2, W])
        probT = tsb("probT", [P, 2, W])
        nsa_t = tsb("nsa_t", [P, 2, NB, GW])
        temporary.close()
        part_h = sb("part_h", [P, PARTS, KT * W // 2], F32R)
        part_l = sb("part_l", [P, PARTS, KT * W // 2], F32R)
        xh = sb("xh", [P, KT, SEQ], F32R)
        xl = sb("xl", [P, KT, SEQ], F32R)
        hTh = sb("hTh", [P, NB, W], F32R)
        hTl = sb("hTl", [P, NB, W], F32R)
        sg = sb("sg", [P, NB, W])
        hid = y[:, 1, :].rearrange("p (s n) -> p s n", s=2)
        ye = y[:, 0, :]

        loaded = [sem(f"ring_loaded{i}") for i in range(RING)]
        landed = [sem(f"piece_landed{i}") for i in range(2 * RING)]
        s_hi = sem("high_part_ready")
        s_lo = sem("low_part_ready")
        s_used = sem("piece_used")
        s_xh = sem("ffn_rows_high")
        s_xl = sem("ffn_rows_low")
        s_rows = sem("vectors_loaded")
        s_small = sem("small_loaded")
        s_x = sem("x_loaded")
        s_vz = sem("vectors_zeroed")
        s_zero = sem("zeroed")
        s_const = sem("constants_built")
        s_rt = sem("rows_turned")
        s_cols = sem("columns_ready")
        s_wsp = sem("ws_turned")
        s_wsc = sem("ws_copied")
        s_ws = sem("ws_masked")
        s_ang = sem("angles_ready")
        s_sin = sem("sines_ready")
        s_chain = sem("vector_chain")
        s_achain = sem("scalar_chain")
        s_pchain = sem("pool_chain")
        s_ms = sem("mean_square_ready")
        s_rs = sem("rms_scale_ready")
        s_xs = sem("rows_scaled")
        s_xp = sem("rows_turned_in_psum")
        s_xTa = sem("turned_by_scalar")
        s_xTv = sem("turned_by_vector")
        s_pp = sem("projection_in_psum")
        s_pea = sem("projection_out_by_scalar")
        s_pev = sem("projection_out_by_vector")
        s_h = sem("residual_ready")
        s_gel = sem("gelu_ready")
        s_gex = sem("gate_exp_ready")
        s_cms = sem("latent_mean_square")
        s_crs = sem("latent_scale")
        s_cn = sem("latent_scaled")
        s_cp = sem("latent_turned")
        s_cT = sem("latent_ready")
        s_qp = sem("q_and_kv_in_psum")
        s_qa = sem("q_and_kv_out")
        s_rope = sem("rope_done")
        s_qTp = sem("mla_qk_turned")
        s_qT = sem("mla_qk_ready")
        s_nTp = sem("nsa_qk_turned")
        s_nT = sem("nsa_qk_ready")
        s_zp = sem("compress_turned")
        s_blk = sem("blocks_ready")
        s_hp = sem("compress_hidden_in_psum")
        s_hg = sem("compress_hidden_ready")
        s_hc = sem("compress_hidden_turned")
        s_hr = sem("compress_hidden_repeated")
        s_kcp = sem("compressed_kv_in_psum")
        s_kc = sem("compressed_kv_ready")
        s_scp = sem("compressed_scores_in_psum")
        s_scm = sem("compressed_scores_masked")
        s_pc = sem("compressed_probs")
        s_pcp = sem("compressed_probs_turned")
        s_pcT = sem("compressed_probs_ready")
        s_oc = sem("compressed_out")
        s_cu = sem("conv_taps_ready")
        s_cv = sem("conv_in_psum")
        s_yc = sem("conv_out")
        s_mv = sem("gmlp_variance")
        s_grs = sem("gmlp_scale")
        s_gv = sem("gmlp_v_ready")
        s_sv = sem("gmlp_mixed")
        s_sp = sem("scores_in_psum")
        s_mx = sem("row_max_ready")
        s_e = sem("probs_ready")
        s_tp = sem("probs_turned")
        s_tc = sem("probs_turned_out")
        s_ov = sem("attention_unit_done")
        s_y = sem("groups_done")
        s_yms = sem("group_mean_square")
        s_wo = sem("output_in_psum")
        s_sg = sem("silu_ready")
        s_hid = sem("hidden_ready")
        s_hT = sem("hidden_turned")
        s_hTh = sem("hidden_turned_high")
        s_hTl = sem("hidden_turned_low")
        s_lp = sem("logits_in_psum")
        s_lm = sem("logit_gap_ready")
        s_le = sem("logit_gap_exp")
        s_sel = sem("selection_ready")
        s_over = sem("crowded_experts_known")
        s_rk = sem("ranks_in_psum")
        s_gm = sem("slot_matrices_ready")
        s_col = sem("expert_columns")
        s_xep = sem("expert_rows_in_psum")
        s_xe = sem("expert_rows_ready")
        s_ggp = sem("gate_matrix_turned")
        s_ggT = sem("gate_matrix_ready")
        s_ye = sem("expert_out_ready")
        s_ysp = sem("expert_scattered")
        s_yadd = sem("expert_add_done")
        s_ysa = sem("expert_added")
        s_out = sem("output_stored")

        def columns(name, i):
            c = row_at[name] + i
            return cols[:, c:c + 1]

        def ring_ready(eng, q):
            eng.wait_ge(loaded[q % RING], 16 * (q // RING + 1))

        def piece_ready(eng, f, j):
            eng.wait_ge(landed[j % (2 * RING)], f * (16 * PIECES // (2 * RING)) + 16 * (j // (2 * RING) + 1))

        def past(eng, signal, value):
            if not (isinstance(value, int) and value <= 0):
                eng.wait_ge(signal, value)

        wtile = [ring[:, s, :] for s in range(RING)]
        piece_in = [ring[:, j // 2, (j % 2) * (KT * W // 2):(j % 2 + 1) * (KT * W // 2)] for j in range(2 * RING)]

        def split_schedule(split, silu, product, turned_out, others):
            for j in range(PIECES + 1):
                if j - PARTS >= 0:
                    part, n, hh = ORDER[j - PARTS]
                    if (part, hh) == (0, 0) and n:
                        turned_out(n - 1)
                    if silu and (part, hh) == (0, 1):
                        silu(n)
                    if product and (part, hh) == (1, 1):
                        product(n)
                if j in others:
                    others[j]()
                if j < PIECES:
                    split(j)
            turned_out(FS - 1)

        YE_AT = 2
        SCATTER_AFTER = 1
        ADD_AT = 4
        SLOTS_AT = 12
        GATHER_AFTER = 23
        ROWS_AT = PIECES - 1

        row_loads = []
        small_loads = []

        def row(name, n, src):
            row_loads.append((vrows[row_at[name]:row_at[name] + n, :], src))

        def small(dst, src):
            small_loads.append((dst, src))

        row("attn", L * KT, attn_norm.rearrange("l (k p) -> (l k) p", p=P))
        row("ffn", L * KT, ffn_norm.rearrange("l (k p) -> (l k) p", p=P))
        row("q", L * QR // P, mla_q_norm.rearrange("l (k p) -> (l k) p", p=P))
        row("kv", L * KVR // P, mla_kv_norm.rearrange("l (k p) -> (l k) p", p=P))
        row("group", L * KT, group_norm.rearrange("l g (k p) -> (l g k) p", p=P))
        row("bs", L * 4, gmlp_b_s.rearrange("l g p -> (l g) p"))
        row("pe_k", L * 16, nsa_pe_k.rearrange("l (a b) d -> (l a) (b d)", b=2))
        row("pe_v", L * 16, nsa_pe_v.rearrange("l (a b) d -> (l a) (b d)", b=2))
        for b in range(NB):
            small(pos_i[:, b:b + 1], positions[0, b * P:(b + 1) * P].rearrange("(p o) -> p o", o=1))
        small(inv[:, :], rope_inv.to_broadcast([P, HALF]))
        small(ws_raw[:, :, :], gmlp_w_s.rearrange("l g i j -> i (l g) j"))
        for l in range(L):
            small(ln_row[:, l, :], gmlp_ln[l:l + 1, :].to_broadcast([P, GW]))
            small(cw_row[:, l, :], conv_w[l:l + 1].rearrange("l k c -> l (k c)").to_broadcast([P, 3 * GW]))
            small(w_uq[:, l, :, :], mla_w_uq[l].rearrange("(k p) n -> p k n", p=P))
            small(w_ukv[:, l, :], mla_w_ukv[l])
            small(w2[:, l, 0, :, :], nsa_w2_k[l].rearrange("(k p) n -> p k n", p=P))
            small(w2[:, l, 1, :, :], nsa_w2_v[l].rearrange("(k p) n -> p k n", p=P))
        small(w_r[:, :, :], moe_router[0].rearrange("(k p) e -> p k e", p=P))
        small(fin_row[:, :], final_norm.rearrange("(o n) -> o n", o=1).to_broadcast([P, D]))
        SMALL = 16 * len(small_loads)

        UNITS = [(kind, b, hs) for kind in range(3) for b, hs in ((0, (0, 1, 2, 3)), (1, (0, 1)), (1, (2, 3)))]
        NU = len(UNITS)
        XB = KT // 2

        block = ctx.enter_context(nc.Block())

        @block.sync
        def _(sp):
            def reader(q):
                l, j = divmod(q, MIX)
                if j < NIN:
                    return s_pp, NIN * NB * l + NB * (j + 1)
                if j < NIN + 2:
                    return s_hp, 2 * l + j - NIN + 1
                return s_wo, 4 * l + 2 * (j - NIN - 2) + 2

            def load(q, dst, src):
                l, j = divmod(q, MIX)
                if j >= RING:
                    sp.wait_ge(*reader(q - RING))
                elif l:
                    sp.wait_ge(s_hi, PIECES - 2 * RING + 2 * (j + 1))
                    sp.wait_ge(s_lo, PIECES - 2 * RING + 2 * (j + 1))
                sp.dma_start(dst, src).then_inc(loaded[q % RING], 16)

            def tiled(q):
                return wtile[q % RING].rearrange("p (k n) -> p k n", k=KT)

            def load_mixer(l):
                q = chunk_mix[l]
                for j, (c, n) in enumerate(IN_CHUNKS):
                    if l == 0 and j == 1:
                        sp.wait_ge(s_rows, 16 * len(row_loads))
                    if l == 0 and j == RING:
                        for dst, src in small_loads:
                            sp.dma_start(dst, src).then_inc(s_small, 16)
                    load(q, tiled(q)[:, :, 0:n], w_in[l, :, c:c + n].rearrange("(k p) n -> p k n", p=P))
                    q += 1
                for w1 in (nsa_w1_k, nsa_w1_v):
                    load(q, wtile[q % RING].rearrange("p (k n) -> p k n", k=16),
                         w1[l].rearrange("(k p) n -> p k n", p=P))
                    q += 1
                for c in range(0, D, W):
                    load(q, tiled(q), w_o[l, :, c:c + W].rearrange("(k p) n -> p k n", p=P))
                    q += 1

            def load_ffn(f, l, wg, wu, wd):
                for j, (part, n, hh) in enumerate(ORDER):
                    if j < 2 * RING:
                        sp.wait_ge(*reader(MIX * (l + 1) - RING + j // 2))
                    past(sp, s_hi, f * PIECES + (j - 2 * RING + 1))
                    past(sp, s_lo, f * PIECES + (j - 2 * RING + 1))
                    if part < 2:
                        src = (wg, wu)[part][hh * D // 2:(hh + 1) * D // 2, n * W:(n + 1) * W]
                        k = KT // 2
                    else:
                        src = wd[n * W + hh * W // 2:n * W + (hh + 1) * W // 2, :]
                        k = 2
                    sp.dma_start(piece_in[j % (2 * RING)].rearrange("p (k n) -> p k n", k=k),
                                 src.rearrange("(k p) n -> p k n", p=P)).then_inc(landed[j % (2 * RING)], 16)

            def load_moe(e, f):
                load_ffn(f, L - 1, *(w[0, bass.ds(e, 1), :, :].rearrange("o k n -> (o k) n")
                                     for w in (moe_w_gate, moe_w_up, moe_w_down)))

            for b in range(NB):
                sp.dma_start(h[:, b, :], x[0, b * P:(b + 1) * P, :]).then_inc(s_x, 16)
            sp.wait_ge(s_vz, 1)
            for dst, src in row_loads[1::2]:
                sp.dma_start(dst, src).then_inc(s_rows, 16)
            load_mixer(0)
            load_ffn(0, 0, dense_w_gate[0], dense_w_up[0], dense_w_down[0])
            load_mixer(1)
            with sp.Fori(0, E) as e:
                load_moe(e, e + 1)
            sp.wait_ge(s_over, 1)
            n_over = sp.value_load(over_i[0:1, 0:1], min_val=0, max_val=MAX_OVER)
            with sp.Fori(0, MAX_OVER) as i:
                with sp.If(n_over > i):
                    e = sp.value_load(over_i[0:1, bass.ds(i + 1, 1)], min_val=0, max_val=E - 1)
                    load_moe(e, i + (E + 1))
            sp.wait_ge(s_y, 2 * L + 1)
            for b in range(NB):
                sp.dma_start(out[0, b * P:(b + 1) * P, :], xs[:, b, :]).then_inc(s_out, 16)
            sp.wait_ge(s_out, 16 * NB)

        @block.gpsimd
        def _(pool):
            pc_n = [0]

            def link(ins):
                pc_n[0] += 1
                ins.then_inc(s_pchain, 1)
                pool.wait_ge(s_pchain, pc_n[0])

            pool.memset(vrows[:, :], 0.0).then_inc(s_vz, 1)
            for t, v in ((ident, 0.0), (amask, 0.0), (tri, 1.0), (ones, 1.0), (neghalf, -0.5), (hidR, 0.0),
                         (vcd, 0.0), (pc, 0.0), (shift, 0.0), (carry, 0.0), (cmask, 0.0), (cvalid, 1.0),
                         (cnt, 0.0)):
                ap = t[tuple(slice(None) for _ in t.shape)]
                last = pool.memset(ap, v)
            last.then_inc(s_zero, 1)
            pool.wait_ge(s_zero, 1)
            link(pool.iota(iota_i[:, :], [[1, P]], base=0, channel_multiplier=0))
            link(pool.affine_select(out=ident[:, :], in_=ident[:, :], compare_op=ALU.not_equal, fill=1.0,
                                    base=0, pattern=[[-1, P]], channel_multiplier=1))
            link(pool.affine_select(out=amask[:, :], in_=amask[:, :], compare_op=ALU.is_ge, fill=NEG,
                                    base=0, pattern=[[-1, P]], channel_multiplier=1))
            link(pool.affine_select(out=tri[:, :], in_=tri[:, :], compare_op=ALU.is_gt, fill=0.0,
                                    base=0, pattern=[[1, P]], channel_multiplier=-1))
            for s in (1, 2):
                link(pool.affine_select(out=shift[:, s - 1, :], in_=shift[:, s - 1, :], compare_op=ALU.not_equal,
                                        fill=1.0, base=s, pattern=[[-1, P]], channel_multiplier=1))
                link(pool.affine_select(out=carry[:, s - 1, :], in_=carry[:, s - 1, :], compare_op=ALU.not_equal,
                                        fill=1.0, base=s - P, pattern=[[-1, P]], channel_multiplier=1))
            for b in range(NB):
                link(pool.affine_select(out=cmask[:, b, :], in_=cmask[:, b, :], compare_op=ALU.is_ge, fill=NEG,
                                        base=b * P - (CMP_LEN - 1), pattern=[[-CMP_STRIDE, 16]],
                                        channel_multiplier=1))
                link(pool.affine_select(out=cvalid[:, b:b + 1], in_=cvalid[:, b:b + 1], compare_op=ALU.is_ge,
                                        fill=0.0, base=b * P - (CMP_LEN - 1), pattern=[[0, 1]],
                                        channel_multiplier=1))
            pool.tensor_copy(iota_s[:, :], iota_i[:, :]).then_inc(s_const, 1)

            def root(src, dst, n, signal):
                link(pool.tensor_scalar(src, src, EPS, None, ALU.add))
                pool.tensor_tensor(dst, src, neghalf[:, 0:n], ALU.pow).then_inc(signal, 1)

            for l in range(L):
                pool.wait_ge(s_ms, 3 * l + 1)
                root(ms[:, 0:NB], rs[:, 0:NB], NB, s_rs)
                pool.wait_ge(s_cms, l + 1)
                root(ms[:, 2:2 + 2 * NB], rs[:, 2:2 + 2 * NB], 2 * NB, s_crs)
                if l == 0:
                    pool.wait_ge(s_wsc, 1)
                    pool.affine_select(out=wsT[:, :, :], in_=wsT[:, :, :], compare_op=ALU.is_ge, fill=0.0,
                                       base=0, pattern=[[0, L * 4], [1, P]],
                                       channel_multiplier=-1).then_inc(s_ws, 1)
                pool.wait_ge(s_mv, l + 1)
                root(mv[:, :, 1], rs[:, 6:6 + NB], NB, s_grs)
                pool.wait_ge(s_ms, 3 * l + 2)
                root(ms[:, 8:8 + 4 * NB], rs[:, 8:8 + 4 * NB], 4 * NB, s_rs)
                pool.wait_ge(s_ms, 3 * l + 3)
                root(ms[:, 0:NB], rs[:, 0:NB], NB, s_rs)
            pool.wait_ge(s_ms, 3 * L + 1)
            root(ms[:, 0:NB], rs[:, 0:NB], NB, s_rs)

        @block.tensor
        def _(pe):
            def mm(o, lhsT, rhs, start, stop):
                return nc.tensor.matmul(o, lhsT, rhs, start=start, stop=stop)

            def turn(o, src, n=P):
                return nc.tensor.transpose(o, src, ident[0:n, 0:n])

            def turn_rows(t):
                pe.wait_ge(s_xs, t + 1)
                for k in range(KT):
                    for b in range(NB):
                        i = turn(bank[k // 2][:, (k % 2) * SEQ + b * P:(k % 2) * SEQ + (b + 1) * P],
                                 xs[:, b, k * P:(k + 1) * P])
                    if k % 2:
                        i.then_inc(s_xp, 1)

            def turn_latents(l):
                pe.wait_ge(s_cn, l + 1)
                for k in range(3):
                    for b in range(NB):
                        i = turn(bank[2 + k // 2][:, (k % 2) * SEQ + b * P:(k % 2) * SEQ + (b + 1) * P],
                                 cn[:, b, k * P:(k + 1) * P])
                i.then_inc(s_cp, 1)
                if l == 0:
                    pe.wait_ge(s_small, SMALL)
                    for g in range(L * 4):
                        i = turn(bank[g // 4][:, (g % 4) * P:(g % 4 + 1) * P], ws_raw[:, g, :])
                    i.then_inc(s_wsp, 1)

            def conv(l):
                pe.wait_ge(s_cu, l + 1)
                if l == 0:
                    pe.wait_ge(s_wsc, 1)
                for b in range(NB):
                    o = bank[1][:, b * GW:(b + 1) * GW]
                    mm(o, ident[:, :], conv_k[:, 2, b, :], True, False)
                    for s in (1, 2):
                        last = mm(o, shift[:, s - 1, :], conv_k[:, 2 - s, b, :], False, b == 0 and s == 2)
                    if b:
                        for s in (1, 2):
                            last = mm(o, carry[:, s - 1, :], conv_k[:, 2 - s, b - 1, :], False, s == 2)
                last.then_inc(s_cv, 1)

            def project(l):
                pe.wait_ge(s_xTa, 4 * (3 * l) + 4)
                pe.wait_ge(s_xTv, 4 * (3 * l) + 4)
                for j, (c, n) in enumerate(IN_CHUNKS):
                    q = chunk_mix[l] + j
                    ring_ready(pe, q)
                    w = wtile[q % RING].rearrange("p (k n) -> p k n", k=KT)
                    if j == NIN - 2:
                        turn_latents(l)
                    if j == NIN - 1:
                        conv(l)
                    for b in range(NB):
                        m = NB * j + b
                        if m >= 4:
                            done = NIN * l + (m - 4) // 2 + 1
                            pe.wait_ge(s_pea if m % 2 == 0 else s_pev, done)
                        for k in range(KT):
                            i = mm(bank[4 + m % 4][:, 0:n], xT[:, k, b * P:(b + 1) * P], w[:, k, 0:n],
                                   k == 0, k == KT - 1)
                        i.then_inc(s_pp, 1)

            def turn_mla(l):
                pe.wait_ge(s_rope, l + 1)
                pe.wait_ge(s_qa, l + 1)
                for hd in range(HEADS):
                    for b in range(NB):
                        cs = slice((hd % 2) * SEQ + b * P, (hd % 2) * SEQ + (b + 1) * P)
                        turn(bank[2 * (hd // 2)][0:QK, cs], q5[:, b, hd, :])
                        i = turn(bank[6 + hd // 2][0:QK, cs], kk[:, b, hd, :])
                i.then_inc(s_qTp, 1)

            def mix(l):
                pe.wait_ge(s_cT, l + 1)
                pe.wait_ge(s_pev, NIN * l + NIN - 1)
                for b in range(NB):
                    for k in range(QR // P):
                        mm(bank[2 * b][:, 0:HEADS * QK], cT[:, k, b * P:(b + 1) * P], w_uq[:, l, k, :],
                           k == 0, k == QR // P - 1)
                mm(bank[3][:, :], cT[:, 2, 0:P], w_ukv[:, l, :], True, True)
                mm(bank[7][:, :], cT[:, 2, P:2 * P], w_ukv[:, l, :], True, True).then_inc(s_qp, 1)
                out_a = NIN * (l + 1)
                pe.wait_ge(s_pea, out_a)
                pe.wait_ge(s_pev, out_a)
                for hd in range(HEADS):
                    for b in range(NB):
                        turn(bank[4 + hd // 2][0:DH, (hd % 2) * SEQ + b * P:(hd % 2) * SEQ + (b + 1) * P],
                             proj[:, b, NQ + hd * DH:NQ + (hd + 1) * DH])
                for j, c in enumerate((NKS, NKW)):
                    for b in range(NB):
                        i = turn(bank[6][0:DH, j * SEQ + b * P:j * SEQ + (b + 1) * P], proj[:, b, c:c + DH])
                i.then_inc(s_nTp, 1)
                pe.wait_ge(s_yc, l + 1)
                for j, c in enumerate((NKC, NVC)):
                    for odd in range(2):
                        for b in range(NB):
                            i = mm(bank[1][odd * DH:(odd + 1) * DH, j * P + b * DH:j * P + (b + 1) * DH],
                                   proj[:, b, c:c + DH], ident[:, odd::2], True, True)
                i.then_inc(s_zp, 1)
                pe.wait_ge(s_gv, l + 1)
                pe.wait_ge(s_nT, l + 1)
                if l == 0:
                    pe.wait_ge(s_ws, 1)
                for b in range(NB):
                    for g in range(4):
                        c = GW + g * DH
                        i = mm(bank[5][:, b * GW + g * DH:b * GW + (g + 1) * DH], wsT[:, l * 4 + g, :],
                               gel[:, b, c:c + DH], True, True)
                i.then_inc(s_sv, 1)
                pe.wait_ge(s_blk, l + 1)
                for j in range(2):
                    q = chunk_mix[l] + NIN + j
                    ring_ready(pe, q)
                    w = wtile[q % RING].rearrange("p (k n) -> p k n", k=16)
                    for k in range(16):
                        i = mm(bank[1][0:NC, j * CH:(j + 1) * CH], blk[:, j, k // 8, :, k % 8], w[:, k, :],
                               k == 0, k == 15)
                    i.then_inc(s_hp, 1)
                    if j == 0:
                        turn_mla(l)
                pe.wait_ge(s_hg, l + 1)
                for j in range(2):
                    for t in range(CH // P):
                        i = turn(bank[1][:, j * 32 + t * 16:j * 32 + t * 16 + NC],
                                 conv_u[0:NC, j, t * P:(t + 1) * P], NC)
                i.then_inc(s_hc, 1)
                pe.wait_ge(s_hr, l + 1)
                for t in range(CH // P):
                    mm(bank[3][0:DH, 0:NC], w2[:, l, 0, t, :], hidT[:, t, 0:NC], t == 0, t == CH // P - 1)
                for t in range(CH // P):
                    i = mm(bank[3][:, 64:64 + DH], hidR[:, t, :, :].rearrange("p h c -> p (h c)"),
                           w2[:, l, 1, t, :], t == 0, t == CH // P - 1)
                i.then_inc(s_kcp, 1)
                pe.wait_ge(s_kc, l + 1)
                for b in range(NB):
                    for hd in range(HEADS):
                        c = (b * HEADS + hd) * 16
                        i = mm(bank[4][:, c:c + NC], nqT[0:DH, hd, b * P:(b + 1) * P], kcT[0:DH, 0:NC], True, True)
                i.then_inc(s_scp, 1)
                pe.wait_ge(s_qT, l + 1)

            def scores(l, n):
                kind, b, hs = UNITS[n]
                m = l * NU + n
                if n < 2:
                    pe.wait_ge(s_qT, l + 1)
                else:
                    pe.wait_ge(s_e, m - 1)
                width = (b + 1) * P
                for j, hd in enumerate(hs):
                    c = j * width
                    if kind == 0:
                        q_, k_ = qT[0:QK, hd, b * P:(b + 1) * P], kT[0:QK, hd, 0:width]
                    else:
                        q_, k_ = nqT[0:DH, hd, b * P:(b + 1) * P], nkT[0:DH, kind - 1, 0:width]
                    mm(bank[n % 2][:, c:c + width], q_, k_, True, False)
                    i = mm(bank[n % 2][:, c + width - P:c + width], ident[:, :], amask[:, :], False, True)
                i.then_inc(s_sp, 1)

            def turn_probs(l, n):
                m = l * NU + n
                pe.wait_ge(s_e, m + 1)
                if n >= 2:
                    pe.wait_ge(s_tc, m - 1)
                for j in range(4):
                    i = turn(bank[2 + n % 2][:, j * P:(j + 1) * P], prob[:, n % 2, j * P:(j + 1) * P])
                i.then_inc(s_tp, 1)

            OUT_BANK = (7, 4, 5)

            def values(l, n):
                kind, b, hs = UNITS[n]
                pe.wait_ge(s_tc, l * NU + n + 1)
                for j, hd in enumerate(hs):
                    o = bank[OUT_BANK[kind]][:, b * GW + hd * DH:b * GW + (hd + 1) * DH]
                    for kb in range(b + 1):
                        v = (vv[:, kb, hd, :] if kind == 0
                             else proj[:, kb, (NVS, NVW)[kind - 1]:(NVS, NVW)[kind - 1] + DH])
                        c = (j * (b + 1) + kb) * P
                        i = mm(o, probT[:, n % 2, c:c + P], v, kb == 0, kb == b)
                i.then_inc(s_ov, 1)

            def attend(l):
                scores(l, 0)
                pe.wait_ge(s_pc, l + 1)
                for b in range(NB):
                    i = turn(bank[3][:, 128 + b * P:128 + (b + 1) * P],
                             pc[:, b, :, :].rearrange("p h c -> p (h c)"))
                i.then_inc(s_pcp, 1)
                scores(l, 1)
                pe.wait_ge(s_pcT, l + 1)
                for b in range(NB):
                    i = mm(bank[6][:, b * GW:(b + 1) * GW], pcT[:, b, :], vcd[:, :], True, True)
                i.then_inc(s_oc, 1)
                for n in range(NU):
                    turn_probs(l, n)
                    if n + 2 < NU:
                        scores(l, n + 2)
                    values(l, n)

            def output(l):
                t = 3 * l + 1
                pe.wait_ge(s_xTa, 4 * t + 4)
                pe.wait_ge(s_xTv, 4 * t + 4)
                for j in range(2):
                    q = chunk_mix[l] + NIN + 2 + j
                    ring_ready(pe, q)
                    w = wtile[q % RING].rearrange("p (k n) -> p k n", k=KT)
                    for b in range(NB):
                        for k in range(KT):
                            i = mm(bank[4 + 2 * j + b][:, :], xT[:, k, b * P:(b + 1) * P], w[:, k, :],
                                   k == 0, k == KT - 1)
                        i.then_inc(s_wo, 1)

            def ffn(f, blocks, others={}):

                def product3(o, xh_, xl_, wh_, wl_, first, last):
                    mm(o, xh_, wh_, first, False)
                    mm(o, xh_, wl_, False, False)
                    return mm(o, xl_, wh_, False, last)

                def turn_hidden(n):
                    pe.wait_ge(s_hid, f * FS + (n + 1))
                    for b in range(blocks):
                        for k in range(4):
                            last = turn(bank[2 + b if blocks == 2 else 1][:, k * P:(k + 1) * P], hid[:, b, k * P:(k + 1) * P])
                    last.then_inc(s_hT, 1)

                def piece(j):
                    part, n, hh = ORDER[j]
                    pe.wait_ge(s_lo, f * PIECES + (j + 1))
                    wh, wl = part_h[:, j % PARTS, :], part_l[:, j % PARTS, :]
                    if part < 2:
                        if (part, hh) == (0, 0):
                            past(pe, s_sg, f * FS + n)
                        if (part, hh) == (1, 0):
                            past(pe, s_hid, f * FS + n)
                            if blocks == 2:
                                past(pe, s_hTl, f * FS + n)
                        for b in range(blocks):
                            for k in range(4):
                                ks, xs_ = slice(k * W, (k + 1) * W), slice(b * P, (b + 1) * P)
                                last = product3(bank[2 * part + b][:, :], xh[:, 4 * hh + k, xs_],
                                                xl[:, 4 * hh + k, xs_], wh[:, ks], wl[:, ks],
                                                hh == 0 and k == 0, hh == 1 and k == 3)
                    else:
                        if hh == 0:
                            pe.wait_ge(s_hTl, f * FS + (n + 1))
                        if hh == 0 and n == 0 and blocks == 1:
                            pe.wait_ge(s_ysa, f)
                        for b in range(blocks):
                            for k in range(2):
                                for side in range(2):
                                    ks = slice(k * D + side * W, k * D + (side + 1) * W)
                                    xs_ = slice((2 * hh + k) * P, (2 * hh + k + 1) * P)
                                    last = product3(bank[4 + 2 * b + side][:, :], hTh[:, b, xs_], hTl[:, b, xs_],
                                                    wh[:, ks], wl[:, ks], n == 0 and hh == 0 and k == 0,
                                                    n == FS - 1 and hh == 1 and k == 1)
                    last.then_inc(s_used, 1)

                for j in range(PIECES - 2):
                    piece(j)
                    if j in others:
                        others[j]()
                    part, n, hh = ORDER[j]
                    if (part, hh) == (0, 0) and n:
                        turn_hidden(n - 1)
                turn_hidden(FS - 1)

                piece(PIECES - 2)
                piece(PIECES - 1)

            def gather(n):
                pe.wait_ge(s_gm, n + 1)
                for k in range(KT):
                    for b in range(NB):
                        last = mm(bank[6 + k // 4][:, (k % 4) * P:(k % 4 + 1) * P], xs[:, b, k * P:(k + 1) * P],
                                  gm[:, b, :], b == 0, b == NB - 1)
                last.then_inc(s_xep, 1)

            def turn_gates(n):
                for b in range(NB):
                    last = turn(bank[3][:, b * P:(b + 1) * P], gg[:, b, :])
                last.then_inc(s_ggp, 1)

            pe.wait_ge(s_const, 1)
            pe.wait_ge(s_rows, 16 * len(row_loads))
            turn(bank[7][:, 0:P], vrows[:, :]).then_inc(s_rt, 1)
            for l in range(L):
                turn_rows(3 * l)
                if l == 0:
                    pe.wait_ge(s_cols, 1)
                else:
                    pe.wait_ge(s_h, 2)
                project(l)
                mix(l)
                attend(l)
                pe.wait_ge(s_y, 2 * l + 1)
                turn_rows(3 * l + 1)
                output(l)
                turn_rows(3 * l + 2)
                pe.wait_ge(s_h, 2 * l + 1)
                pe.wait_ge(s_xTa, 4 * (3 * l + 2) + 4)
                pe.wait_ge(s_xTv, 4 * (3 * l + 2) + 4)
                if l == 0:
                    pe.wait_ge(s_xl, 2)
                    ffn(0, 2)
            for b in range(NB):
                for k in range(KT):
                    i = mm(bank[0][:, b * E:(b + 1) * E], xT[:, k, b * P:(b + 1) * P], w_r[:, k, :],
                           k == 0, k == KT - 1)
            i.then_inc(s_lp, 1)
            pe.wait_ge(s_sel, 1)
            mm(bank[1][:, 0:E], tri[:, :], rsg[:, 1, 0, :], True, True)
            mm(bank[1][:, E:2 * E], tri[:, :], rsg[:, 1, 1, :], True, False)
            mm(bank[1][:, E:2 * E], ones[:, :], rsg[:, 1, 0, :], False, True)
            mm(bank[1][:, 2 * E:3 * E], ones[:, :], rsg[:, 1, 0, :], True, False)
            mm(bank[1][:, 2 * E:3 * E], ones[:, :], rsg[:, 1, 1, :], False, True).then_inc(s_rk, 1)

            def scatter(m):
                pe.wait_ge(s_ye, m + 1)
                for b in range(NB):
                    for half in range(2):
                        last = mm(bank[6 - 2 * b + half][:, :], ggT[:, b, :], ye[:, half * W:(half + 1) * W],
                                  True, True)
                last.then_inc(s_ysp, 1)

            gather(0)
            with pe.Fori(0, E) as e:
                def scatter_before():
                    pe.wait_ge(s_ggT, e + 1)
                    scatter(e)
                    turn_gates(e)

                pe.wait_ge(s_xl, e + 3)
                ffn(e + 1, 1, {SCATTER_AFTER: scatter_before, GATHER_AFTER: lambda: gather(e + 1)})
            pe.wait_ge(s_ggT, E + 1)
            scatter(E)
            pe.wait_ge(s_over, 1)
            n_over = pe.value_load(over_i[0:1, 0:1], min_val=0, max_val=MAX_OVER)
            with pe.Fori(0, MAX_OVER) as i:
                with pe.If(n_over > i):
                    n = i + (E + 1)
                    pe.wait_ge(s_xl, n + 2)
                    pe.wait_ge(s_ysa, n)
                    pe.wait_ge(s_ggT, n)
                    gather(n)
                    turn_gates(n)
                    pe.wait_ge(s_xl, n + 3)
                    pe.wait_ge(s_ggT, n + 1)
                    ffn(n, 1)
                    scatter(n)

        @block.scalar
        def _(act):
            act.wait_ge(s_vz, 1)
            for dst, src in row_loads[0::2]:
                act.dma_start(dst, src).then_inc(s_rows, 16)

            def copy(dst, src, scale=1.0):
                return nc.scalar.activation(dst, src, ACT.Copy, scale=scale)

            sq = [0]

            def square(src, scale, total):
                if sq[0]:
                    act.wait_ge(s_achain, sq[0])
                sq[0] += 1
                nc.scalar.activation(junk[:, 0:src.shape[-1]], src, ACT.Square, scale=scale,
                                     accum_out=total).then_inc(s_achain, 1)

            def squares_done(signal):
                act.wait_ge(s_achain, sq[0])
                act.sem_inc(signal, 1)

            def mean_squares(src, first):
                for b in range(NB):
                    square(src[:, b, :], D ** -0.5, ms[:, first + b:first + b + 1])
                squares_done(s_ms)

            def turned(t, name, first):
                for k in (0, 1, 4, 5):
                    act.wait_ge(s_xp, XB * t + k // 2 + 1)
                    copy(xT[:, k, :], bank[k // 2][:, (k % 2) * SEQ:(k % 2 + 1) * SEQ],
                         columns(name, first + k)).then_inc(s_xTa, 1)

            act.wait_ge(s_x, 16 * NB)
            mean_squares(h, 0)
            act.wait_ge(s_rt, 1)
            copy(cols[:, :], bank[7][:, 0:P]).then_inc(s_cols, 1)
            act.wait_ge(s_cols, 1)

            for l in range(L):
                if l:
                    act.wait_ge(s_h, 2)
                    mean_squares(h, 0)
                turned(3 * l, "attn", KT * l)
                for j, (c, n) in enumerate(IN_CHUNKS):
                    act.wait_ge(s_pp, NIN * NB * l + NB * j + 1)
                    copy(proj[:, 0, c:c + n], bank[4 + (NB * j) % 4][:, 0:n]).then_inc(s_pea, 1)
                    if j == 0:
                        act.wait_ge(s_pea, NIN * l + 1)
                        act.wait_ge(s_pev, NIN * l + 1)
                        for b in range(NB):
                            square(proj[:, b, CQ:CQ + QR], QR ** -0.5, ms[:, 2 + b:3 + b])
                            square(proj[:, b, CKV:CKV + KVR], KVR ** -0.5, ms[:, 4 + b:5 + b])
                        squares_done(s_cms)
                    if j == NIN - 3:
                        act.wait_ge(s_cp, l + 1)
                        for k in range(2):
                            copy(cT[:, k, :], bank[2][:, k * SEQ:(k + 1) * SEQ], columns("q", 2 * l + k))
                        copy(cT[:, 2, :], bank[3][:, 0:SEQ], columns("kv", l)).then_inc(s_cT, 1)
                        if l == 0:
                            act.wait_ge(s_wsp, 1)
                            copy(wsT[:, 0:4, :].rearrange("p g j -> p (g j)"), bank[0][:, :])
                            copy(wsT[:, 4:8, :].rearrange("p g j -> p (g j)"), bank[1][:, :]).then_inc(s_wsc, 1)
                    if j == NIN - 2:
                        act.wait_ge(s_pea, NIN * l + NIN - 1)
                        act.wait_ge(s_pev, NIN * l + NIN - 1)
                        nc.scalar.activation(gel[:, :, :], proj[:, :, GU:GU + 2 * GW],
                                             ACT.Gelu_apprx_tanh).then_inc(s_gel, 1)
                        if l == 0:
                            act.wait_ge(s_ang, 1)
                            nc.scalar.activation(sin_t[:, :, :], turns[:, :, :], ACT.Sin)
                            nc.scalar.activation(cos_t[:, :, :], ang[:, :, :], ACT.Sin).then_inc(s_sin, 1)
                act.wait_ge(s_qp, l + 1)
                for b in range(NB):
                    copy(q5[:, b, 0:HEADS, :], bank[2 * b][:, 0:HEADS * QK].rearrange("p (h d) -> p h d", h=HEADS))
                    kv = bank[(3, 7)[b]][:, :].rearrange("p (h d) -> p h d", h=HEADS)
                    copy(kk[:, b, :, 0:NOPE], kv[:, :, 0:NOPE])
                    copy(vv[:, b, :, :], kv[:, :, NOPE:])
                    i = copy(q5[:, b, HEADS, NOPE:QK], proj[:, b, KR:KR + ROPE])
                i.then_inc(s_qa, 1)
                act.wait_ge(s_nTp, l + 1)
                for j in range(2):
                    copy(nqT[0:DH, 2 * j:2 * j + 2, :].rearrange("p h t -> p (h t)"), bank[4 + j][0:DH, :], DH ** -0.5)
                copy(nkT[0:DH, :, :].rearrange("p h t -> p (h t)"), bank[6][0:DH, :]).then_inc(s_nT, 1)
                act.wait_ge(s_qTp, l + 1)
                for j in range(2):
                    copy(qT[0:QK, 2 * j:2 * j + 2, :].rearrange("p h t -> p (h t)"), bank[2 * j][0:QK, :], QK ** -0.5)
                    i = copy(kT[0:QK, 2 * j:2 * j + 2, :].rearrange("p h t -> p (h t)"), bank[6 + j][0:QK, :])
                i.then_inc(s_qT, 1)
                act.wait_ge(s_pea, NIN * (l + 1))
                act.wait_ge(s_pev, NIN * (l + 1))
                act.wait_ge(s_hp, 2 * l + 2)
                nc.scalar.activation(conv_u[0:NC, :, :].rearrange("p b c -> p (b c)"), bank[1][0:NC, :],
                                     ACT.Gelu_apprx_tanh).then_inc(s_hg, 1)
                nc.scalar.activation(gexp[:, :, :], proj[:, :, NGL:END], ACT.Exp, scale=-1.0).then_inc(s_gex, 1)
                act.wait_ge(s_scm, l + 1)
                nc.scalar.activation(pc[:, :, :, 0:NC].rearrange("p b h c -> p (b h) c"), sc[:, :, 0:NC],
                                     ACT.Exp).then_inc(s_pc, 1)

                def turned_probs(n):
                    m = l * NU + n
                    act.wait_ge(s_tp, m + 1)
                    if n >= 2:
                        act.wait_ge(s_ov, m - 1)
                    copy(probT[:, n % 2, :], bank[2 + n % 2][:, :]).then_inc(s_tc, 1)

                for n, (kind, b, hs) in enumerate(UNITS):
                    m = l * NU + n
                    width = (b + 1) * P
                    act.wait_ge(s_mx, m + 1)
                    if n >= 2:
                        act.wait_ge(s_tp, m - 1)
                    for j, hd in enumerate(hs):
                        i = nc.scalar.activation(
                            prob[:, n % 2, j * width:(j + 1) * width], bank[n % 2][:, j * width:(j + 1) * width],
                            ACT.Exp, bias=nmax[:, n % 2, j:j + 1],
                            accum_out=psums[:, kind, b * HEADS + hd:b * HEADS + hd + 1])
                    i.then_inc(s_e, 1)
                    if n >= 1:
                        turned_probs(n - 1)
                turned_probs(NU - 1)
                act.wait_ge(s_y, 2 * l + 1)
                for b in range(NB):
                    for g in range(4):
                        square(y[:, b, g * GW:(g + 1) * GW], GW ** -0.5, ms[:, 8 + 4 * b + g:9 + 4 * b + g])
                squares_done(s_ms)
                turned(3 * l + 1, "group", KT * l)
                act.wait_ge(s_h, 2 * l + 1)
                mean_squares(h, 0)
                turned(3 * l + 2, "ffn", KT * l)
                if l == 0:
                    act.wait_ge(s_xTa, 12)
                    act.wait_ge(s_xTv, 12)
                    for k in range(0, KT, 4):
                        copy(xh[:, k:k + 4, :], xT[:, k:k + 4, :]).then_inc(s_xh, 1)

                    def ffn(f, blocks, others={}):
                        def split(j):
                            piece_ready(act, f, j)
                            past(act, s_used, f * PIECES + (j - PARTS + 1))
                            copy(part_h[:, j % PARTS, :], piece_in[j % (2 * RING)]).then_inc(s_hi, 1)

                        def silu(n):
                            act.wait_ge(s_used, f * PIECES + (AT[0, n, 1] + 1))
                            past(act, s_hid, f * FS + n)
                            for b in range(blocks):
                                i = nc.scalar.activation(sg[:, b, :], bank[b][:, :], ACT.Silu)
                            i.then_inc(s_sg, 1)

                        def turned_out(n):
                            act.wait_ge(s_hT, f * FS + (n + 1))
                            for b in range(blocks):
                                i = copy(hTh[:, b, :], bank[2 + b if blocks == 2 else 1][:, :])
                            i.then_inc(s_hTh, 1)

                        split_schedule(split, silu, None, turned_out, others)

                    ffn(0, 2)
            act.wait_ge(s_lm, 1)
            nc.scalar.activation(gd[:, 1, :], gd[:, 0, :], ACT.Exp).then_inc(s_le, 1)

            def rows_out(n):
                act.wait_ge(s_xep, n + 1)
                for k in range(KT):
                    i = copy(xh[:, k, 0:P], bank[6 + k // 4][:, (k % 4) * P:(k % 4 + 1) * P],
                             columns("ffn", KT * (L - 1) + k))
                i.then_inc(s_xe, 1)

            def gates_out(n):
                act.wait_ge(s_ggp, n + 1)
                copy(ggT[:, :, :].rearrange("p b t -> p (b t)"), bank[3][:, 0:NB * P]).then_inc(s_ggT, 1)

            rows_out(0)
            with act.Fori(0, E) as e:
                ffn(e + 1, 1, {ADD_AT: lambda: gates_out(e), ROWS_AT: lambda: rows_out(e + 1)})
            act.wait_ge(s_over, 1)
            n_over = act.value_load(over_i[0:1, 0:1], min_val=0, max_val=MAX_OVER)
            with act.Fori(0, MAX_OVER) as i:
                with act.If(n_over > i):
                    rows_out(i + (E + 1))
                    gates_out(i + E)
                    ffn(i + (E + 1), 1)
            act.wait_ge(s_h, 2 * L)
            mean_squares(h, 0)

        @block.vector
        def _(dve):
            ch = [0]

            def link(ins):
                ch[0] += 1
                ins.then_inc(s_chain, 1)
                dve.wait_ge(s_chain, ch[0])

            def tt(o, a, b, op):
                return nc.vector.tensor_tensor(o, a, b, op)

            def ts(o, a, s1, s2, op0, op1=None):
                if op1 is None:
                    return nc.vector.tensor_scalar(o, a, s1, None, op0)
                return nc.vector.tensor_scalar(o, a, s1, s2, op0, op1)

            dve.wait_ge(s_const, 1)
            link(ts(w8[:, :], iota_s[:, 0:E], -1.0, float(E), ALU.mult, ALU.add))

            def scale_rows(src, t):
                dve.wait_ge(s_rs, t + 1)
                if t:
                    dve.wait_ge(s_xp, XB * t)
                for b in range(NB):
                    i = ts(xs[:, b, :], src[:, b, :], rs[:, b:b + 1], None, ALU.mult)
                i.then_inc(s_xs, 1)

            def turned(t, name, first):
                if t == 0:
                    dve.wait_ge(s_cols, 1)
                for k in (2, 3, 6, 7):
                    dve.wait_ge(s_xp, XB * t + k // 2 + 1)
                    ts(xT[:, k, :], bank[k // 2][:, (k % 2) * SEQ:(k % 2 + 1) * SEQ], columns(name, first + k), None,
                       ALU.mult).then_inc(s_xTv, 1)

            for l in range(L):
                scale_rows(h, 3 * l)
                turned(3 * l, "attn", KT * l)
                for j, (c, n) in enumerate(IN_CHUNKS):
                    dve.wait_ge(s_pp, NIN * NB * l + NB * j + 2)
                    nc.vector.tensor_copy(proj[:, 1, c:c + n], bank[4 + (NB * j + 1) % 4][:, 0:n]).then_inc(s_pev, 1)
                    if j == 1:
                        dve.wait_ge(s_crs, l + 1)
                        for b in range(NB):
                            ts(cn[:, b, 0:QR], proj[:, b, CQ:CQ + QR], rs[:, 2 + b:3 + b], None, ALU.mult)
                            i = ts(cn[:, b, QR:], proj[:, b, CKV:CKV + KVR], rs[:, 4 + b:5 + b], None, ALU.mult)
                        i.then_inc(s_cn, 1)
                    if j == NIN - 3:
                        dve.wait_ge(s_pea, NIN * l + j + 1)
                        dve.wait_ge(s_pev, NIN * l + j + 1)
                        if l == 0:
                            dve.wait_ge(s_small, SMALL)
                        link(tt(conv_u[:, :, :], proj[:, :, CC:CC + GW], proj[:, :, CHV:CHV + GW], ALU.mult))
                        for k in range(3):
                            w = cw_row[:, l:l + 1, k * GW:(k + 1) * GW].to_broadcast([P, NB, GW])
                            i = tt(conv_k[:, k, :, :], conv_u[:, :, :], w, ALU.mult)
                        i.then_inc(s_cu, 1)
                        if l == 0:
                            link(nc.vector.tensor_copy(pos_f[:, :], pos_i[:, :]))
                            for b in range(NB):
                                link(ts(ang[:, b, :], inv[:, :], pos_f[:, b:b + 1], None, ALU.mult))
                            link(ts(turns[:, :, :], ang[:, :, :], 0.15915494309189535, ROUND_MAGIC, ALU.mult, ALU.add))
                            link(ts(turns[:, :, :], turns[:, :, :], -ROUND_MAGIC, None, ALU.add))
                            for part in (TWO_PI_HI, TWO_PI_LO):
                                link(ts(sin_t[:, :, :], turns[:, :, :], part, None, ALU.mult))
                                link(tt(ang[:, :, :], ang[:, :, :], sin_t[:, :, :], ALU.subtract))
                            link(ts(turns[:, :, :], ang[:, :, :], PI_SAFE, -PI_SAFE, ALU.min, ALU.max))
                            link(ts(ang[:, :, :], ang[:, :, :], 1.5707963267948966, None, ALU.add))
                            link(ts(cos_t[:, :, :], ang[:, :, :], PI_SAFE, -6.283185307179586, ALU.is_gt, ALU.mult))
                            link(tt(ang[:, :, :], ang[:, :, :], cos_t[:, :, :], ALU.add))
                            ts(ang[:, :, :], ang[:, :, :], PI_SAFE, -PI_SAFE, ALU.min, ALU.max).then_inc(s_ang, 1)
                    if j == NIN - 2:
                        dve.wait_ge(s_gel, l + 1)
                        for b in range(NB):
                            link(nc.vector.bn_stats(bn[:, b, :], gel[:, b, GW:]))
                            i = nc.vector.bn_aggr(mv[:, b, :], bn[:, b, :])
                        i.then_inc(s_mv, 1)
                        dve.wait_ge(s_grs, l + 1)
                        for b in range(NB):
                            link(ts(gel[:, b, GW:], gel[:, b, GW:], mv[:, b, 0:1], rs[:, 6 + b:7 + b],
                                    ALU.subtract, ALU.mult))
                        tt(gel[:, :, GW:], gel[:, :, GW:], ln_row[:, l:l + 1, :].to_broadcast([P, NB, GW]),
                           ALU.mult).then_inc(s_gv, 1)
                        dve.wait_ge(s_cv, l + 1)
                        tt(y[:, :, GW:2 * GW], bank[1][:, :].rearrange("p (b n) -> p b n", b=NB),
                           proj[:, :, CB:CB + GW], ALU.mult).then_inc(s_yc, 1)
                        dve.wait_ge(s_yc, l + 1)
                dve.wait_ge(s_zp, l + 1)
                for j, name in enumerate(("pe_k", "pe_v")):
                    z = bank[1][:, j * P:(j + 1) * P].rearrange("p (c r) -> p c r", r=8)
                    for a in range(2):
                        c = row_at[name] + 16 * l + 8 * a
                        pe_ = cols[:, None, c:c + 8].to_broadcast([P, NC, 8])
                        i = tt(blk[:, j, a, :, :], z[:, a:a + NC, :], pe_, ALU.add)
                i.then_inc(s_blk, 1)
                dve.wait_ge(s_qa, l + 1)
                if l == 0:
                    dve.wait_ge(s_sin, 1)
                x1, x2 = q5[:, :, :, NOPE:NOPE + HALF], q5[:, :, :, NOPE + HALF:]
                five = [P, NB, HEADS + 1, HALF]
                cos_b = cos_t[:, :, None, :].to_broadcast(five)
                sin_b = sin_t[:, :, None, :].to_broadcast(five)
                tt(rt[:, 0], x1, cos_b, ALU.mult)
                tt(rt[:, 1], x2, sin_b, ALU.mult)
                tt(rt[:, 2], x1, sin_b, ALU.mult)
                link(tt(rt[:, 3], x2, cos_b, ALU.mult))
                tt(x1, rt[:, 0], rt[:, 1], ALU.subtract)
                link(tt(x2, rt[:, 2], rt[:, 3], ALU.add))
                for b in range(NB):
                    i = nc.vector.tensor_copy(kk[:, b, :, NOPE:],
                                              q5[:, b, HEADS:HEADS + 1, NOPE:].to_broadcast([P, HEADS, ROPE]))
                i.then_inc(s_rope, 1)
                dve.wait_ge(s_sv, l + 1)
                for g in range(4):
                    link(nc.vector.scalar_tensor_tensor(
                        out=y[:, :, 2 * GW + g * DH:2 * GW + (g + 1) * DH],
                        in0=bank[5][:, :].rearrange("p (b n) -> p b n", b=NB)[:, :, g * DH:(g + 1) * DH],
                        scalar=columns("bs", 4 * l + g), in1=gel[:, :, g * DH:(g + 1) * DH],
                        op0=ALU.add, op1=ALU.mult))
                dve.wait_ge(s_hc, l + 1)
                hid_ps = bank[1][:, 0:64].rearrange("p (j t c) -> p j t c", j=2, t=2)
                nc.vector.tensor_copy(hidT[:, :, 0:NC], hid_ps[:, 0, :, 0:NC])
                for t in range(CH // P):
                    i = nc.vector.tensor_copy(hidR[:, t, :, 0:NC],
                                              hid_ps[:, 1, t:t + 1, 0:NC].to_broadcast([P, HEADS, NC]))
                i.then_inc(s_hr, 1)
                dve.wait_ge(s_kcp, l + 1)
                nc.vector.tensor_copy(kcT[0:DH, 0:NC], bank[3][0:DH, 0:NC])
                for hd in range(HEADS):
                    i = nc.vector.tensor_copy(vcd[32 * hd:32 * hd + 32, hd * DH:(hd + 1) * DH],
                                              bank[3][32 * hd:32 * hd + 32, 64:64 + DH])
                i.then_inc(s_kc, 1)
                dve.wait_ge(s_gex, l + 1)
                link(ts(gexp[:, :, :], gexp[:, :, :], 1.0, None, ALU.add))
                link(nc.vector.reciprocal(gsig[:, :, :], gexp[:, :, :]))
                dve.wait_ge(s_scp, l + 1)
                for b in range(NB):
                    link(tt(sc[:, b * HEADS:(b + 1) * HEADS, :][:, :, 0:NC],
                            bank[4][:, b * 64:(b + 1) * 64].rearrange("p (h c) -> p h c", c=16)[:, :, 0:NC],
                            cmask[:, b:b + 1, 0:NC].to_broadcast([P, HEADS, NC]), ALU.add))
                link(nc.vector.tensor_reduce(scm[:, :], sc[:, :, 0:NC], AX_X, ALU.max))
                tt(sc[:, :, 0:NC], sc[:, :, 0:NC], scm[:, :, None].to_broadcast([P, NB * HEADS, NC]),
                   ALU.subtract).then_inc(s_scm, 1)

                def row_max(n):
                    kind, b, hs = UNITS[n]
                    m = l * NU + n
                    dve.wait_ge(s_sp, m + 1)
                    if n >= 2:
                        dve.wait_ge(s_e, m - 1)
                    nc.vector.tensor_reduce(
                        nmax[:, n % 2, 0:len(hs)],
                        bank[n % 2][:, :].rearrange("p (h k) -> p h k", h=len(hs)), AX_X, ALU.max,
                        negate=True).then_inc(s_mx, 1)

                row_max(0)
                dve.wait_ge(s_pc, l + 1)
                link(nc.vector.tensor_reduce(pcs[:, :], pc[:, :, :, 0:NC].rearrange("p b h c -> p (b h) c"),
                                             AX_X, ALU.add))
                dve.wait_ge(s_pcp, l + 1)
                nc.vector.tensor_copy(pcT[:, :, :].rearrange("p b t -> p (b t)"),
                                      bank[3][:, 128:128 + NB * P]).then_inc(s_pcT, 1)
                row_max(1)
                link(nc.vector.reciprocal(pcs[:, :], pcs[:, :]))
                link(tt(pcs[:, :].rearrange("p (b h) -> p b h", b=NB), pcs[:, :].rearrange("p (b h) -> p b h", b=NB),
                        cvalid[:, :, None].to_broadcast([P, NB, HEADS]), ALU.mult))
                for n in range(2, NU):
                    row_max(n)
                dve.wait_ge(s_ov, l * NU + NU)
                link(nc.vector.reciprocal(prec[:, :, :], psums[:, :, :]))
                full = [P, NB * HEADS, DH]

                def spread(ap):
                    return ap[:, :, None].to_broadcast(full)

                def heads(ap):
                    return ap.rearrange("p (h d) -> p h d", d=DH)

                for b in range(NB):
                    link(tt(y[:, b, 0:GW].rearrange("p (h d) -> p h d", d=DH),
                            heads(bank[7][:, :])[:, b * HEADS:(b + 1) * HEADS, :],
                            prec[:, 0, b * HEADS:(b + 1) * HEADS, None].to_broadcast([P, HEADS, DH]), ALU.mult))
                gate3 = gsig[:, :, :].rearrange("p b (h k) -> p (b h) k", k=3)
                tt(coef[:, 0, :], pcs[:, :], gate3[:, :, 0], ALU.mult)
                tt(coef[:, 1, :], prec[:, 1, :], gate3[:, :, 1], ALU.mult)
                link(tt(coef[:, 2, :], prec[:, 2, :], gate3[:, :, 2], ALU.mult))
                dve.wait_ge(s_oc, l + 1)
                t0 = nsa_t[:, 0].rearrange("p b (h d) -> p (b h) d", d=DH)
                t1 = nsa_t[:, 1].rearrange("p b (h d) -> p (b h) d", d=DH)
                tt(t0, heads(bank[6][:, :]), spread(coef[:, 0, :]), ALU.mult)
                link(tt(t1, heads(bank[4][:, :]), spread(coef[:, 1, :]), ALU.mult))
                link(tt(t0, t0, t1, ALU.add))
                link(tt(t1, heads(bank[5][:, :]), spread(coef[:, 2, :]), ALU.mult))
                tt(y[:, :, 3 * GW:], nsa_t[:, 0], nsa_t[:, 1], ALU.add).then_inc(s_y, 1)
                dve.wait_ge(s_y, 2 * l + 1)
                dve.wait_ge(s_rs, 3 * l + 2)
                dve.wait_ge(s_xp, XB * (3 * l + 1))
                for b in range(NB):
                    for g in range(4):
                        i = ts(xs[:, b, g * GW:(g + 1) * GW], y[:, b, g * GW:(g + 1) * GW],
                               rs[:, 8 + 4 * b + g:9 + 4 * b + g], None, ALU.mult)
                i.then_inc(s_xs, 1)
                turned(3 * l + 1, "group", KT * l)
                for j in range(2):
                    dve.wait_ge(s_wo, 4 * l + 2 * (j + 1))
                    for b in range(NB):
                        i = tt(h[:, b, j * W:(j + 1) * W], h[:, b, j * W:(j + 1) * W], bank[4 + 2 * j + b][:, :],
                               ALU.add)
                i.then_inc(s_h, 1)
                dve.wait_ge(s_h, 2 * l + 1)
                scale_rows(h, 3 * l + 2)
                turned(3 * l + 2, "ffn", KT * l)
                dve.sem_inc(s_y, 1)
                if l == 0:
                    dve.wait_ge(s_xTa, 12)
                    dve.wait_ge(s_xTv, 12)
                    for j, k in enumerate(range(0, KT, 4)):
                        dve.wait_ge(s_xh, j + 1)
                        tt(xl[:, k:k + 4, :], xT[:, k:k + 4, :], xh[:, k:k + 4, :].bitcast(F32),
                           ALU.subtract).then_inc(s_xl, 1)

                    def ffn(f, blocks, others={}):
                        def split(j):
                            dve.wait_ge(s_hi, f * PIECES + (j + 1))
                            tt(part_l[:, j % PARTS, :], piece_in[j % (2 * RING)], part_h[:, j % PARTS, :].bitcast(F32),
                               ALU.subtract).then_inc(s_lo, 1)

                        def product(n):
                            dve.wait_ge(s_sg, f * FS + (n + 1))
                            dve.wait_ge(s_used, f * PIECES + (AT[1, n, 1] + 1))
                            past(dve, s_hT, f * FS + n)
                            for b in range(blocks):
                                i = tt(hid[:, b, :], bank[2 + b][:, :], sg[:, b, :], ALU.mult)
                            i.then_inc(s_hid, 1)

                        def turned_out(n):
                            dve.wait_ge(s_hTh, f * FS + (n + 1))
                            for b in range(blocks):
                                i = tt(hTl[:, b, :], bank[2 + b if blocks == 2 else 1][:, :],
                                       hTh[:, b, :].bitcast(F32), ALU.subtract)
                            i.then_inc(s_hTl, 1)

                        split_schedule(split, None, product, turned_out, others)

                    ffn(0, 2)
                    dve.wait_ge(s_used, PIECES)
                    for b in range(NB):
                        for half in range(2):
                            i = tt(h[:, b, half * W:(half + 1) * W], h[:, b, half * W:(half + 1) * W],
                                   bank[4 + 2 * b + half][:, :], ALU.add)
                    i.then_inc(s_h, 1)
                    dve.wait_ge(s_h, 2)

            dve.wait_ge(s_lp, 1)
            wide = [P, NB, E]
            link(nc.vector.tensor_copy(lg[:, :, :].rearrange("p b e -> p (b e)"), bank[0][:, 0:NB * E]))
            for k in range(2):
                src = lg if k == 0 else lg2
                link(nc.vector.tensor_reduce(top[:, k, :], src[:, :, :], AX_X, ALU.max))
                link(tt(rt_a[:, :, :], src[:, :, :], top[:, k, :, None].to_broadcast(wide), ALU.is_equal))
                link(tt(rt_a[:, :, :], rt_a[:, :, :], w8[:, None, :].to_broadcast(wide), ALU.mult))
                link(nc.vector.tensor_reduce(fst[:, :], rt_a[:, :, :], AX_X, ALU.max))
                link(tt(oh[:, k], rt_a[:, :, :], fst[:, :, None].to_broadcast(wide), ALU.is_equal))
                if k == 0:
                    link(ts(lg2[:, :, :], oh[:, 0], -HUGE, None, ALU.mult))
                    link(tt(lg2[:, :, :], lg2[:, :, :], lg[:, :, :], ALU.add))
            tt(gd[:, 0, :], top[:, 1, :], top[:, 0, :], ALU.subtract).then_inc(s_lm, 1)
            tt(rsg[:, 1], oh[:, 0], oh[:, 1], ALU.add).then_inc(s_sel, 1)
            dve.wait_ge(s_le, 1)
            link(ts(gd[:, 2, :], gd[:, 1, :], 1.0, None, ALU.add))
            link(nc.vector.reciprocal(gw[:, 0, :], gd[:, 2, :]))
            link(tt(gw[:, 1, :], gd[:, 1, :], gw[:, 0, :], ALU.mult))
            for k in range(2):
                link(tt(oh[:, k], oh[:, k], gw[:, k, :, None].to_broadcast(wide), ALU.mult))
            link(tt(rsg[:, 2], oh[:, 0], oh[:, 1], ALU.add))
            dve.wait_ge(s_rk, 1)
            nc.vector.tensor_copy(total[:, :], bank[1][:, NB * E:(NB + 1) * E])
            link(nc.vector.tensor_copy(rsg[:, 0].rearrange("p b e -> p (b e)"), bank[1][:, 0:NB * E]))

            def slots(n, key):
                ts(eqm[:, :], key, cnt[:, 0:1], None, ALU.is_equal).then_inc(s_col, 1)
                dve.wait_ge(s_col, COLS * n + 1)
                tt(pick[:, :, :], rsg[:, :, :, :].rearrange("p k b e -> p (k b) e"),
                   eqm[:, None, :].to_broadcast([P, 3 * NB, E]), ALU.mult).then_inc(s_col, 1)
                ts(cnt[:, 0:1], cnt[:, 0:1], 1.0, None, ALU.add).then_inc(s_col, 1)
                dve.wait_ge(s_col, COLS * n + 3)
                nc.vector.tensor_reduce(col[:, :], pick[:, :, :], AX_X, ALU.add).then_inc(s_col, 1)
                dve.wait_ge(s_col, COLS * n + 4)
                for b in range(NB):
                    ts(gm[:, b, :], iota_s[:, :], col[:, b:b + 1], col[:, NB + b:NB + b + 1],
                       ALU.is_equal, ALU.mult)
                    i = ts(gg[:, b, :], iota_s[:, :], col[:, b:b + 1], col[:, 2 * NB + b:2 * NB + b + 1],
                           ALU.is_equal, ALU.mult)
                i.then_inc(s_gm, 1)

            COLS = 4

            def rows_low(n):
                dve.wait_ge(s_xe, n + 1)
                for k in range(KT):
                    i = nc.vector.scalar_tensor_tensor(
                        out=xl[:, k, 0:P], in0=bank[6 + k // 4][:, (k % 4) * P:(k % 4 + 1) * P],
                        scalar=columns("ffn", KT * (L - 1) + k), in1=xh[:, k, 0:P].bitcast(F32),
                        op0=ALU.mult, op1=ALU.subtract)
                i.then_inc(s_xl, 1)

            def rows_from(m):
                dve.wait_ge(s_used, (m + 1) * PIECES)
                nc.vector.tensor_copy(ye[:, 0:W], bank[4][:, :])
                nc.vector.tensor_copy(ye[:, W:], bank[5][:, :]).then_inc(s_ye, 1)

            def add(m):
                dve.wait_ge(s_ysp, m + 1)
                past(dve, s_yadd, m)
                for b in range(NB):
                    for half in range(2):
                        i = tt(h[:, b, half * W:(half + 1) * W], h[:, b, half * W:(half + 1) * W],
                               bank[6 - 2 * b + half][:, :], ALU.add)
                i.then_inc(s_yadd, 1)
                dve.wait_ge(s_yadd, m + 1)
                dve.sem_inc(s_ysa, 1)

            experts = iota_s[:, 0:E]
            nc.vector.memset(ggT[:, :, :], 0.0).then_inc(s_ggT, 1)
            slots(0, experts)
            rows_low(0)
            link(ts(okey[:, 0, :], total[:, :], float(SLOTS), None, ALU.is_gt))
            link(nc.vector.tensor_tensor_scan(okey[:, 1, :], ones[:, 0:E], okey[:, 0, :], 0.0,
                                              ALU.mult, ALU.add))
            link(nc.vector.tensor_reduce(over_f[:, 0:1], okey[:, 1, :], AX_X, ALU.max))
            link(tt(okey[:, 0, :], okey[:, 0, :], okey[:, 1, :], ALU.mult))
            link(tt(over_e[:, :, :], okey[:, 0:1, :].to_broadcast([P, MAX_OVER, E]),
                    iota_s[:, 1:MAX_OVER + 1, None].to_broadcast([P, MAX_OVER, E]), ALU.is_equal))
            link(tt(over_e[:, :, :], over_e[:, :, :], iota_s[:, None, 0:E].to_broadcast([P, MAX_OVER, E]), ALU.mult))
            link(nc.vector.tensor_reduce(over_f[:, 1:], over_e[:, :, :], AX_X, ALU.add))
            nc.vector.tensor_copy(over_i[:, :], over_f[:, :]).then_inc(s_over, 1)
            with dve.Fori(0, E) as e:
                def next_slots():
                    dve.wait_ge(s_xep, e + 1)
                    dve.wait_ge(s_ggp, e + 1)
                    slots(e + 1, experts)

                ffn(e + 1, 1, {YE_AT: lambda: rows_from(e), ADD_AT: lambda: add(e), SLOTS_AT: next_slots,
                               ROWS_AT: lambda: rows_low(e + 1)})
            rows_from(E)
            add(E)
            dve.wait_ge(s_col, COLS * (E + 1))
            link(ts(rsg[:, 0], rsg[:, 0], -float(SLOTS), None, ALU.add))
            link(nc.vector.memset(cnt[:, :], 1.0))
            dve.wait_ge(s_over, 1)
            n_over = dve.value_load(over_i[0:1, 0:1], min_val=0, max_val=MAX_OVER)
            with dve.Fori(0, MAX_OVER) as i:
                with dve.If(n_over > i):
                    n = i + (E + 1)
                    dve.wait_ge(s_xep, n)
                    dve.wait_ge(s_ggp, i + E)
                    slots(n, okey[:, 0, :])
                    rows_low(n)
                    ffn(n, 1)
                    rows_from(n)
                    add(n)
            dve.sem_inc(s_h, 1)
            dve.wait_ge(s_rs, 3 * L + 1)
            for b in range(NB):
                link(ts(xs[:, b, :], h[:, b, :], rs[:, b:b + 1], None, ALU.mult))
                i = tt(xs[:, b, :], xs[:, b, :], fin_row[:, :], ALU.mult)
            i.then_inc(s_y, 1)


_INS = ['x', 'positions', 'rope_inv', 'attn_norm', 'w_in', 'mla_q_norm', 'mla_w_uq', 'mla_kv_norm', 'mla_w_ukv',
        'conv_w', 'gmlp_ln', 'gmlp_w_s', 'gmlp_b_s', 'nsa_pe_k', 'nsa_w1_k', 'nsa_w2_k', 'nsa_pe_v', 'nsa_w1_v',
        'nsa_w2_v', 'group_norm', 'w_o', 'ffn_norm', 'dense_w_gate', 'dense_w_up', 'dense_w_down',
        'moe_router', 'moe_w_gate', 'moe_w_up', 'moe_w_down', 'final_norm']


def kernel(**inputs):
    import numpy as _np
    import concourse.bacc as _bacc
    from concourse import mybir as _mybir
    from concourse.bass_utils import run_bass_kernel_spmd as _run

    rope_inv = (_np.float32(10000.0) ** (-_np.arange(HALF, dtype=_np.float32) / _np.float32(HALF))).reshape(1, HALF)
    nc = _bacc.Bacc("TRN2", target_bir_lowering=False, num_devices=1)
    arrays, args = {}, []
    for name in _INS:
        a = _np.ascontiguousarray(rope_inv if name == 'rope_inv' else inputs[name])
        arrays[f"in_{name}_dram"] = a
        args.append(nc.dram_tensor(f"in_{name}_dram", a.shape, _mybir.dt.from_np(a.dtype), kind="ExternalInput").ap())
    shape = tuple(inputs['x'].shape)
    args.append(nc.dram_tensor("out_0_dram", shape, F32, kind="ExternalOutput").ap())
    hybrid_trunk(nc, *args)
    r = _run(nc, [arrays], core_ids=[0])
    return r.results[0]["out_0_dram"]
```

```python
from contextlib import ExitStack

import concourse.bass as bass
from concourse import mybir

ALU = mybir.AluOpType
ACT = mybir.ActivationFunctionType
F32 = mybir.dt.float32
F32R = mybir.dt.float32r
I32 = mybir.dt.int32
AX_X = mybir.AxisListType.X

P = 128
EPS = 1e-6
NEG = -1e30
HUGE = 3.0e38
NOPE, ROPE, HEADS = 64, 32, 4
QK = NOPE + ROPE
HALF = ROPE // 2
DH = 64
CMP_STRIDE, CMP_LEN = 16, 32
TWO_PI_HI = 6.28125
TWO_PI_LO = 0.0019353071795864769
ROUND_MAGIC = 12582912.0
PI_SAFE = 3.1415925
W = 512
RING = 3
PARTS = 3


def hybrid_trunk(nc, x, positions, rope_inv, attn_norm, w_in, mla_q_norm, mla_w_uq, mla_kv_norm, mla_w_ukv,
                 conv_w, gmlp_ln, gmlp_w_s, gmlp_b_s, nsa_pe_k, nsa_w1_k, nsa_w2_k, nsa_pe_v, nsa_w1_v, nsa_w2_v,
                 group_norm, w_o, ffn_norm, dense_w_gate, dense_w_up, dense_w_down,
                 moe_router, moe_w_gate, moe_w_up, moe_w_down, final_norm, out):
    _, SEQ, D = x.shape
    L = attn_norm.shape[0]
    NB = SEQ // P
    KT = D // P
    D_IN = w_in.shape[2]
    FF = dense_w_gate.shape[2]
    FS = FF // W
    E = moe_w_gate.shape[1]
    GW = D // 4
    QR, KVR = mla_q_norm.shape[1], mla_kv_norm.shape[1]
    NC = SEQ // CMP_STRIDE - CMP_LEN // CMP_STRIDE + 1
    CH = nsa_w1_k.shape[2]
    assert NB == 2 and L == 2 and KT == 8 and FF % W == 0 and E == 8

    sizes = [QR, KVR, ROPE, GW, GW, GW, GW, GW, HEADS * DH] + [DH] * 6 + [HEADS * 3]
    at = [sum(sizes[:i]) for i in range(len(sizes) + 1)]
    (CQ, CKV, KR, CB, CC, CHV, GU, GV, NQ, NKC, NVC, NKS, NVS, NKW, NVW, NGL, END) = at
    assert END == D_IN
    IN_CHUNKS = [(c, min(W, D_IN - c)) for c in range(0, D_IN, W)]
    NIN = len(IN_CHUNKS)

    MIX = NIN + 4
    assert MIX % RING == 0
    ORDER = [(0, 0, 0), (0, 0, 1), (1, 0, 0), (1, 0, 1)]
    for n in range(1, FS):
        ORDER += [(0, n, 0), (0, n, 1), (1, n, 0), (1, n, 1), (2, n - 1, 0), (2, n - 1, 1)]
    ORDER += [(2, FS - 1, 0), (2, FS - 1, 1)]
    PIECES = len(ORDER)
    AT = {piece: j for j, piece in enumerate(ORDER)}
    assert PIECES % (2 * RING) == 0 and PIECES % PARTS == 0
    chunk_mix = [0, MIX]
    SLOTS = P
    MAX_OVER = 2 * SEQ // (SLOTS + 1)

    row_at, rows = {}, 0
    for name, n in (("attn", L * KT), ("ffn", L * KT), ("q", L * QR // P), ("kv", L * KVR // P),
                    ("group", L * KT), ("bs", L * 4), ("pe_k", L * 16), ("pe_v", L * 16)):
        row_at[name] = rows
        rows += n
    assert rows <= P

    with ExitStack() as ctx:
        def sb(name, shape, dt=F32):
            return ctx.enter_context(nc.sbuf_tensor(name, shape, dt))

        def sem(name):
            return ctx.enter_context(nc.semaphore(name))

        bank = [ctx.enter_context(nc.psum_tensor(f"bank{i}", [P, W], F32)) for i in range(8)]

        ring = sb("ring", [P, RING, KT * W])
        h = sb("h", [P, NB, D])
        xs = sb("xs", [P, NB, D])
        with nc.sbuf_tensor("pxh", [P, KT, SEQ], F32R) as pxh:
            pass
        xT = sb("xT", [P, KT, SEQ])
        y = sb("y", [P, NB, D])
        vrows = sb("vrows", [P, P])
        cols = sb("cols", [P, P])
        ident = sb("ident", [P, P])
        amask = sb("amask", [P, P])
        tri = sb("tri", [P, P])
        ones = sb("ones", [P, P])
        shift = sb("shift", [P, 2, P])
        carry = sb("carry", [P, 2, P])
        iota_i = sb("iota_i", [P, P], I32)
        iota_s = sb("iota_s", [P, P])
        cmask = sb("cmask", [P, NB, 16])
        cvalid = sb("cvalid", [P, NB])
        neghalf = sb("neghalf", [P, 16])
        pos_i = sb("pos_i", [P, NB], I32)
        pos_f = sb("pos_f", [P, NB])
        inv = sb("inv", [P, HALF])
        ang = sb("ang", [P, NB, HALF])
        turns = sb("turns", [P, NB, HALF])
        sin_t = sb("sin_t", [P, NB, HALF])
        cos_t = sb("cos_t", [P, NB, HALF])
        ln_row = sb("ln_row", [P, L, GW])
        cw_row = sb("cw_row", [P, L, 3 * GW])
        fin_row = sb("fin_row", [P, D])
        w_uq = sb("w_uq", [P, L, QR // P, HEADS * QK])
        w_ukv = sb("w_ukv", [P, L, HEADS * 2 * DH])
        w2 = sb("w2", [P, L, 2, CH // P, DH])
        ws_raw = y[:, 0, :].rearrange("p (g j) -> p g j", g=L * 4)
        wsT = sb("wsT", [P, L * 4, P])
        w_r = sb("w_r", [P, KT, E])
        bn = sb("bn", [P, NB, 6])
        mv = sb("mv", [P, NB, 2])
        hidT = sb("hidT", [P, CH // P, 16])
        hidR = sb("hidR", [P, CH // P, HEADS, 32])
        kcT = sb("kcT", [P, 16])
        vcd = sb("vcd", [P, HEADS * DH])
        sc = sb("sc", [P, NB * HEADS, 16])
        scm = sb("scm", [P, NB * HEADS])
        pc = sb("pc", [P, NB, HEADS, 32])
        pcs = sb("pcs", [P, NB * HEADS])
        nmax = sb("nmax", [P, 2, HEADS])
        psums = sb("psums", [P, 3, NB * HEADS])
        prec = sb("prec", [P, 3, NB * HEADS])
        gexp = sb("gexp", [P, NB, HEADS * 3])
        gsig = sb("gsig", [P, NB, HEADS * 3])
        coef = sb("coef", [P, 3, NB * HEADS])
        ms = sb("ms", [P, 16])
        rs = sb("rs", [P, 16])
        lg = sb("lg", [P, NB, E])
        lg2 = sb("lg2", [P, NB, E])
        w8 = sb("w8", [P, E])
        rt_a = sb("rt_a", [P, NB, E])
        oh = sb("oh", [P, 2, NB, E])
        top = sb("top", [P, 2, NB])
        fst = sb("fst", [P, NB])
        gw = sb("gw", [P, 2, NB])
        gd = sb("gd", [P, 3, NB])
        rsg = sb("rsg", [P, 3, NB, E])
        cnt = sb("cnt", [P, 2])
        total = sb("total", [P, E])
        okey = sb("okey", [P, 2, E])
        over_e = sb("over_e", [P, MAX_OVER, E])
        over_f = sb("over_f", [P, 1 + MAX_OVER])
        over_i = sb("over_i", [P, 1 + MAX_OVER], I32)
        eqm = sb("eqm", [P, E])
        pick = sb("pick", [P, 3 * NB, E])
        col = sb("col", [P, 3 * NB])
        gm = sb("gm", [P, NB, P])
        gg = sb("gg", [P, NB, P])
        ggT = sb("ggT", [P, NB, P])

        temporary = ExitStack()

        def tsb(name, shape):
            return temporary.enter_context(nc.sbuf_tensor(name, shape, F32))

        proj = tsb("proj", [P, NB, D_IN])
        gel = tsb("gel", [P, NB, 2 * GW])
        conv_u = tsb("conv_u", [P, NB, GW])
        conv_k = tsb("conv_k", [P, 3, NB, GW])
        cn = tsb("cn", [P, NB, QR + KVR])
        with nc.sbuf_tensor("mask_r", [P, 3, P], F32R) as mask_r:
            pass
        cT = tsb("cT", [P, 3, SEQ])
        projecting = ExitStack()
        in_h = projecting.enter_context(nc.sbuf_tensor("in_h", [P, 2, KT * W // 2], F32R))
        in_l = projecting.enter_context(nc.sbuf_tensor("in_l", [P, 2, KT * W // 2], F32R))
        pxl = projecting.enter_context(nc.sbuf_tensor("pxl", [P, KT, SEQ], F32R))
        projecting.close()
        q5 = tsb("q5", [P, NB, HEADS + 1, QK])
        kk = tsb("kk", [P, NB, HEADS, QK])
        vv = tsb("vv", [P, NB, HEADS, DH])
        rt = tsb("rt", [P, 4, NB, HEADS + 1, HALF])
        qT = tsb("qT", [P, HEADS, SEQ])
        kT = tsb("kT", [P, HEADS, SEQ])
        nqT = tsb("nqT", [P, HEADS, SEQ])
        nkT = tsb("nkT", [P, 2, SEQ])
        blk = tsb("blk", [P, 2, 2, NC, 8])
        pcT = tsb("pcT", [P, NB, P])
        prob = tsb("prob", [P, 2, W])
        probT = tsb("probT", [P, 2, W])
        nsa_t = tsb("nsa_t", [P, 2, NB, GW])
        junk = tsb("junk", [P, D])
        temporary.close()
        part_h = sb("part_h", [P, PARTS, KT * W // 2], F32R)
        part_l = sb("part_l", [P, PARTS, KT * W // 2], F32R)
        xh = sb("xh", [P, KT, SEQ], F32R)
        xl = sb("xl", [P, KT, SEQ], F32R)
        hTh = sb("hTh", [P, NB, W], F32R)
        hTl = sb("hTl", [P, NB, W], F32R)
        sg = sb("sg", [P, NB, W])
        hid = y[:, 1, :].rearrange("p (s n) -> p s n", s=2)
        ye = y[:, 0, :]

        loaded = [sem(f"ring_loaded{i}") for i in range(RING)]
        landed = [sem(f"piece_landed{i}") for i in range(2 * RING)]
        s_hi = sem("high_part_ready")
        s_lo = sem("low_part_ready")
        s_used = sem("piece_used")
        s_xh = sem("ffn_rows_high")
        s_xl = sem("ffn_rows_low")
        s_rows = sem("vectors_loaded")
        s_small = sem("small_loaded")
        s_x = sem("x_loaded")
        s_vz = sem("vectors_zeroed")
        s_zero = sem("zeroed")
        s_const = sem("constants_built")
        s_rt = sem("rows_turned")
        s_cols = sem("columns_ready")
        s_wsp = sem("ws_turned")
        s_wsc = sem("ws_copied")
        s_ws = sem("ws_masked")
        s_ang = sem("angles_ready")
        s_sin = sem("sines_ready")
        s_chain = sem("vector_chain")
        s_achain = sem("scalar_chain")
        s_pchain = sem("pool_chain")
        s_ms = sem("mean_square_ready")
        s_rs = sem("rms_scale_ready")
        s_xs = sem("rows_scaled")
        s_gms = sem("group_mean_squares")
        s_gsc = sem("group_scales")
        s_gxs = sem("groups_scaled")
        s_hb = sem("residual_block_ready")
        s_hms = sem("block_mean_square")
        s_hrs = sem("block_scale")
        s_yg = sem("gmlp_out")
        s_ym = sem("mla_out")
        s_xp = sem("rows_turned_in_psum")
        s_xTa = sem("turned_by_scalar")
        s_xTv = sem("turned_by_vector")
        s_pxh = sem("projected_rows_high")
        s_pxl = sem("projected_rows_low")
        s_first = sem("first_half_chunk_loaded")
        s_hd = sem("dense_residual_block_ready")
        s_mr = sem("mask_rounded")
        s_inh = sem("input_weights_high")
        s_inl = sem("input_weights_low")
        s_inu = sem("first_half_chunk_used")
        s_pp = sem("projection_in_psum")
        s_pea = sem("projection_out_by_scalar")
        s_pev = sem("projection_out_by_vector")
        s_h = sem("residual_ready")
        s_gel = sem("gelu_ready")
        s_gex = sem("gate_exp_ready")
        s_cms = sem("latent_mean_square")
        s_crs = sem("latent_scale")
        s_cn = sem("latent_scaled")
        s_cp = sem("latent_turned")
        s_cT = sem("latent_ready")
        s_qp = sem("q_and_kv_in_psum")
        s_qa = sem("q_and_kv_out")
        s_rope = sem("rope_done")
        s_qTp = sem("mla_qk_turned")
        s_qT = sem("mla_qk_ready")
        s_nTp = sem("nsa_qk_turned")
        s_nT = sem("nsa_qk_ready")
        s_zp = sem("compress_turned")
        s_blk = sem("blocks_ready")
        s_hp = sem("compress_hidden_in_psum")
        s_hg = sem("compress_hidden_ready")
        s_hc = sem("compress_hidden_turned")
        s_hr = sem("compress_hidden_repeated")
        s_kcp = sem("compressed_kv_in_psum")
        s_kc = sem("compressed_kv_ready")
        s_scp = sem("compressed_scores_in_psum")
        s_scm = sem("compressed_scores_masked")
        s_pc = sem("compressed_probs")
        s_pcp = sem("compressed_probs_turned")
        s_pcT = sem("compressed_probs_ready")
        s_oc = sem("compressed_out")
        s_cu = sem("conv_taps_ready")
        s_cv = sem("conv_in_psum")
        s_yc = sem("conv_out")
        s_mv = sem("gmlp_variance")
        s_grs = sem("gmlp_scale")
        s_gv = sem("gmlp_v_ready")
        s_sv = sem("gmlp_mixed")
        s_sp = sem("scores_in_psum")
        s_mx = sem("row_max_ready")
        s_e = sem("probs_ready")
        s_tp = sem("probs_turned")
        s_tc = sem("probs_turned_out")
        s_ov = sem("attention_unit_done")
        s_y = sem("groups_done")
        s_wo = sem("output_in_psum")
        s_sg = sem("silu_ready")
        s_hid = sem("hidden_ready")
        s_hT = sem("hidden_turned")
        s_hTh = sem("hidden_turned_high")
        s_hTl = sem("hidden_turned_low")
        s_lp = sem("logits_in_psum")
        s_lm = sem("logit_gap_ready")
        s_le = sem("logit_gap_exp")
        s_sel = sem("selection_ready")
        s_over = sem("crowded_experts_known")
        s_rk = sem("ranks_in_psum")
        s_gm = sem("slot_matrices_ready")
        s_col = sem("expert_columns")
        s_xep = sem("expert_rows_in_psum")
        s_xe = sem("expert_rows_ready")
        s_ggp = sem("gate_matrix_turned")
        s_ggT = sem("gate_matrix_ready")
        s_ye = sem("expert_out_ready")
        s_ysp = sem("expert_scattered")
        s_yadd = sem("expert_add_done")
        s_ysa = sem("expert_added")
        s_out = sem("output_stored")

        def columns(name, i):
            c = row_at[name] + i
            return cols[:, c:c + 1]

        def ring_ready(eng, q):
            eng.wait_ge(loaded[q % RING], 16 * (q // RING + 1))

        def half_chunk(q, hh, n):
            return wtile[q % RING].rearrange("p (k n) -> p k n", k=KT)[:, KT // 2 * hh:KT // 2 * (hh + 1), 0:n]

        def half_part(part, i, n):
            return part[:, i % 2, :].rearrange("p (k n) -> p k n", k=KT // 2)[:, :, 0:n]

        def piece_ready(eng, f, j):
            eng.wait_ge(landed[j % (2 * RING)], f * (16 * PIECES // (2 * RING)) + 16 * (j // (2 * RING) + 1))

        def past(eng, signal, value):
            if not (isinstance(value, int) and value <= 0):
                eng.wait_ge(signal, value)

        wtile = [ring[:, s, :] for s in range(RING)]
        piece_in = [ring[:, j // 2, (j % 2) * (KT * W // 2):(j % 2 + 1) * (KT * W // 2)] for j in range(2 * RING)]

        def split_schedule(split, silu, product, turned_out, others):
            for j in range(PIECES + 1):
                if j - PARTS >= 0:
                    part, n, hh = ORDER[j - PARTS]
                    if (part, hh) == (0, 0) and n:
                        turned_out(n - 1)
                    if silu and (part, hh) == (0, 1):
                        silu(n)
                    if product and (part, hh) == (1, 1):
                        product(n)
                if j in others:
                    others[j]()
                if j < PIECES:
                    split(j)
            turned_out(FS - 1)

        AHEAD = ((0, 1), (2,))

        def unless_ahead(eng, f, split):
            def split_rest(j):
                if isinstance(f, int):
                    if j not in AHEAD[0]:
                        split(j)
                    return
                for group in AHEAD:
                    if j == group[0]:
                        with eng.If(f > 1):
                            for jj in group:
                                split(jj)
                    if j in group:
                        return
                split(j)
            return split_rest

        YE_AT = 2
        SCATTER_AFTER = 1
        ADD_AT = 4
        SLOTS_AT = 12
        GATHER_AFTER = 23
        ROWS_AT = PIECES - 1

        row_loads = []
        small_loads = []

        def row(name, n, src):
            row_loads.append((vrows[row_at[name]:row_at[name] + n, :], src))

        def small(dst, src):
            small_loads.append((dst, src))

        row("attn", L * KT, attn_norm.rearrange("l (k p) -> (l k) p", p=P))
        row("ffn", L * KT, ffn_norm.rearrange("l (k p) -> (l k) p", p=P))
        row("q", L * QR // P, mla_q_norm.rearrange("l (k p) -> (l k) p", p=P))
        row("kv", L * KVR // P, mla_kv_norm.rearrange("l (k p) -> (l k) p", p=P))
        row("group", L * KT, group_norm.rearrange("l g (k p) -> (l g k) p", p=P))
        row("bs", L * 4, gmlp_b_s.rearrange("l g p -> (l g) p"))
        row("pe_k", L * 16, nsa_pe_k.rearrange("l (a b) d -> (l a) (b d)", b=2))
        row("pe_v", L * 16, nsa_pe_v.rearrange("l (a b) d -> (l a) (b d)", b=2))
        for b in range(NB):
            small(pos_i[:, b:b + 1], positions[0, b * P:(b + 1) * P].rearrange("(p o) -> p o", o=1))
        small(inv[:, :], rope_inv.to_broadcast([P, HALF]))
        small(ws_raw[:, :, :], gmlp_w_s.rearrange("l g i j -> i (l g) j"))
        for l in range(L):
            small(ln_row[:, l, :], gmlp_ln[l:l + 1, :].to_broadcast([P, GW]))
            small(cw_row[:, l, :], conv_w[l:l + 1].rearrange("l k c -> l (k c)").to_broadcast([P, 3 * GW]))
            small(w_uq[:, l, :, :], mla_w_uq[l].rearrange("(k p) n -> p k n", p=P))
            small(w_ukv[:, l, :], mla_w_ukv[l])
            small(w2[:, l, 0, :, :], nsa_w2_k[l].rearrange("(k p) n -> p k n", p=P))
            small(w2[:, l, 1, :, :], nsa_w2_v[l].rearrange("(k p) n -> p k n", p=P))
        small(w_r[:, :, :], moe_router[0].rearrange("(k p) e -> p k e", p=P))
        small(fin_row[:, :], final_norm.rearrange("(o n) -> o n", o=1).to_broadcast([P, D]))
        SMALL = 16 * len(small_loads)

        UNITS = [(kind, b, hs) for kind in range(3) for b, hs in ((0, (0, 1, 2, 3)), (1, (0, 1)), (1, (2, 3)))]
        NU = len(UNITS)
        TURN_BANK = (3, 2, 3, 3)
        WO_BANK = ((7, 0), (1, 2))
        XB = KT // 2

        block = ctx.enter_context(nc.Block())

        @block.sync
        def _(sp):
            def reader(q):
                l, j = divmod(q, MIX)
                if j < NIN:
                    return s_inl, 2 * NIN * l + 2 * (j + 1)
                if j < NIN + 2:
                    return s_hp, 2 * l + j - NIN + 1
                return s_wo, 4 * l + 3 + (j - NIN - 2)

            def load(q, dst, src):
                l, j = divmod(q, MIX)
                if j >= RING:
                    sp.wait_ge(*reader(q - RING))
                elif l:
                    sp.wait_ge(s_hi, PIECES - 2 * RING + 2 * (j + 1))
                    sp.wait_ge(s_lo, PIECES - 2 * RING + 2 * (j + 1))
                sp.dma_start(dst, src).then_inc(loaded[q % RING], 16)

            def tiled(q):
                return wtile[q % RING].rearrange("p (k n) -> p k n", k=KT)

            def load_mixer(l):
                q = chunk_mix[l]
                for j, (c, n) in enumerate(IN_CHUNKS):
                    if l == 0 and j == 1:
                        sp.wait_ge(s_rows, 16 * len(row_loads))
                    if l == 0 and j == RING:
                        for dst, src in small_loads:
                            sp.dma_start(dst, src).then_inc(s_small, 16)
                    src = w_in[l, :, c:c + n].rearrange("(k p) n -> p k n", p=P)
                    if q == 0:
                        sp.dma_start(half_chunk(0, 0, n), src[:, 0:KT // 2, :]).then_inc(s_first, 16)
                        sp.dma_start(half_chunk(0, 1, n), src[:, KT // 2:, :]).then_inc(loaded[0], 16)
                    else:
                        load(q, tiled(q)[:, :, 0:n], src)
                    q += 1
                for w1 in (nsa_w1_k, nsa_w1_v):
                    load(q, wtile[q % RING].rearrange("p (k n) -> p k n", k=16),
                         w1[l].rearrange("(k p) n -> p k n", p=P))
                    q += 1
                for c in range(0, D, W):
                    load(q, tiled(q), w_o[l, :, c:c + W].rearrange("(k p) n -> p k n", p=P))
                    q += 1

            def load_ffn(f, l, wg, wu, wd):
                for j, (part, n, hh) in enumerate(ORDER):
                    if j < 2 * RING:
                        sp.wait_ge(*reader(MIX * (l + 1) - RING + j // 2))
                    past(sp, s_hi, f * PIECES + (j - 2 * RING + 1))
                    past(sp, s_lo, f * PIECES + (j - 2 * RING + 1))
                    if part < 2:
                        src = (wg, wu)[part][hh * D // 2:(hh + 1) * D // 2, n * W:(n + 1) * W]
                        k = KT // 2
                    else:
                        src = wd[n * W + hh * W // 2:n * W + (hh + 1) * W // 2, :]
                        k = 2
                    sp.dma_start(piece_in[j % (2 * RING)].rearrange("p (k n) -> p k n", k=k),
                                 src.rearrange("(k p) n -> p k n", p=P)).then_inc(landed[j % (2 * RING)], 16)

            def load_moe(e, f):
                load_ffn(f, L - 1, *(w[0, bass.ds(e, 1), :, :].rearrange("o k n -> (o k) n")
                                     for w in (moe_w_gate, moe_w_up, moe_w_down)))

            for b in range(NB):
                sp.dma_start(h[:, b, :], x[0, b * P:(b + 1) * P, :]).then_inc(s_x, 16)
            sp.wait_ge(s_vz, 1)
            for dst, src in row_loads[1::2]:
                sp.dma_start(dst, src).then_inc(s_rows, 16)
            load_mixer(0)
            load_ffn(0, 0, dense_w_gate[0], dense_w_up[0], dense_w_down[0])
            load_mixer(1)
            with sp.Fori(0, E) as e:
                load_moe(e, e + 1)
            sp.wait_ge(s_over, 1)
            n_over = sp.value_load(over_i[0:1, 0:1], min_val=0, max_val=MAX_OVER)
            with sp.Fori(0, MAX_OVER) as i:
                with sp.If(n_over > i):
                    e = sp.value_load(over_i[0:1, bass.ds(i + 1, 1)], min_val=0, max_val=E - 1)
                    load_moe(e, i + (E + 1))
            for b in range(NB):
                sp.wait_ge(s_y, 2 * L + b + 1)
                sp.dma_start(out[0, b * P:(b + 1) * P, :], xs[:, b, :]).then_inc(s_out, 16)
            sp.wait_ge(s_out, 16 * NB)

        @block.gpsimd
        def _(pool):
            pc_n = [0]

            def link(ins):
                pc_n[0] += 1
                ins.then_inc(s_pchain, 1)
                pool.wait_ge(s_pchain, pc_n[0])

            pool.memset(vrows[:, :], 0.0).then_inc(s_vz, 1)
            for t, v in ((ident, 0.0), (amask, 0.0), (tri, 1.0), (ones, 1.0), (neghalf, -0.5), (hidR, 0.0),
                         (vcd, 0.0), (pc, 0.0), (shift, 0.0), (carry, 0.0), (cmask, 0.0), (cvalid, 1.0),
                         (cnt, 0.0)):
                ap = t[tuple(slice(None) for _ in t.shape)]
                last = pool.memset(ap, v)
            last.then_inc(s_zero, 1)
            pool.wait_ge(s_zero, 1)
            link(pool.iota(iota_i[:, :], [[1, P]], base=0, channel_multiplier=0))
            link(pool.affine_select(out=ident[:, :], in_=ident[:, :], compare_op=ALU.not_equal, fill=1.0,
                                    base=0, pattern=[[-1, P]], channel_multiplier=1))
            link(pool.affine_select(out=amask[:, :], in_=amask[:, :], compare_op=ALU.is_ge, fill=NEG,
                                    base=0, pattern=[[-1, P]], channel_multiplier=1))
            link(pool.affine_select(out=tri[:, :], in_=tri[:, :], compare_op=ALU.is_gt, fill=0.0,
                                    base=0, pattern=[[1, P]], channel_multiplier=-1))
            for s in (1, 2):
                link(pool.affine_select(out=shift[:, s - 1, :], in_=shift[:, s - 1, :], compare_op=ALU.not_equal,
                                        fill=1.0, base=s, pattern=[[-1, P]], channel_multiplier=1))
                link(pool.affine_select(out=carry[:, s - 1, :], in_=carry[:, s - 1, :], compare_op=ALU.not_equal,
                                        fill=1.0, base=s - P, pattern=[[-1, P]], channel_multiplier=1))
            for b in range(NB):
                link(pool.affine_select(out=cmask[:, b, :], in_=cmask[:, b, :], compare_op=ALU.is_ge, fill=NEG,
                                        base=b * P - (CMP_LEN - 1), pattern=[[-CMP_STRIDE, 16]],
                                        channel_multiplier=1))
                link(pool.affine_select(out=cvalid[:, b:b + 1], in_=cvalid[:, b:b + 1], compare_op=ALU.is_ge,
                                        fill=0.0, base=b * P - (CMP_LEN - 1), pattern=[[0, 1]],
                                        channel_multiplier=1))
            pool.tensor_copy(iota_s[:, :], iota_i[:, :]).then_inc(s_const, 1)

            def root(src, dst, n, signal):
                link(pool.tensor_scalar(src, src, EPS, None, ALU.add))
                pool.tensor_tensor(dst, src, neghalf[:, 0:n], ALU.pow).then_inc(signal, 1)

            for l in range(L):
                pool.wait_ge(s_ms, l + 1)
                root(ms[:, 0:NB], rs[:, 0:NB], NB, s_rs)
                pool.wait_ge(s_cms, l + 1)
                root(ms[:, 2:2 + 2 * NB], rs[:, 2:2 + 2 * NB], 2 * NB, s_crs)
                if l == 0:
                    pool.wait_ge(s_wsc, 1)
                    pool.affine_select(out=wsT[:, :, :], in_=wsT[:, :, :], compare_op=ALU.is_ge, fill=0.0,
                                       base=0, pattern=[[0, L * 4], [1, P]],
                                       channel_multiplier=-1).then_inc(s_ws, 1)
                pool.wait_ge(s_mv, l + 1)
                root(mv[:, :, 1], rs[:, 6:6 + NB], NB, s_grs)
                pool.wait_ge(s_gms, 2 * l + 1)
                root(ms[:, 8:8 + 3 * NB], rs[:, 8:8 + 3 * NB], 3 * NB, s_gsc)
                pool.wait_ge(s_gms, 2 * l + 2)
                root(ms[:, 8 + 3 * NB:8 + 4 * NB], rs[:, 8 + 3 * NB:8 + 4 * NB], NB, s_gsc)
                for b in range(NB):
                    pool.wait_ge(s_hms, NB * l + b + 1)
                    root(ms[:, b:b + 1], rs[:, b:b + 1], 1, s_hrs)
            pool.wait_ge(s_ms, L + 1)
            root(ms[:, 0:NB], rs[:, 0:NB], NB, s_rs)

        @block.tensor
        def _(pe):
            def mm(o, lhsT, rhs, start, stop):
                return nc.tensor.matmul(o, lhsT, rhs, start=start, stop=stop)

            def turn(o, src, n=P):
                return nc.tensor.transpose(o, src, ident[0:n, 0:n])

            def turn_rows(t):
                pe.wait_ge(s_xs, 2 * (t // 3) + (1 if t % 3 == 0 else 2))
                for k in range(KT):
                    for b in range(NB):
                        i = turn(bank[k // 2][:, (k % 2) * SEQ + b * P:(k % 2) * SEQ + (b + 1) * P],
                                 xs[:, b, k * P:(k + 1) * P])
                    if k % 2:
                        i.then_inc(s_xp, 1)

            def turn_latents(l):
                pe.wait_ge(s_cn, l + 1)
                for k in range(3):
                    for b in range(NB):
                        i = turn(bank[2 + k // 2][:, (k % 2) * SEQ + b * P:(k % 2) * SEQ + (b + 1) * P],
                                 cn[:, b, k * P:(k + 1) * P])
                i.then_inc(s_cp, 1)
                if l == 0:
                    pe.wait_ge(s_small, SMALL)
                    for g in range(L * 4):
                        i = turn(bank[g // 4][:, (g % 4) * P:(g % 4 + 1) * P], ws_raw[:, g, :])
                    i.then_inc(s_wsp, 1)

            def conv(l):
                pe.wait_ge(s_cu, l + 1)
                if l == 0:
                    pe.wait_ge(s_wsc, 1)
                for b in range(NB):
                    o = bank[1][:, b * GW:(b + 1) * GW]
                    mm(o, ident[:, :], conv_k[:, 2, b, :], True, False)
                    for s in (1, 2):
                        last = mm(o, shift[:, s - 1, :], conv_k[:, 2 - s, b, :], False, b == 0 and s == 2)
                    if b:
                        for s in (1, 2):
                            last = mm(o, carry[:, s - 1, :], conv_k[:, 2 - s, b - 1, :], False, s == 2)
                last.then_inc(s_cv, 1)

            def product3(o, xh_, xl_, wh_, wl_, first, last):
                mm(o, xh_, wh_, first, False)
                mm(o, xh_, wl_, False, False)
                return mm(o, xl_, wh_, False, last)

            def project(l):
                for j, (c, n) in enumerate(IN_CHUNKS):
                    if j == NIN - 2:
                        turn_latents(l)
                    if j == NIN - 1:
                        conv(l)
                    for hh in range(2):
                        p = 2 * j + hh
                        if j == 0:
                            pe.wait_ge(s_pxl, 2 * l + hh + 1)
                        pe.wait_ge(s_inl, 2 * NIN * l + p + 1)
                        wh, wl = half_part(in_h, p, n), half_part(in_l, p, n)
                        for b in range(NB):
                            m = NB * j + b
                            if m >= 4 and hh == 0:
                                done = NIN * l + (m - 4) // 2 + 1
                                pe.wait_ge(s_pea if m % 2 == 0 else s_pev, done)
                            for k in range(KT // 2):
                                kk_ = KT // 2 * hh + k
                                i = product3(bank[4 + m % 4][:, 0:n], pxh[:, kk_, b * P:(b + 1) * P],
                                             pxl[:, kk_, b * P:(b + 1) * P], wh[:, k, :], wl[:, k, :],
                                             kk_ == 0, kk_ == KT - 1)
                            if hh:
                                i.then_inc(s_pp, 1)
                            elif b == NB - 1:
                                i.then_inc(s_inu, 1)

            def turn_mla(l):
                pe.wait_ge(s_rope, l + 1)
                pe.wait_ge(s_qa, l + 1)
                for hd in range(HEADS):
                    for b in range(NB):
                        cs = slice((hd % 2) * SEQ + b * P, (hd % 2) * SEQ + (b + 1) * P)
                        turn(bank[2 * (hd // 2)][0:QK, cs], q5[:, b, hd, :])
                        i = turn(bank[6 + hd // 2][0:QK, cs], kk[:, b, hd, :])
                i.then_inc(s_qTp, 1)

            def mix(l):
                pe.wait_ge(s_cT, l + 1)
                pe.wait_ge(s_pev, NIN * l + NIN - 1)
                for b in range(NB):
                    for k in range(QR // P):
                        mm(bank[2 * b][:, 0:HEADS * QK], cT[:, k, b * P:(b + 1) * P], w_uq[:, l, k, :],
                           k == 0, k == QR // P - 1)
                mm(bank[3][:, :], cT[:, 2, 0:P], w_ukv[:, l, :], True, True)
                mm(bank[7][:, :], cT[:, 2, P:2 * P], w_ukv[:, l, :], True, True).then_inc(s_qp, 1)
                out_a = NIN * (l + 1)
                pe.wait_ge(s_pea, out_a)
                pe.wait_ge(s_pev, out_a)
                for hd in range(HEADS):
                    for b in range(NB):
                        turn(bank[4 + hd // 2][0:DH, (hd % 2) * SEQ + b * P:(hd % 2) * SEQ + (b + 1) * P],
                             proj[:, b, NQ + hd * DH:NQ + (hd + 1) * DH])
                for j, c in enumerate((NKS, NKW)):
                    for b in range(NB):
                        i = turn(bank[6][0:DH, j * SEQ + b * P:j * SEQ + (b + 1) * P], proj[:, b, c:c + DH])
                i.then_inc(s_nTp, 1)
                pe.wait_ge(s_yc, l + 1)
                for j, c in enumerate((NKC, NVC)):
                    for odd in range(2):
                        for b in range(NB):
                            i = mm(bank[1][odd * DH:(odd + 1) * DH, j * P + b * DH:j * P + (b + 1) * DH],
                                   proj[:, b, c:c + DH], ident[:, odd::2], True, True)
                i.then_inc(s_zp, 1)
                pe.wait_ge(s_gv, l + 1)
                pe.wait_ge(s_nT, l + 1)
                if l == 0:
                    pe.wait_ge(s_ws, 1)
                for b in range(NB):
                    for g in range(4):
                        c = GW + g * DH
                        i = mm(bank[5][:, b * GW + g * DH:b * GW + (g + 1) * DH], wsT[:, l * 4 + g, :],
                               gel[:, b, c:c + DH], True, True)
                i.then_inc(s_sv, 1)
                pe.wait_ge(s_blk, l + 1)
                for j in range(2):
                    q = chunk_mix[l] + NIN + j
                    ring_ready(pe, q)
                    w = wtile[q % RING].rearrange("p (k n) -> p k n", k=16)
                    for k in range(16):
                        i = mm(bank[1][0:NC, j * CH:(j + 1) * CH], blk[:, j, k // 8, :, k % 8], w[:, k, :],
                               k == 0, k == 15)
                    i.then_inc(s_hp, 1)
                    if j == 0:
                        turn_mla(l)
                pe.wait_ge(s_hg, l + 1)
                for j in range(2):
                    for t in range(CH // P):
                        i = turn(bank[1][:, j * 32 + t * 16:j * 32 + t * 16 + NC],
                                 conv_u[0:NC, j, t * P:(t + 1) * P], NC)
                i.then_inc(s_hc, 1)
                pe.wait_ge(s_hr, l + 1)
                for t in range(CH // P):
                    mm(bank[3][0:DH, 0:NC], w2[:, l, 0, t, :], hidT[:, t, 0:NC], t == 0, t == CH // P - 1)
                for t in range(CH // P):
                    i = mm(bank[3][:, 64:64 + DH], hidR[:, t, :, :].rearrange("p h c -> p (h c)"),
                           w2[:, l, 1, t, :], t == 0, t == CH // P - 1)
                i.then_inc(s_kcp, 1)
                pe.wait_ge(s_kc, l + 1)
                for b in range(NB):
                    for hd in range(HEADS):
                        c = (b * HEADS + hd) * 16
                        i = mm(bank[4][:, c:c + NC], nqT[0:DH, hd, b * P:(b + 1) * P], kcT[0:DH, 0:NC], True, True)
                i.then_inc(s_scp, 1)
                pe.wait_ge(s_qT, l + 1)

            def scores(l, n):
                kind, b, hs = UNITS[n]
                m = l * NU + n
                if n < 2:
                    pe.wait_ge(s_qT, l + 1)
                    pe.wait_ge(s_mr, l + 1)
                else:
                    pe.wait_ge(s_e, m - 1)
                width = (b + 1) * P
                mask = mask_r[:, 2 - b:3, :].rearrange("p (o b) k -> p o (b k)", o=1)
                mm(bank[n % 2][:, :].rearrange("p (h k) -> p h k", k=width), mask_r[:, 0, :],
                   mask.to_broadcast([P, len(hs), width]), True, False)
                for j, hd in enumerate(hs):
                    c = j * width
                    if kind == 0:
                        q_, k_ = qT[0:QK, hd, b * P:(b + 1) * P], kT[0:QK, hd, 0:width]
                    else:
                        q_, k_ = nqT[0:DH, hd, b * P:(b + 1) * P], nkT[0:DH, kind - 1, 0:width]
                    i = mm(bank[n % 2][:, c:c + width], q_, k_, False, j == len(hs) - 1)
                i.then_inc(s_sp, 1)

            def turn_probs(l, n):
                m = l * NU + n
                pe.wait_ge(s_e, m + 1)
                if n >= 2:
                    pe.wait_ge(s_tc, m - 1)
                for j in range(4):
                    i = turn(bank[2 + n % 2][:, j * P:(j + 1) * P], prob[:, n % 2, j * P:(j + 1) * P])
                i.then_inc(s_tp, 1)

            OUT_BANK = (7, 4, 5)

            def values(l, n):
                kind, b, hs = UNITS[n]
                pe.wait_ge(s_tc, l * NU + n + 1)
                for j, hd in enumerate(hs):
                    o = bank[OUT_BANK[kind]][:, b * GW + hd * DH:b * GW + (hd + 1) * DH]
                    for kb in range(b + 1):
                        v = (vv[:, kb, hd, :] if kind == 0
                             else proj[:, kb, (NVS, NVW)[kind - 1]:(NVS, NVW)[kind - 1] + DH])
                        c = (j * (b + 1) + kb) * P
                        i = mm(o, probT[:, n % 2, c:c + P], v, kb == 0, kb == b)
                i.then_inc(s_ov, 1)

            def attend(l):
                scores(l, 0)
                pe.wait_ge(s_pc, l + 1)
                for b in range(NB):
                    i = turn(bank[3][:, 128 + b * P:128 + (b + 1) * P],
                             pc[:, b, :, :].rearrange("p h c -> p (h c)"))
                i.then_inc(s_pcp, 1)
                scores(l, 1)
                pe.wait_ge(s_pcT, l + 1)
                for b in range(NB):
                    i = mm(bank[6][:, b * GW:(b + 1) * GW], pcT[:, b, :], vcd[:, :], True, True)
                i.then_inc(s_oc, 1)
                for n in range(NU):
                    turn_probs(l, n)
                    if n + 2 < NU:
                        scores(l, n + 2)
                    if n == NU - 1:
                        turn_group(l, 0)
                    values(l, n)

            def turn_group(l, g):
                pe.wait_ge(s_gxs, 2 * l + (2 if g == 3 else 1))
                if g == 0:
                    pe.wait_ge(s_tc, NU * (l + 1) - 1)
                elif g == 1:
                    pe.wait_ge(s_tc, NU * (l + 1))
                else:
                    pe.wait_ge(s_xTa, 4 * (3 * l + 1) + (2 if g == 2 else 4))
                for k in (2 * g, 2 * g + 1):
                    for b in range(NB):
                        i = turn(bank[TURN_BANK[g]][:, (k % 2) * SEQ + b * P:(k % 2) * SEQ + (b + 1) * P],
                                 xs[:, b, k * P:(k + 1) * P])
                i.then_inc(s_xp, 1)

            def output(l):
                turn_group(l, 1)
                turn_group(l, 2)
                t = 4 * (3 * l + 1)
                tiles = []
                for j in range(2):
                    q = chunk_mix[l] + NIN + 2 + j
                    ring_ready(pe, q)
                    tiles.append(wtile[q % RING].rearrange("p (k n) -> p k n", k=KT))
                pe.wait_ge(s_xTa, t + 4)
                pe.wait_ge(s_xTv, t + 2)
                for b in range(NB):
                    for j in range(2):
                        for k in range(KT - 2):
                            mm(bank[WO_BANK[b][j]][:, :], xT[:, k, b * P:(b + 1) * P], tiles[j][:, k, :],
                               k == 0, False)
                turn_group(l, 3)
                pe.wait_ge(s_xTv, t + 4)
                for b in range(NB):
                    for j in range(2):
                        for k in (KT - 2, KT - 1):
                            i = mm(bank[WO_BANK[b][j]][:, :], xT[:, k, b * P:(b + 1) * P], tiles[j][:, k, :],
                                   False, k == KT - 1)
                        i.then_inc(s_wo, 1)

            def ffn(f, blocks, others={}):

                def turn_hidden(n):
                    pe.wait_ge(s_hid, f * FS + (n + 1))
                    for b in range(blocks):
                        for k in range(4):
                            last = turn(bank[2 + b if blocks == 2 else 1][:, k * P:(k + 1) * P], hid[:, b, k * P:(k + 1) * P])
                    last.then_inc(s_hT, 1)

                def piece(j):
                    part, n, hh = ORDER[j]
                    pe.wait_ge(s_lo, f * PIECES + (j + 1))
                    wh, wl = part_h[:, j % PARTS, :], part_l[:, j % PARTS, :]
                    if part < 2:
                        if blocks == 2 and j < 2:
                            pe.wait_ge(s_xl, j + 1)
                        if (part, hh) == (0, 0):
                            past(pe, s_sg, f * FS + n)
                        if (part, hh) == (1, 0):
                            past(pe, s_hid, f * FS + n)
                            if blocks == 2:
                                past(pe, s_hTl, f * FS + n)
                        for b in range(blocks):
                            for k in range(4):
                                ks, xs_ = slice(k * W, (k + 1) * W), slice(b * P, (b + 1) * P)
                                last = product3(bank[2 * part + b][:, :], xh[:, 4 * hh + k, xs_],
                                                xl[:, 4 * hh + k, xs_], wh[:, ks], wl[:, ks],
                                                hh == 0 and k == 0, hh == 1 and k == 3)
                    else:
                        if hh == 0:
                            pe.wait_ge(s_hTl, f * FS + (n + 1))
                        if hh == 0 and n == 0 and blocks == 1:
                            pe.wait_ge(s_ysa, f)
                        for b in range(blocks):
                            for k in range(2):
                                for side in range(2):
                                    ks = slice(k * D + side * W, k * D + (side + 1) * W)
                                    xs_ = slice((2 * hh + k) * P, (2 * hh + k + 1) * P)
                                    last = product3(bank[4 + 2 * b + side][:, :], hTh[:, b, xs_], hTl[:, b, xs_],
                                                    wh[:, ks], wl[:, ks], n == 0 and hh == 0 and k == 0,
                                                    n == FS - 1 and hh == 1 and k == 1)
                    last.then_inc(s_used, 1)

                for j in range(PIECES - 2):
                    piece(j)
                    if j in others:
                        others[j]()
                    part, n, hh = ORDER[j]
                    if (part, hh) == (0, 0) and n:
                        turn_hidden(n - 1)
                turn_hidden(FS - 1)

                piece(PIECES - 2)
                piece(PIECES - 1)

            def gather(n):
                pe.wait_ge(s_gm, n + 1)
                for k in range(KT):
                    for b in range(NB):
                        last = mm(bank[6 + k // 4][:, (k % 4) * P:(k % 4 + 1) * P], xs[:, b, k * P:(k + 1) * P],
                                  gm[:, b, :], b == 0, b == NB - 1)
                last.then_inc(s_xep, 1)

            def turn_gates(n):
                for b in range(NB):
                    last = turn(bank[3][:, b * P:(b + 1) * P], gg[:, b, :])
                last.then_inc(s_ggp, 1)

            pe.wait_ge(s_const, 1)
            pe.wait_ge(s_rows, 16 * len(row_loads))
            turn(bank[7][:, 0:P], vrows[:, :]).then_inc(s_rt, 1)
            for l in range(L):
                turn_rows(3 * l)
                if l == 0:
                    pe.wait_ge(s_cols, 1)
                else:
                    pe.wait_ge(s_h, 2)
                project(l)
                mix(l)
                attend(l)
                output(l)
                turn_rows(3 * l + 2)
                pe.wait_ge(s_h, 2 * l + 1)
                if l:
                    pe.wait_ge(s_xTa, 4 * (3 * l + 2) + 4)
                    pe.wait_ge(s_xTv, 4 * (3 * l + 2) + 4)
                else:
                    ffn(0, 2)
            for b in range(NB):
                for k in range(KT):
                    i = mm(bank[0][:, b * E:(b + 1) * E], xT[:, k, b * P:(b + 1) * P], w_r[:, k, :],
                           k == 0, k == KT - 1)
            i.then_inc(s_lp, 1)
            pe.wait_ge(s_sel, 1)
            mm(bank[1][:, 0:E], tri[:, :], rsg[:, 1, 0, :], True, True)
            mm(bank[1][:, E:2 * E], tri[:, :], rsg[:, 1, 1, :], True, False)
            mm(bank[1][:, E:2 * E], ones[:, :], rsg[:, 1, 0, :], False, True)
            mm(bank[1][:, 2 * E:3 * E], ones[:, :], rsg[:, 1, 0, :], True, False)
            mm(bank[1][:, 2 * E:3 * E], ones[:, :], rsg[:, 1, 1, :], False, True).then_inc(s_rk, 1)

            def scatter(m):
                pe.wait_ge(s_ye, m + 1)
                for b in range(NB):
                    for half in range(2):
                        last = mm(bank[6 - 2 * b + half][:, :], ggT[:, b, :], ye[:, half * W:(half + 1) * W],
                                  True, True)
                last.then_inc(s_ysp, 1)

            gather(0)
            with pe.Fori(0, E) as e:
                def scatter_before():
                    pe.wait_ge(s_ggT, e + 1)
                    scatter(e)
                    turn_gates(e)

                pe.wait_ge(s_xl, e + 3)
                ffn(e + 1, 1, {SCATTER_AFTER: scatter_before, GATHER_AFTER: lambda: gather(e + 1)})
            pe.wait_ge(s_ggT, E + 1)
            scatter(E)
            pe.wait_ge(s_over, 1)
            n_over = pe.value_load(over_i[0:1, 0:1], min_val=0, max_val=MAX_OVER)
            with pe.Fori(0, MAX_OVER) as i:
                with pe.If(n_over > i):
                    n = i + (E + 1)
                    pe.wait_ge(s_xl, n + 2)
                    pe.wait_ge(s_ysa, n)
                    pe.wait_ge(s_ggT, n)
                    gather(n)
                    turn_gates(n)
                    pe.wait_ge(s_xl, n + 3)
                    pe.wait_ge(s_ggT, n + 1)
                    ffn(n, 1)
                    scatter(n)

        @block.scalar
        def _(act):
            act.wait_ge(s_vz, 1)
            for dst, src in row_loads[0::2]:
                act.dma_start(dst, src).then_inc(s_rows, 16)

            def copy(dst, src, scale=1.0):
                return nc.scalar.activation(dst, src, ACT.Copy, scale=scale)

            sq = [0]

            def square(src, scale, total):
                if sq[0]:
                    act.wait_ge(s_achain, sq[0])
                sq[0] += 1
                nc.scalar.activation(junk[:, 0:src.shape[-1]], src, ACT.Square, scale=scale,
                                     accum_out=total).then_inc(s_achain, 1)

            def squares_done(signal):
                act.wait_ge(s_achain, sq[0])
                act.sem_inc(signal, 1)

            def mean_squares(src, first):
                for b in range(NB):
                    square(src[:, b, :], D ** -0.5, ms[:, first + b:first + b + 1])
                squares_done(s_ms)

            def turned(t, name, first):
                for k in (0, 1, 4, 5):
                    act.wait_ge(s_xp, XB * t + k // 2 + 1)
                    copy(xT[:, k, :], bank[k // 2][:, (k % 2) * SEQ:(k % 2 + 1) * SEQ],
                         columns(name, first + k)).then_inc(s_xTa, 1)

            def split(f, j):
                piece_ready(act, f, j)
                past(act, s_used, f * PIECES + (j - PARTS + 1))
                copy(part_h[:, j % PARTS, :], piece_in[j % (2 * RING)]).then_inc(s_hi, 1)

            def in_high(l, p):
                j, hh = divmod(p, 2)
                q = chunk_mix[l] + j
                if l == 0 and p == 0:
                    act.wait_ge(s_first, 16)
                else:
                    ring_ready(act, q)
                if j and hh:
                    act.wait_ge(s_pp, NIN * NB * l + NB * j)
                elif j:
                    act.wait_ge(s_inu, NIN * l + j)
                elif l and not hh:
                    act.wait_ge(s_used, PIECES)
                n = IN_CHUNKS[j][1]
                copy(half_part(in_h, p, n), half_chunk(q, hh, n)).then_inc(s_inh, 1)

            def group_squares(g):
                for b in range(NB):
                    c = 8 + NB * g + b
                    square(y[:, b, g * GW:(g + 1) * GW], GW ** -0.5, ms[:, c:c + 1])

            def group_out(l, g):
                act.wait_ge(s_xp, XB * (3 * l + 1) + g + 1)
                for k in (2 * g, 2 * g + 1):
                    copy(xT[:, k, :], bank[3][:, (k % 2) * SEQ:(k % 2 + 1) * SEQ],
                         columns("group", KT * l + k)).then_inc(s_xTa, 1)

            act.wait_ge(s_x, 16 * NB)
            mean_squares(h, 0)
            act.wait_ge(s_rt, 1)
            copy(cols[:, :], bank[7][:, 0:P]).then_inc(s_cols, 1)
            act.wait_ge(s_cols, 1)

            for l in range(L):
                in_high(l, 0)
                if l:
                    for b in range(NB):
                        act.wait_ge(s_hd, b + 1)
                        square(h[:, b, :], D ** -0.5, ms[:, b:b + 1])
                    squares_done(s_ms)
                    in_high(l, 1)
                for k in range(KT):
                    if k % 2 == 0:
                        act.wait_ge(s_xp, XB * 3 * l + k // 2 + 1)
                    copy(pxh[:, k, :], bank[k // 2][:, (k % 2) * SEQ:(k % 2 + 1) * SEQ],
                         columns("attn", KT * l + k)).then_inc(s_pxh if k % 2 else s_xTa, 1)
                    if k == 3 and l == 0:
                        in_high(l, 1)
                for j, (c, n) in enumerate(IN_CHUNKS):
                    if j + 1 < NIN:
                        in_high(l, 2 * j + 2)
                    act.wait_ge(s_pp, NIN * NB * l + NB * j + 1)
                    copy(proj[:, 0, c:c + n], bank[4 + (NB * j) % 4][:, 0:n]).then_inc(s_pea, 1)
                    if j + 1 < NIN:
                        in_high(l, 2 * j + 3)
                    if j == 0:
                        act.wait_ge(s_pea, NIN * l + 1)
                        act.wait_ge(s_pev, NIN * l + 1)
                        for b in range(NB):
                            square(proj[:, b, CQ:CQ + QR], QR ** -0.5, ms[:, 2 + b:3 + b])
                            square(proj[:, b, CKV:CKV + KVR], KVR ** -0.5, ms[:, 4 + b:5 + b])
                        squares_done(s_cms)
                    if j == NIN - 3:
                        act.wait_ge(s_cp, l + 1)
                        for k in range(2):
                            copy(cT[:, k, :], bank[2][:, k * SEQ:(k + 1) * SEQ], columns("q", 2 * l + k))
                        copy(cT[:, 2, :], bank[3][:, 0:SEQ], columns("kv", l)).then_inc(s_cT, 1)
                        if l == 0:
                            act.wait_ge(s_wsp, 1)
                            copy(wsT[:, 0:4, :].rearrange("p g j -> p (g j)"), bank[0][:, :])
                            copy(wsT[:, 4:8, :].rearrange("p g j -> p (g j)"), bank[1][:, :]).then_inc(s_wsc, 1)
                    if j == NIN - 2:
                        act.wait_ge(s_pea, NIN * l + NIN - 1)
                        act.wait_ge(s_pev, NIN * l + NIN - 1)
                        nc.scalar.activation(gel[:, :, :], proj[:, :, GU:GU + 2 * GW],
                                             ACT.Gelu_apprx_tanh).then_inc(s_gel, 1)
                        if l == 0:
                            act.wait_ge(s_ang, 1)
                            nc.scalar.activation(sin_t[:, :, :], turns[:, :, :], ACT.Sin)
                            nc.scalar.activation(cos_t[:, :, :], ang[:, :, :], ACT.Sin).then_inc(s_sin, 1)
                act.wait_ge(s_qp, l + 1)
                for b in range(NB):
                    copy(q5[:, b, 0:HEADS, :], bank[2 * b][:, 0:HEADS * QK].rearrange("p (h d) -> p h d", h=HEADS))
                    kv = bank[(3, 7)[b]][:, :].rearrange("p (h d) -> p h d", h=HEADS)
                    copy(kk[:, b, :, 0:NOPE], kv[:, :, 0:NOPE])
                    copy(vv[:, b, :, :], kv[:, :, NOPE:])
                    i = copy(q5[:, b, HEADS, NOPE:QK], proj[:, b, KR:KR + ROPE])
                i.then_inc(s_qa, 1)
                copy(mask_r[:, 0, :], ident[:, :])
                copy(mask_r[:, 1, :], ident[:, :], 0.0)
                copy(mask_r[:, 2, :], amask[:, :]).then_inc(s_mr, 1)
                act.wait_ge(s_nTp, l + 1)
                for j in range(2):
                    copy(nqT[0:DH, 2 * j:2 * j + 2, :].rearrange("p h t -> p (h t)"), bank[4 + j][0:DH, :], DH ** -0.5)
                copy(nkT[0:DH, :, :].rearrange("p h t -> p (h t)"), bank[6][0:DH, :]).then_inc(s_nT, 1)
                act.wait_ge(s_qTp, l + 1)
                for j in range(2):
                    copy(qT[0:QK, 2 * j:2 * j + 2, :].rearrange("p h t -> p (h t)"), bank[2 * j][0:QK, :], QK ** -0.5)
                    i = copy(kT[0:QK, 2 * j:2 * j + 2, :].rearrange("p h t -> p (h t)"), bank[6 + j][0:QK, :])
                i.then_inc(s_qT, 1)
                act.wait_ge(s_yc, l + 1)
                act.wait_ge(s_yg, l + 1)
                group_squares(1)
                group_squares(2)
                act.wait_ge(s_pea, NIN * (l + 1))
                act.wait_ge(s_pev, NIN * (l + 1))
                act.wait_ge(s_hp, 2 * l + 2)
                nc.scalar.activation(conv_u[0:NC, :, :].rearrange("p b c -> p (b c)"), bank[1][0:NC, :],
                                     ACT.Gelu_apprx_tanh).then_inc(s_hg, 1)
                nc.scalar.activation(gexp[:, :, :], proj[:, :, NGL:END], ACT.Exp, scale=-1.0).then_inc(s_gex, 1)
                act.wait_ge(s_scm, l + 1)
                nc.scalar.activation(pc[:, :, :, 0:NC].rearrange("p b h c -> p (b h) c"), sc[:, :, 0:NC],
                                     ACT.Exp).then_inc(s_pc, 1)

                def turned_probs(n):
                    m = l * NU + n
                    act.wait_ge(s_tp, m + 1)
                    if n >= 2:
                        act.wait_ge(s_ov, m - 1)
                    copy(probT[:, n % 2, :], bank[2 + n % 2][:, :]).then_inc(s_tc, 1)

                for n, (kind, b, hs) in enumerate(UNITS):
                    m = l * NU + n
                    width = (b + 1) * P
                    act.wait_ge(s_mx, m + 1)
                    if n >= 2:
                        act.wait_ge(s_tp, m - 1)
                    for j, hd in enumerate(hs):
                        i = nc.scalar.activation(
                            prob[:, n % 2, j * width:(j + 1) * width], bank[n % 2][:, j * width:(j + 1) * width],
                            ACT.Exp, bias=nmax[:, n % 2, j:j + 1],
                            accum_out=psums[:, kind, b * HEADS + hd:b * HEADS + hd + 1])
                    i.then_inc(s_e, 1)
                    if n >= 1:
                        turned_probs(n - 1)
                    if n == 5:
                        act.wait_ge(s_ym, l + 1)
                        group_squares(0)
                        squares_done(s_gms)
                turned_probs(NU - 1)
                group_out(l, 0)
                group_out(l, 2)
                act.wait_ge(s_y, 2 * l + 1)
                group_squares(3)
                squares_done(s_gms)
                for j in AHEAD[0]:
                    split(l, j)
                for b in range(NB):
                    act.wait_ge(s_hb, NB * l + b + 1)
                    square(h[:, b, :], D ** -0.5, ms[:, b:b + 1])
                    squares_done(s_hms)
                if l:
                    turned(3 * l + 2, "ffn", KT * l)
                else:
                    for k in range(KT):
                        if k % 2 == 0:
                            act.wait_ge(s_xp, XB * 2 + k // 2 + 1)
                        copy(xh[:, k, :], bank[k // 2][:, (k % 2) * SEQ:(k % 2 + 1) * SEQ],
                             columns("ffn", k)).then_inc(s_xh if k % 2 else s_xTa, 1)

                    def ffn(f, blocks, others={}):
                        def silu(n):
                            act.wait_ge(s_used, f * PIECES + (AT[0, n, 1] + 1))
                            past(act, s_hid, f * FS + n)
                            for b in range(blocks):
                                i = nc.scalar.activation(sg[:, b, :], bank[b][:, :], ACT.Silu)
                            i.then_inc(s_sg, 1)

                        def turned_out(n):
                            act.wait_ge(s_hT, f * FS + (n + 1))
                            for b in range(blocks):
                                i = copy(hTh[:, b, :], bank[2 + b if blocks == 2 else 1][:, :])
                            i.then_inc(s_hTh, 1)

                        split_schedule(unless_ahead(act, f, lambda j: split(f, j)), silu, None, turned_out, others)

                    ffn(0, 2)
            for j in AHEAD[1]:
                split(1, j)
            act.wait_ge(s_lm, 1)
            nc.scalar.activation(gd[:, 1, :], gd[:, 0, :], ACT.Exp).then_inc(s_le, 1)

            def rows_from(m):
                act.wait_ge(s_used, (m + 1) * PIECES)
                copy(ye[:, 0:W], bank[4][:, :])
                copy(ye[:, W:], bank[5][:, :]).then_inc(s_ye, 1)

            def rows_out(n):
                act.wait_ge(s_xep, n + 1)
                for k in range(KT):
                    i = copy(xh[:, k, 0:P], bank[6 + k // 4][:, (k % 4) * P:(k % 4 + 1) * P],
                             columns("ffn", KT * (L - 1) + k))
                i.then_inc(s_xe, 1)

            def gates_out(n):
                act.wait_ge(s_ggp, n + 1)
                copy(ggT[:, :, :].rearrange("p b t -> p (b t)"), bank[3][:, 0:NB * P]).then_inc(s_ggT, 1)

            rows_out(0)
            with act.Fori(0, E) as e:
                ffn(e + 1, 1, {YE_AT: lambda: rows_from(e), ADD_AT: lambda: gates_out(e), ROWS_AT: lambda: rows_out(e + 1)})
            rows_from(E)
            act.wait_ge(s_over, 1)
            n_over = act.value_load(over_i[0:1, 0:1], min_val=0, max_val=MAX_OVER)
            with act.Fori(0, MAX_OVER) as i:
                with act.If(n_over > i):
                    rows_out(i + (E + 1))
                    gates_out(i + E)
                    ffn(i + (E + 1), 1)
                    rows_from(i + (E + 1))
            act.wait_ge(s_h, 2 * L)
            mean_squares(h, 0)

        @block.vector
        def _(dve):
            ch = [0]

            def link(ins):
                ch[0] += 1
                ins.then_inc(s_chain, 1)
                dve.wait_ge(s_chain, ch[0])

            def tt(o, a, b, op):
                return nc.vector.tensor_tensor(o, a, b, op)

            def ts(o, a, s1, s2, op0, op1=None):
                if op1 is None:
                    return nc.vector.tensor_scalar(o, a, s1, None, op0)
                return nc.vector.tensor_scalar(o, a, s1, s2, op0, op1)

            dve.wait_ge(s_const, 1)
            link(ts(w8[:, :], iota_s[:, 0:E], -1.0, float(E), ALU.mult, ALU.add))

            def scale_rows(src, t):
                if t % 3 == 0:
                    dve.wait_ge(s_rs, t // 3 + 1)
                if t:
                    dve.wait_ge(s_xp, XB * t)
                for b in range(NB):
                    if t % 3:
                        dve.wait_ge(s_hrs, NB * (t // 3) + b + 1)
                    i = ts(xs[:, b, :], src[:, b, :], rs[:, b:b + 1], None, ALU.mult)
                i.then_inc(s_xs, 1)

            def split(f, j):
                dve.wait_ge(s_hi, f * PIECES + (j + 1))
                tt(part_l[:, j % PARTS, :], piece_in[j % (2 * RING)], part_h[:, j % PARTS, :].bitcast(F32),
                   ALU.subtract).then_inc(s_lo, 1)

            def in_low(l, p):
                j, hh = divmod(p, 2)
                dve.wait_ge(s_inh, 2 * NIN * l + p + 1)
                n = IN_CHUNKS[j][1]
                tt(half_part(in_l, p, n), half_chunk(chunk_mix[l] + j, hh, n), half_part(in_h, p, n).bitcast(F32),
                   ALU.subtract).then_inc(s_inl, 1)

            def scale_group(g):
                for b in range(NB):
                    c = 8 + NB * g + b
                    i = ts(xs[:, b, g * GW:(g + 1) * GW], y[:, b, g * GW:(g + 1) * GW], rs[:, c:c + 1], None,
                           ALU.mult)
                return i

            def group_out(l, g, b):
                dve.wait_ge(s_xp, XB * (3 * l + 1) + g + 1)
                for k in (2 * g, 2 * g + 1):
                    ts(xT[:, k, :], bank[b][:, (k % 2) * SEQ:(k % 2 + 1) * SEQ], columns("group", KT * l + k), None,
                       ALU.mult).then_inc(s_xTv, 1)

            def turned(t, name, first):
                if t == 0:
                    dve.wait_ge(s_cols, 1)
                for k in (2, 3, 6, 7):
                    dve.wait_ge(s_xp, XB * t + k // 2 + 1)
                    ts(xT[:, k, :], bank[k // 2][:, (k % 2) * SEQ:(k % 2 + 1) * SEQ], columns(name, first + k), None,
                       ALU.mult).then_inc(s_xTv, 1)

            for l in range(L):
                if l:
                    in_low(l, 0)
                scale_rows(h, 3 * l)
                in_low(l, 0 if l == 0 else 1)
                if l == 0:
                    dve.wait_ge(s_cols, 1)
                for k in range(KT):
                    if k % 2 == 0:
                        dve.wait_ge(s_pxh, 4 * l + k // 2 + 1)
                    i = nc.vector.scalar_tensor_tensor(
                        out=pxl[:, k, :], in0=bank[k // 2][:, (k % 2) * SEQ:(k % 2 + 1) * SEQ],
                        scalar=columns("attn", KT * l + k), in1=pxh[:, k, :].bitcast(F32), op0=ALU.mult, op1=ALU.subtract)
                    if k % 4 == 3:
                        i.then_inc(s_pxl, 1)
                    elif k % 2 == 0:
                        i.then_inc(s_xTv, 1)
                    if k == 3 and l == 0:
                        in_low(l, 1)
                for j, (c, n) in enumerate(IN_CHUNKS):
                    if j + 1 < NIN:
                        in_low(l, 2 * j + 2)
                    dve.wait_ge(s_pp, NIN * NB * l + NB * j + 2)
                    nc.vector.tensor_copy(proj[:, 1, c:c + n], bank[4 + (NB * j + 1) % 4][:, 0:n]).then_inc(s_pev, 1)
                    if j + 1 < NIN:
                        in_low(l, 2 * j + 3)
                    if j == 1:
                        dve.wait_ge(s_crs, l + 1)
                        for b in range(NB):
                            ts(cn[:, b, 0:QR], proj[:, b, CQ:CQ + QR], rs[:, 2 + b:3 + b], None, ALU.mult)
                            i = ts(cn[:, b, QR:], proj[:, b, CKV:CKV + KVR], rs[:, 4 + b:5 + b], None, ALU.mult)
                        i.then_inc(s_cn, 1)
                    if j == NIN - 3:
                        dve.wait_ge(s_pea, NIN * l + j + 1)
                        dve.wait_ge(s_pev, NIN * l + j + 1)
                        if l == 0:
                            dve.wait_ge(s_small, SMALL)
                        link(tt(conv_u[:, :, :], proj[:, :, CC:CC + GW], proj[:, :, CHV:CHV + GW], ALU.mult))
                        for k in range(3):
                            w = cw_row[:, l:l + 1, k * GW:(k + 1) * GW].to_broadcast([P, NB, GW])
                            i = tt(conv_k[:, k, :, :], conv_u[:, :, :], w, ALU.mult)
                        i.then_inc(s_cu, 1)
                        if l == 0:
                            link(nc.vector.tensor_copy(pos_f[:, :], pos_i[:, :]))
                            for b in range(NB):
                                link(ts(ang[:, b, :], inv[:, :], pos_f[:, b:b + 1], None, ALU.mult))
                            link(ts(turns[:, :, :], ang[:, :, :], 0.15915494309189535, ROUND_MAGIC, ALU.mult, ALU.add))
                            link(ts(turns[:, :, :], turns[:, :, :], -ROUND_MAGIC, None, ALU.add))
                            for part in (TWO_PI_HI, TWO_PI_LO):
                                link(ts(sin_t[:, :, :], turns[:, :, :], part, None, ALU.mult))
                                link(tt(ang[:, :, :], ang[:, :, :], sin_t[:, :, :], ALU.subtract))
                            link(ts(turns[:, :, :], ang[:, :, :], PI_SAFE, -PI_SAFE, ALU.min, ALU.max))
                            link(ts(ang[:, :, :], ang[:, :, :], 1.5707963267948966, None, ALU.add))
                            link(ts(cos_t[:, :, :], ang[:, :, :], PI_SAFE, -6.283185307179586, ALU.is_gt, ALU.mult))
                            link(tt(ang[:, :, :], ang[:, :, :], cos_t[:, :, :], ALU.add))
                            ts(ang[:, :, :], ang[:, :, :], PI_SAFE, -PI_SAFE, ALU.min, ALU.max).then_inc(s_ang, 1)
                    if j == NIN - 2:
                        dve.wait_ge(s_gel, l + 1)
                        for b in range(NB):
                            link(nc.vector.bn_stats(bn[:, b, :], gel[:, b, GW:]))
                            i = nc.vector.bn_aggr(mv[:, b, :], bn[:, b, :])
                        i.then_inc(s_mv, 1)
                        dve.wait_ge(s_grs, l + 1)
                        for b in range(NB):
                            link(ts(gel[:, b, GW:], gel[:, b, GW:], mv[:, b, 0:1], rs[:, 6 + b:7 + b],
                                    ALU.subtract, ALU.mult))
                        tt(gel[:, :, GW:], gel[:, :, GW:], ln_row[:, l:l + 1, :].to_broadcast([P, NB, GW]),
                           ALU.mult).then_inc(s_gv, 1)
                        dve.wait_ge(s_cv, l + 1)
                        tt(y[:, :, GW:2 * GW], bank[1][:, :].rearrange("p (b n) -> p b n", b=NB),
                           proj[:, :, CB:CB + GW], ALU.mult).then_inc(s_yc, 1)
                        dve.wait_ge(s_yc, l + 1)
                dve.wait_ge(s_zp, l + 1)
                for j, name in enumerate(("pe_k", "pe_v")):
                    z = bank[1][:, j * P:(j + 1) * P].rearrange("p (c r) -> p c r", r=8)
                    for a in range(2):
                        c = row_at[name] + 16 * l + 8 * a
                        pe_ = cols[:, None, c:c + 8].to_broadcast([P, NC, 8])
                        i = tt(blk[:, j, a, :, :], z[:, a:a + NC, :], pe_, ALU.add)
                i.then_inc(s_blk, 1)
                dve.wait_ge(s_qa, l + 1)
                if l == 0:
                    dve.wait_ge(s_sin, 1)
                x1, x2 = q5[:, :, :, NOPE:NOPE + HALF], q5[:, :, :, NOPE + HALF:]
                five = [P, NB, HEADS + 1, HALF]
                cos_b = cos_t[:, :, None, :].to_broadcast(five)
                sin_b = sin_t[:, :, None, :].to_broadcast(five)
                tt(rt[:, 0], x1, cos_b, ALU.mult)
                tt(rt[:, 1], x2, sin_b, ALU.mult)
                tt(rt[:, 2], x1, sin_b, ALU.mult)
                link(tt(rt[:, 3], x2, cos_b, ALU.mult))
                tt(x1, rt[:, 0], rt[:, 1], ALU.subtract)
                link(tt(x2, rt[:, 2], rt[:, 3], ALU.add))
                for b in range(NB):
                    i = nc.vector.tensor_copy(kk[:, b, :, NOPE:],
                                              q5[:, b, HEADS:HEADS + 1, NOPE:].to_broadcast([P, HEADS, ROPE]))
                i.then_inc(s_rope, 1)
                dve.wait_ge(s_sv, l + 1)
                for g in range(4):
                    i = nc.vector.scalar_tensor_tensor(
                        out=y[:, :, 2 * GW + g * DH:2 * GW + (g + 1) * DH],
                        in0=bank[5][:, :].rearrange("p (b n) -> p b n", b=NB)[:, :, g * DH:(g + 1) * DH],
                        scalar=columns("bs", 4 * l + g), in1=gel[:, :, g * DH:(g + 1) * DH],
                        op0=ALU.add, op1=ALU.mult)
                i.then_inc(s_yg, 1)
                dve.wait_ge(s_yg, l + 1)
                dve.wait_ge(s_hc, l + 1)
                hid_ps = bank[1][:, 0:64].rearrange("p (j t c) -> p j t c", j=2, t=2)
                nc.vector.tensor_copy(hidT[:, :, 0:NC], hid_ps[:, 0, :, 0:NC])
                for t in range(CH // P):
                    i = nc.vector.tensor_copy(hidR[:, t, :, 0:NC],
                                              hid_ps[:, 1, t:t + 1, 0:NC].to_broadcast([P, HEADS, NC]))
                i.then_inc(s_hr, 1)
                dve.wait_ge(s_kcp, l + 1)
                nc.vector.tensor_copy(kcT[0:DH, 0:NC], bank[3][0:DH, 0:NC])
                for hd in range(HEADS):
                    i = nc.vector.tensor_copy(vcd[32 * hd:32 * hd + 32, hd * DH:(hd + 1) * DH],
                                              bank[3][32 * hd:32 * hd + 32, 64:64 + DH])
                i.then_inc(s_kc, 1)
                dve.wait_ge(s_gex, l + 1)
                link(ts(gexp[:, :, :], gexp[:, :, :], 1.0, None, ALU.add))
                link(nc.vector.reciprocal(gsig[:, :, :], gexp[:, :, :]))
                dve.wait_ge(s_scp, l + 1)
                for b in range(NB):
                    link(tt(sc[:, b * HEADS:(b + 1) * HEADS, :][:, :, 0:NC],
                            bank[4][:, b * 64:(b + 1) * 64].rearrange("p (h c) -> p h c", c=16)[:, :, 0:NC],
                            cmask[:, b:b + 1, 0:NC].to_broadcast([P, HEADS, NC]), ALU.add))
                link(nc.vector.tensor_reduce(scm[:, :], sc[:, :, 0:NC], AX_X, ALU.max))
                tt(sc[:, :, 0:NC], sc[:, :, 0:NC], scm[:, :, None].to_broadcast([P, NB * HEADS, NC]),
                   ALU.subtract).then_inc(s_scm, 1)

                def row_max(n):
                    kind, b, hs = UNITS[n]
                    m = l * NU + n
                    dve.wait_ge(s_sp, m + 1)
                    if n >= 2:
                        dve.wait_ge(s_e, m - 1)
                    nc.vector.tensor_reduce(
                        nmax[:, n % 2, 0:len(hs)],
                        bank[n % 2][:, :].rearrange("p (h k) -> p h k", h=len(hs)), AX_X, ALU.max,
                        negate=True).then_inc(s_mx, 1)

                row_max(0)
                dve.wait_ge(s_pc, l + 1)
                link(nc.vector.tensor_reduce(pcs[:, :], pc[:, :, :, 0:NC].rearrange("p b h c -> p (b h) c"),
                                             AX_X, ALU.add))
                dve.wait_ge(s_pcp, l + 1)
                nc.vector.tensor_copy(pcT[:, :, :].rearrange("p b t -> p (b t)"),
                                      bank[3][:, 128:128 + NB * P]).then_inc(s_pcT, 1)
                row_max(1)
                link(nc.vector.reciprocal(pcs[:, :], pcs[:, :]))
                link(tt(pcs[:, :].rearrange("p (b h) -> p b h", b=NB), pcs[:, :].rearrange("p (b h) -> p b h", b=NB),
                        cvalid[:, :, None].to_broadcast([P, NB, HEADS]), ALU.mult))
                for n in range(2, NU):
                    row_max(n)
                    if n == 5:
                        dve.wait_ge(s_ov, l * NU + 3)
                        link(nc.vector.reciprocal(prec[:, 0, :], psums[:, 0, :]))
                        for b in range(NB):
                            i = tt(y[:, b, 0:GW].rearrange("p (h d) -> p h d", d=DH),
                                   bank[7][:, b * GW:(b + 1) * GW].rearrange("p (h d) -> p h d", d=DH),
                                   prec[:, 0, b * HEADS:(b + 1) * HEADS, None].to_broadcast([P, HEADS, DH]),
                                   ALU.mult)
                        i.then_inc(s_ym, 1)
                        dve.wait_ge(s_ym, l + 1)
                dve.wait_ge(s_gsc, 2 * l + 1)
                dve.wait_ge(s_xp, XB * (3 * l + 1))
                scale_group(0)
                scale_group(1)
                scale_group(2).then_inc(s_gxs, 1)
                group_out(l, 1, 2)
                dve.wait_ge(s_ov, l * NU + NU)
                link(nc.vector.reciprocal(prec[:, 1:, :], psums[:, 1:, :]))
                full = [P, NB * HEADS, DH]

                def spread(ap):
                    return ap[:, :, None].to_broadcast(full)

                def heads(ap):
                    return ap.rearrange("p (h d) -> p h d", d=DH)

                gate3 = gsig[:, :, :].rearrange("p b (h k) -> p (b h) k", k=3)
                tt(coef[:, 0, :], pcs[:, :], gate3[:, :, 0], ALU.mult)
                tt(coef[:, 1, :], prec[:, 1, :], gate3[:, :, 1], ALU.mult)
                link(tt(coef[:, 2, :], prec[:, 2, :], gate3[:, :, 2], ALU.mult))
                dve.wait_ge(s_oc, l + 1)
                t0 = nsa_t[:, 0].rearrange("p b (h d) -> p (b h) d", d=DH)
                t1 = nsa_t[:, 1].rearrange("p b (h d) -> p (b h) d", d=DH)
                tt(t0, heads(bank[6][:, :]), spread(coef[:, 0, :]), ALU.mult)
                link(tt(t1, heads(bank[4][:, :]), spread(coef[:, 1, :]), ALU.mult))
                link(tt(t0, t0, t1, ALU.add))
                link(tt(t1, heads(bank[5][:, :]), spread(coef[:, 2, :]), ALU.mult))
                tt(y[:, :, 3 * GW:], nsa_t[:, 0], nsa_t[:, 1], ALU.add).then_inc(s_y, 1)
                dve.wait_ge(s_gsc, 2 * l + 2)
                scale_group(3).then_inc(s_gxs, 1)
                for j in AHEAD[0]:
                    split(l, j)
                group_out(l, 3, 3)
                for b in range(NB):
                    for j in range(2):
                        dve.wait_ge(s_wo, 4 * l + 2 * b + j + 1)
                        i = tt(h[:, b, j * W:(j + 1) * W], h[:, b, j * W:(j + 1) * W],
                               bank[WO_BANK[b][j]][:, :], ALU.add)
                    i.then_inc(s_hb, 1)
                dve.wait_ge(s_hb, NB * (l + 1))
                dve.sem_inc(s_h, 1)
                scale_rows(h, 3 * l + 2)
                dve.sem_inc(s_y, 1)
                if l:
                    turned(3 * l + 2, "ffn", KT * l)
                else:
                    for k in range(KT):
                        if k % 2 == 0:
                            dve.wait_ge(s_xh, k // 2 + 1)
                        i = nc.vector.scalar_tensor_tensor(
                            out=xl[:, k, :], in0=bank[k // 2][:, (k % 2) * SEQ:(k % 2 + 1) * SEQ],
                            scalar=columns("ffn", k), in1=xh[:, k, :].bitcast(F32),
                            op0=ALU.mult, op1=ALU.subtract)
                        if k % 4 == 3:
                            i.then_inc(s_xl, 1)
                        elif k % 2 == 0:
                            i.then_inc(s_xTv, 1)

                    def ffn(f, blocks, others={}):
                        def product(n):
                            dve.wait_ge(s_sg, f * FS + (n + 1))
                            dve.wait_ge(s_used, f * PIECES + (AT[1, n, 1] + 1))
                            past(dve, s_hT, f * FS + n)
                            for b in range(blocks):
                                i = tt(hid[:, b, :], bank[2 + b][:, :], sg[:, b, :], ALU.mult)
                            i.then_inc(s_hid, 1)

                        def turned_out(n):
                            dve.wait_ge(s_hTh, f * FS + (n + 1))
                            for b in range(blocks):
                                i = tt(hTl[:, b, :], bank[2 + b if blocks == 2 else 1][:, :],
                                       hTh[:, b, :].bitcast(F32), ALU.subtract)
                            i.then_inc(s_hTl, 1)

                        split_schedule(unless_ahead(dve, f, lambda j: split(f, j)), None, product, turned_out, others)

                    ffn(0, 2)
                    dve.wait_ge(s_used, PIECES)
                    for b in range(NB):
                        for half in range(2):
                            i = tt(h[:, b, half * W:(half + 1) * W], h[:, b, half * W:(half + 1) * W],
                                   bank[4 + 2 * b + half][:, :], ALU.add)
                        i.then_inc(s_hd, 1)
                    dve.wait_ge(s_hd, NB)
                    dve.sem_inc(s_h, 1)
                    dve.wait_ge(s_h, 2)

            dve.wait_ge(s_lp, 1)
            wide = [P, NB, E]
            link(nc.vector.tensor_copy(lg[:, :, :].rearrange("p b e -> p (b e)"), bank[0][:, 0:NB * E]))
            for k in range(2):
                src = lg if k == 0 else lg2
                link(nc.vector.tensor_reduce(top[:, k, :], src[:, :, :], AX_X, ALU.max))
                link(tt(rt_a[:, :, :], src[:, :, :], top[:, k, :, None].to_broadcast(wide), ALU.is_equal))
                link(tt(rt_a[:, :, :], rt_a[:, :, :], w8[:, None, :].to_broadcast(wide), ALU.mult))
                link(nc.vector.tensor_reduce(fst[:, :], rt_a[:, :, :], AX_X, ALU.max))
                link(tt(oh[:, k], rt_a[:, :, :], fst[:, :, None].to_broadcast(wide), ALU.is_equal))
                if k == 0:
                    link(ts(lg2[:, :, :], oh[:, 0], -HUGE, None, ALU.mult))
                    link(tt(lg2[:, :, :], lg2[:, :, :], lg[:, :, :], ALU.add))
            tt(gd[:, 0, :], top[:, 1, :], top[:, 0, :], ALU.subtract).then_inc(s_lm, 1)
            tt(rsg[:, 1], oh[:, 0], oh[:, 1], ALU.add).then_inc(s_sel, 1)
            dve.wait_ge(s_le, 1)
            link(ts(gd[:, 2, :], gd[:, 1, :], 1.0, None, ALU.add))
            link(nc.vector.reciprocal(gw[:, 0, :], gd[:, 2, :]))
            link(tt(gw[:, 1, :], gd[:, 1, :], gw[:, 0, :], ALU.mult))
            for k in range(2):
                link(tt(oh[:, k], oh[:, k], gw[:, k, :, None].to_broadcast(wide), ALU.mult))
            link(tt(rsg[:, 2], oh[:, 0], oh[:, 1], ALU.add))
            dve.wait_ge(s_rk, 1)
            nc.vector.tensor_copy(total[:, :], bank[1][:, NB * E:(NB + 1) * E])
            link(nc.vector.tensor_copy(rsg[:, 0].rearrange("p b e -> p (b e)"), bank[1][:, 0:NB * E]))

            def slots(n, key):
                ts(eqm[:, :], key, cnt[:, 0:1], None, ALU.is_equal).then_inc(s_col, 1)
                dve.wait_ge(s_col, COLS * n + 1)
                tt(pick[:, :, :], rsg[:, :, :, :].rearrange("p k b e -> p (k b) e"),
                   eqm[:, None, :].to_broadcast([P, 3 * NB, E]), ALU.mult).then_inc(s_col, 1)
                ts(cnt[:, 0:1], cnt[:, 0:1], 1.0, None, ALU.add).then_inc(s_col, 1)
                dve.wait_ge(s_col, COLS * n + 3)
                nc.vector.tensor_reduce(col[:, :], pick[:, :, :], AX_X, ALU.add).then_inc(s_col, 1)
                dve.wait_ge(s_col, COLS * n + 4)
                for b in range(NB):
                    ts(gm[:, b, :], iota_s[:, :], col[:, b:b + 1], col[:, NB + b:NB + b + 1],
                       ALU.is_equal, ALU.mult)
                    i = ts(gg[:, b, :], iota_s[:, :], col[:, b:b + 1], col[:, 2 * NB + b:2 * NB + b + 1],
                           ALU.is_equal, ALU.mult)
                i.then_inc(s_gm, 1)

            COLS = 4

            def rows_low(n):
                dve.wait_ge(s_xe, n + 1)
                for k in range(KT):
                    i = nc.vector.scalar_tensor_tensor(
                        out=xl[:, k, 0:P], in0=bank[6 + k // 4][:, (k % 4) * P:(k % 4 + 1) * P],
                        scalar=columns("ffn", KT * (L - 1) + k), in1=xh[:, k, 0:P].bitcast(F32),
                        op0=ALU.mult, op1=ALU.subtract)
                i.then_inc(s_xl, 1)

            def add(m):
                dve.wait_ge(s_ysp, m + 1)
                past(dve, s_yadd, m)
                for b in range(NB):
                    for half in range(2):
                        i = tt(h[:, b, half * W:(half + 1) * W], h[:, b, half * W:(half + 1) * W],
                               bank[6 - 2 * b + half][:, :], ALU.add)
                i.then_inc(s_yadd, 1)
                dve.wait_ge(s_yadd, m + 1)
                dve.sem_inc(s_ysa, 1)

            experts = iota_s[:, 0:E]
            nc.vector.memset(ggT[:, :, :], 0.0).then_inc(s_ggT, 1)
            slots(0, experts)
            for j in AHEAD[1]:
                split(1, j)
            rows_low(0)
            link(ts(okey[:, 0, :], total[:, :], float(SLOTS), None, ALU.is_gt))
            link(nc.vector.tensor_tensor_scan(okey[:, 1, :], ones[:, 0:E], okey[:, 0, :], 0.0,
                                              ALU.mult, ALU.add))
            link(nc.vector.tensor_reduce(over_f[:, 0:1], okey[:, 1, :], AX_X, ALU.max))
            link(tt(okey[:, 0, :], okey[:, 0, :], okey[:, 1, :], ALU.mult))
            link(tt(over_e[:, :, :], okey[:, 0:1, :].to_broadcast([P, MAX_OVER, E]),
                    iota_s[:, 1:MAX_OVER + 1, None].to_broadcast([P, MAX_OVER, E]), ALU.is_equal))
            link(tt(over_e[:, :, :], over_e[:, :, :], iota_s[:, None, 0:E].to_broadcast([P, MAX_OVER, E]), ALU.mult))
            link(nc.vector.tensor_reduce(over_f[:, 1:], over_e[:, :, :], AX_X, ALU.add))
            nc.vector.tensor_copy(over_i[:, :], over_f[:, :]).then_inc(s_over, 1)
            with dve.Fori(0, E) as e:
                def next_slots():
                    dve.wait_ge(s_xep, e + 1)
                    dve.wait_ge(s_ggp, e + 1)
                    slots(e + 1, experts)

                ffn(e + 1, 1, {ADD_AT: lambda: add(e), SLOTS_AT: next_slots,
                               ROWS_AT: lambda: rows_low(e + 1)})
            add(E)
            dve.wait_ge(s_col, COLS * (E + 1))
            link(ts(rsg[:, 0], rsg[:, 0], -float(SLOTS), None, ALU.add))
            link(nc.vector.memset(cnt[:, :], 1.0))
            dve.wait_ge(s_over, 1)
            n_over = dve.value_load(over_i[0:1, 0:1], min_val=0, max_val=MAX_OVER)
            with dve.Fori(0, MAX_OVER) as i:
                with dve.If(n_over > i):
                    n = i + (E + 1)
                    dve.wait_ge(s_xep, n)
                    dve.wait_ge(s_ggp, i + E)
                    slots(n, okey[:, 0, :])
                    rows_low(n)
                    ffn(n, 1)
                    add(n)
            dve.sem_inc(s_h, 1)
            dve.wait_ge(s_rs, L + 1)
            for b in range(NB):
                nc.vector.scalar_tensor_tensor(out=xs[:, b, :], in0=h[:, b, :], scalar=rs[:, b:b + 1],
                                               in1=fin_row[:, :], op0=ALU.mult, op1=ALU.mult).then_inc(s_y, 1)


_INS = ['x', 'positions', 'rope_inv', 'attn_norm', 'w_in', 'mla_q_norm', 'mla_w_uq', 'mla_kv_norm', 'mla_w_ukv',
        'conv_w', 'gmlp_ln', 'gmlp_w_s', 'gmlp_b_s', 'nsa_pe_k', 'nsa_w1_k', 'nsa_w2_k', 'nsa_pe_v', 'nsa_w1_v',
        'nsa_w2_v', 'group_norm', 'w_o', 'ffn_norm', 'dense_w_gate', 'dense_w_up', 'dense_w_down',
        'moe_router', 'moe_w_gate', 'moe_w_up', 'moe_w_down', 'final_norm']


def kernel(**inputs):
    import numpy as _np
    import concourse.bacc as _bacc
    from concourse import mybir as _mybir
    from concourse.bass_utils import run_bass_kernel_spmd as _run

    rope_inv = (_np.float32(10000.0) ** (-_np.arange(HALF, dtype=_np.float32) / _np.float32(HALF))).reshape(1, HALF)
    nc = _bacc.Bacc("TRN2", target_bir_lowering=False, num_devices=1)
    arrays, args = {}, []
    for name in _INS:
        a = _np.ascontiguousarray(rope_inv if name == 'rope_inv' else inputs[name])
        arrays[f"in_{name}_dram"] = a
        args.append(nc.dram_tensor(f"in_{name}_dram", a.shape, _mybir.dt.from_np(a.dtype), kind="ExternalInput").ap())
    shape = tuple(inputs['x'].shape)
    args.append(nc.dram_tensor("out_0_dram", shape, F32, kind="ExternalOutput").ap())
    hybrid_trunk(nc, *args)
    r = _run(nc, [arrays], core_ids=[0])
    return r.results[0]["out_0_dram"]
```
